# Optimizing a Trainium2 kernel written in Bass

```python
import math
import jax, jax.numpy as jnp
from jax import lax
import numpy as np

D_MODEL = 1024
BATCH = 1
SEQ = 256
DEPTH = 2

D_MIX = D_MODEL
D_CONV = D_MIX // 4
D_POOL = D_MIX // 4
D_ATTN = D_MIX // 2
N_HEADS = 4
HEAD_DIM = D_ATTN // (2 * N_HEADS)
V_DIM = 2 * HEAD_DIM
CONV_WIDTH = 31
POOL_WINDOWS = (2, 4, 8, 16)
N_POOL_GROUPS = len(POOL_WINDOWS)
POOL_GROUP_DIM = D_POOL // N_POOL_GROUPS
D_FF = 256 * ((8 * D_MODEL // 3 + 255) // 256)
D_IN = 2 * D_CONV + D_POOL + 3 * D_ATTN
Q_BLOCK = 128
NORM_EPS = 1e-6


def rms_norm(x, g):
    xf = x.astype(jnp.float32)
    y = xf * lax.rsqrt(jnp.mean(xf * xf, axis=-1, keepdims=True) + NORM_EPS)
    return (y * g.astype(jnp.float32)).astype(x.dtype)

def layer_norm(x, g, b):
    xf = x.astype(jnp.float32)
    mu = jnp.mean(xf, axis=-1, keepdims=True)
    xc = xf - mu
    y = xc * lax.rsqrt(jnp.mean(xc * xc, axis=-1, keepdims=True) + NORM_EPS)
    return (y * g.astype(jnp.float32) + b.astype(jnp.float32)).astype(x.dtype)

def swiglu_ffn(h, w_gate, w_up, w_down):
    return (jax.nn.silu(h @ w_gate) * (h @ w_up)) @ w_down

def conformer_conv(u, w_dw, b_dw, ln_g, ln_b):
    a, gate = jnp.split(u, 2, axis=-1)
    z = a * jax.nn.sigmoid(gate)
    z = lax.conv_general_dilated(
        z, w_dw[:, None, :], window_strides=(1,),
        padding=((CONV_WIDTH // 2, CONV_WIDTH // 2),),
        dimension_numbers=("NWC", "WIO", "NWC"),
        feature_group_count=D_CONV) + b_dw
    return jax.nn.silu(layer_norm(z, ln_g, ln_b))

def multiscale_pool(u, w_grp, scale):
    B_, S_, _ = u.shape
    uf = u.astype(jnp.float32)
    cs = jnp.concatenate([jnp.zeros((B_, 1, D_POOL), jnp.float32), jnp.cumsum(uf, axis=1)], axis=1)
    t = jnp.arange(S_, dtype=jnp.int32)
    outs = []
    for g, w in enumerate(POOL_WINDOWS):
        sl = slice(g * POOL_GROUP_DIM, (g + 1) * POOL_GROUP_DIM)
        lo = jnp.clip(t - w // 2, 0, S_)
        hi = jnp.clip(t + w // 2, 0, S_)
        csg = cs[..., sl]
        win_sum = jnp.take(csg, hi, axis=1) - jnp.take(csg, lo, axis=1)
        cnt = (hi - lo).astype(jnp.float32)[None, :, None]
        outs.append(win_sum / cnt - uf[..., sl])
    d = jnp.stack(outs, axis=2)
    y = jnp.einsum("bsgc,gcd->bsgd", d, w_grp.astype(jnp.float32)).reshape(B_, S_, D_POOL)
    return (y * scale.astype(jnp.float32)).astype(u.dtype)

def diff_attention(q, k, v, lam, slopes):
    B_, S_ = q.shape[0], q.shape[1]
    n_blk = S_ // Q_BLOCK
    q_blocks = jnp.moveaxis(q.reshape(B_, n_blk, Q_BLOCK, N_HEADS, 2, HEAD_DIM), 1, 0)
    k_pos = jnp.arange(S_, dtype=jnp.int32)

    def block(args):
        q_blk, blk = args
        q_pos = blk * Q_BLOCK + jnp.arange(Q_BLOCK, dtype=jnp.int32)
        dist = jnp.abs(q_pos[:, None] - k_pos[None, :]).astype(jnp.float32)
        s = jnp.einsum("bqhcd,bkhcd->bhcqk", q_blk, k, preferred_element_type=jnp.float32)
        s = s - slopes[None, :, None, None, None] * dist
        p = jax.nn.softmax(s, axis=-1)
        a = p[:, :, 0] - lam * p[:, :, 1]
        return jnp.einsum("bhqk,bkhe->bqhe", a.astype(v.dtype), v)

    o = lax.map(block, (q_blocks, jnp.arange(n_blk, dtype=jnp.int32)))
    return jnp.moveaxis(o, 0, 1).reshape(B_, S_, N_HEADS, V_DIM)

def first_inputs(seed: int = 0) -> dict:
    key = jax.random.key(seed)
    ks = iter(jax.random.split(key, 32))

    def nrm(shape, scale):
        return jax.random.normal(next(ks), shape, jnp.float32) * scale

    def gain(shape):
        return 1.0 + 0.02 * jax.random.normal(next(ks), shape, jnp.float32)

    L = DEPTH
    return {
        "x": nrm((BATCH, SEQ, D_MODEL), 1.0),
        "ffn1_norm": gain((L, D_MODEL)),
        "ffn1_w_gate": nrm((L, D_MODEL, D_FF), D_MODEL ** -0.5),
        "ffn1_w_up": nrm((L, D_MODEL, D_FF), D_MODEL ** -0.5),
        "ffn1_w_down": nrm((L, D_FF, D_MODEL), D_FF ** -0.5),
        "mix_norm": gain((L, D_MODEL)),
        "w_in": nrm((L, D_MODEL, D_IN), D_MODEL ** -0.5),
        "conv_dw": nrm((L, CONV_WIDTH, D_CONV), CONV_WIDTH ** -0.5),
        "conv_dw_bias": nrm((L, D_CONV), 0.02),
        "conv_ln_gain": gain((L, D_CONV)),
        "conv_ln_bias": nrm((L, D_CONV), 0.02),
        "pool_w": nrm((L, N_POOL_GROUPS, POOL_GROUP_DIM, POOL_GROUP_DIM), POOL_GROUP_DIM ** -0.5),
        "pool_scale": 1.0 + 0.1 * jax.random.normal(next(ks), (L, D_POOL), jnp.float32),
        "q_norm": gain((L, HEAD_DIM)),
        "k_norm": gain((L, HEAD_DIM)),
        "lambda_q1": nrm((L, HEAD_DIM), 0.1),
        "lambda_k1": nrm((L, HEAD_DIM), 0.1),
        "lambda_q2": nrm((L, HEAD_DIM), 0.1),
        "lambda_k2": nrm((L, HEAD_DIM), 0.1),
        "attn_subln": gain((L, V_DIM)),
        "w_out": nrm((L, D_MIX, D_MODEL), D_MIX ** -0.5),
        "ffn2_norm": gain((L, D_MODEL)),
        "ffn2_w_gate": nrm((L, D_MODEL, D_FF), D_MODEL ** -0.5),
        "ffn2_w_up": nrm((L, D_MODEL, D_FF), D_MODEL ** -0.5),
        "ffn2_w_down": nrm((L, D_FF, D_MODEL), D_FF ** -0.5),
        "post_norm": gain((L, D_MODEL)),
    }

def first_block(x, ffn1_norm, ffn1_w_gate, ffn1_w_up, ffn1_w_down, mix_norm, w_in,
              conv_dw, conv_dw_bias, conv_ln_gain, conv_ln_bias, pool_w, pool_scale,
              q_norm, k_norm, lambda_q1, lambda_k1, lambda_q2, lambda_k2, attn_subln,
              w_out, ffn2_norm, ffn2_w_gate, ffn2_w_up, ffn2_w_down, post_norm):
    B_, S_ = x.shape[0], x.shape[1]
    slopes = jnp.exp2(-8.0 * jnp.arange(1, N_HEADS + 1, dtype=jnp.float32) / N_HEADS)
    for l in range(DEPTH):
        lambda_init = 0.8 - 0.6 * math.exp(-0.3 * l)
        x = x + 0.5 * swiglu_ffn(rms_norm(x, ffn1_norm[l]), ffn1_w_gate[l], ffn1_w_up[l], ffn1_w_down[l])
        h = rms_norm(x, mix_norm[l])
        u = h @ w_in[l]
        u_conv = u[..., :2 * D_CONV]
        u_pool = u[..., 2 * D_CONV:2 * D_CONV + D_POOL]
        q, k, v = jnp.split(u[..., 2 * D_CONV + D_POOL:], 3, axis=-1)
        y_conv = conformer_conv(u_conv, conv_dw[l], conv_dw_bias[l], conv_ln_gain[l], conv_ln_bias[l])
        y_pool = multiscale_pool(u_pool, pool_w[l], pool_scale[l])
        q = rms_norm(q.reshape(B_, S_, N_HEADS, 2, HEAD_DIM), q_norm[l]) * (HEAD_DIM ** -0.5)
        k = rms_norm(k.reshape(B_, S_, N_HEADS, 2, HEAD_DIM), k_norm[l])
        v = v.reshape(B_, S_, N_HEADS, V_DIM)
        lam = (jnp.exp(jnp.sum(lambda_q1[l].astype(jnp.float32) * lambda_k1[l].astype(jnp.float32)))
               - jnp.exp(jnp.sum(lambda_q2[l].astype(jnp.float32) * lambda_k2[l].astype(jnp.float32)))
               + lambda_init)
        o = diff_attention(q, k, v, lam, slopes)
        y_attn = (rms_norm(o, attn_subln[l]) * (1.0 - lambda_init)).reshape(B_, S_, D_ATTN)
        y = jnp.concatenate([y_conv, y_pool, y_attn.astype(y_conv.dtype)], axis=-1) @ w_out[l]
        x = x + y
        x = x + 0.5 * swiglu_ffn(rms_norm(x, ffn2_norm[l]), ffn2_w_gate[l], ffn2_w_up[l], ffn2_w_down[l])
        x = rms_norm(x, post_norm[l])
    return x


GRID_W = 64
CTX_LEN = 256
N_EVEN = (DEPTH + 1) // 2
N_ODD = DEPTH // 2
EPS = 1e-6

FOURIER_GROUPS = 4
FOURIER_GROUP_DIM = 128
FOURIER_WIDTH = FOURIER_GROUPS * FOURIER_GROUP_DIM
CONV_GROUPS = 4
CONV_WIDTH_2 = 512
CONV_K = 3
EVEN_IN = FOURIER_WIDTH + 3 * CONV_WIDTH_2
EVEN_OUT = FOURIER_WIDTH + CONV_WIDTH_2

N_HEADS_2 = 16
N_KV_HEADS = 4
GQA_GROUP = N_HEADS_2 // N_KV_HEADS
HEAD_DIM_2 = 64
Q_DIM = N_HEADS_2 * HEAD_DIM_2
KV_DIM = N_KV_HEADS * HEAD_DIM_2
QKV_OUT = Q_DIM + 2 * KV_DIM
WINDOW = 128
ATT_BLOCK = 128
ROPE_BASE = 10000.0
ROPE_PAIRS_PER_AXIS = HEAD_DIM_2 // 4
NEG_INF = -1e30

N_GROUPS = 4
EXPERTS_PER_GROUP = 8
N_EXPERTS = N_GROUPS * EXPERTS_PER_GROUP
TOP_K = 2
D_FF_EXPERT = 512
MOE_BLOCK = 128


def rms_norm_2(x, g):
    xf = x.astype(jnp.float32)
    y = xf * lax.rsqrt(jnp.mean(xf * xf, axis=-1, keepdims=True) + EPS)
    return (y * g.astype(jnp.float32)).astype(x.dtype)

def modulate(h, shift, scale):
    return h * (1 + scale) + shift

def fourier_mix(a):
    b_, l_, _ = a.shape
    a4 = a.reshape(b_, l_, FOURIER_GROUPS, FOURIER_GROUP_DIM).astype(jnp.float32)
    f = jnp.fft.fftn(a4, axes=(1, 3), norm="ortho").real
    return f.reshape(b_, l_, FOURIER_WIDTH).astype(a.dtype)

def short_conv_mix(b_gate, c_gate, h, w):
    u = c_gate * h
    up = jnp.pad(u, ((0, 0), (1, 1), (0, 0)))
    y = w[0] * up[:, :-2] + w[1] * up[:, 1:-1] + w[2] * up[:, 2:]
    return b_gate * y

def even_mixer(h, w_in, conv_w, w_out):
    p = h @ w_in
    a, b_gate, c_gate, hv = jnp.split(
        p, [FOURIER_WIDTH, FOURIER_WIDTH + CONV_WIDTH_2, FOURIER_WIDTH + 2 * CONV_WIDTH_2], axis=-1)
    y = jnp.concatenate([fourier_mix(a), short_conv_mix(b_gate, c_gate, hv, conv_w)], axis=-1)
    return y @ w_out

def axial_rope_tables(n_tok):
    t = jnp.arange(n_tok, dtype=jnp.int32)
    pos = jnp.stack([t // GRID_W, t % GRID_W], axis=-1).astype(jnp.float32)
    freqs = ROPE_BASE ** (-jnp.arange(ROPE_PAIRS_PER_AXIS, dtype=jnp.float32) / ROPE_PAIRS_PER_AXIS)
    ang = pos[:, :, None] * freqs
    return jnp.cos(ang), jnp.sin(ang)

def apply_axial_rope(x, cos, sin):
    b_, l_, h_, _ = x.shape
    xf = x.astype(jnp.float32).reshape(b_, l_, h_, 2, 2, ROPE_PAIRS_PER_AXIS)
    x1, x2 = xf[..., 0, :], xf[..., 1, :]
    cs, sn = cos[None, :, None], sin[None, :, None]
    out = jnp.stack([x1 * cs - x2 * sn, x1 * sn + x2 * cs], axis=-2)
    return out.reshape(x.shape).astype(x.dtype)

def project_q(h, w_qkv, q_g):
    b_, l_, _ = h.shape
    q = (h @ w_qkv[:, :Q_DIM]).reshape(b_, l_, N_HEADS_2, HEAD_DIM_2)
    return rms_norm_2(q, q_g)

def project_kv(h, w_qkv, k_g):
    b_, l_, _ = h.shape
    kv = h @ w_qkv[:, Q_DIM:]
    k = rms_norm_2(kv[..., :KV_DIM].reshape(b_, l_, N_KV_HEADS, HEAD_DIM_2), k_g)
    v = kv[..., KV_DIM:].reshape(b_, l_, N_KV_HEADS, HEAD_DIM_2)
    return k, v

def window_attention(hl, hc, w_qkv, q_g, k_g, sink, w_o, need_ctx_out):
    B, L, _ = hl.shape
    Lc = hc.shape[1]
    scale = HEAD_DIM_2 ** -0.5
    cos, sin = axial_rope_tables(L)
    ql = apply_axial_rope(project_q(hl, w_qkv, q_g), cos, sin) * scale
    kl, vl = project_kv(hl, w_qkv, k_g)
    kl = apply_axial_rope(kl, cos, sin)
    kc, vc = project_kv(hc, w_qkv, k_g)
    sink_g = sink.reshape(N_KV_HEADS, GQA_GROUP).astype(jnp.float32)

    n_blocks = L // ATT_BLOCK
    qg = ql.reshape(B, L, N_KV_HEADS, GQA_GROUP, HEAD_DIM_2)
    pad = ((0, 0), (ATT_BLOCK, ATT_BLOCK), (0, 0), (0, 0))
    kp, vp = jnp.pad(kl, pad), jnp.pad(vl, pad)
    qi = jnp.arange(ATT_BLOCK)
    kj = jnp.arange(3 * ATT_BLOCK)
    band = jnp.abs(kj[None, :] - ATT_BLOCK - qi[:, None]) <= WINDOW

    def block(bidx):
        start = bidx * ATT_BLOCK
        qb = lax.dynamic_slice_in_dim(qg, start, ATT_BLOCK, axis=1)
        kb = lax.dynamic_slice_in_dim(kp, start, 3 * ATT_BLOCK, axis=1)
        vb = lax.dynamic_slice_in_dim(vp, start, 3 * ATT_BLOCK, axis=1)
        kpos = start - ATT_BLOCK + kj
        mask = band & ((kpos >= 0) & (kpos < L))[None, :]
        s_loc = jnp.einsum("bqkgd,bskd->bkgqs", qb, kb, preferred_element_type=jnp.float32)
        s_loc = jnp.where(mask, s_loc, NEG_INF)
        s_ctx = jnp.einsum("bqkgd,bskd->bkgqs", qb, kc, preferred_element_type=jnp.float32)
        s_sink = jnp.broadcast_to(sink_g[None, :, :, None, None], s_loc.shape[:-1] + (1,))
        p = jax.nn.softmax(jnp.concatenate([s_loc, s_ctx, s_sink], axis=-1), axis=-1)
        p_loc = p[..., :3 * ATT_BLOCK].astype(vb.dtype)
        p_ctx = p[..., 3 * ATT_BLOCK:3 * ATT_BLOCK + Lc].astype(vc.dtype)
        return (jnp.einsum("bkgqs,bskd->bqkgd", p_loc, vb)
                + jnp.einsum("bkgqs,bskd->bqkgd", p_ctx, vc))

    ob = lax.map(block, jnp.arange(n_blocks))
    yl = jnp.moveaxis(ob, 0, 1).reshape(B, L, Q_DIM) @ w_o

    if not need_ctx_out:
        return yl, None
    qc = project_q(hc, w_qkv, q_g).reshape(B, Lc, N_KV_HEADS, GQA_GROUP, HEAD_DIM_2) * scale
    s = jnp.einsum("bqkgd,bskd->bkgqs", qc, kc, preferred_element_type=jnp.float32)
    s_sink = jnp.broadcast_to(sink_g[None, :, :, None, None], s.shape[:-1] + (1,))
    p = jax.nn.softmax(jnp.concatenate([s, s_sink], axis=-1), axis=-1)[..., :Lc].astype(vc.dtype)
    yc = jnp.einsum("bkgqs,bskd->bqkgd", p, vc).reshape(B, Lc, Q_DIM) @ w_o
    return yl, yc

def hier_moe(xf, w_rg, b_rg, w_re, b_re, w1, w3, w2):
    T, D = xf.shape
    xr = xf.astype(jnp.float32)
    g_logits = xr @ w_rg.astype(jnp.float32) + b_rg.astype(jnp.float32)
    g_prob = jax.nn.softmax(g_logits, axis=-1)
    g_val, g_idx = lax.top_k(g_prob, 1)
    e_logits = (xr @ w_re.astype(jnp.float32) + b_re.astype(jnp.float32)).reshape(
        T, N_GROUPS, EXPERTS_PER_GROUP)
    e_in = jnp.take_along_axis(e_logits, g_idx[:, :, None], axis=1)[:, 0]
    top_v, top_i = lax.top_k(e_in, TOP_K)
    gate = jax.nn.softmax(top_v, axis=-1) * g_val
    expert = g_idx * EXPERTS_PER_GROUP + top_i

    A = T * TOP_K
    e_flat = expert.reshape(A)
    t_flat = jnp.repeat(jnp.arange(T, dtype=jnp.int32), TOP_K)
    g_flat = gate.reshape(A)
    counts = jnp.bincount(e_flat, length=N_EXPERTS)
    padded = (counts + MOE_BLOCK - 1) // MOE_BLOCK * MOE_BLOCK
    pad_end = jnp.cumsum(padded)
    pad_start = pad_end - padded
    raw_start = jnp.cumsum(counts) - counts
    order = jnp.argsort(e_flat)
    e_s = e_flat[order]
    dest = pad_start[e_s] + jnp.arange(A) - raw_start[e_s]
    n_blocks = -(-A // MOE_BLOCK) + N_EXPERTS
    R = n_blocks * MOE_BLOCK
    row_tok = jnp.full((R,), T, jnp.int32).at[dest].set(t_flat[order])
    row_gate = jnp.zeros((R,), jnp.float32).at[dest].set(g_flat[order])
    block_exp = jnp.clip(jnp.searchsorted(pad_end, jnp.arange(n_blocks) * MOE_BLOCK, side="right"),
                         0, N_EXPERTS - 1)

    x_pad = jnp.concatenate([xf, jnp.zeros((1, D), xf.dtype)], axis=0)
    xb = x_pad[row_tok].reshape(n_blocks, MOE_BLOCK, D)

    def expert_block(args):
        xblk, e = args
        return (jax.nn.silu(xblk @ w1[e]) * (xblk @ w3[e])) @ w2[e]

    yb = lax.map(expert_block, (xb, block_exp)).reshape(R, D)
    out = jnp.zeros((T + 1, D), yb.dtype).at[row_tok].add(yb * row_gate[:, None].astype(yb.dtype))
    return out[:T]

def second_inputs(seed: int = 0) -> dict:
    key = jax.random.key(seed)
    ks = jax.random.split(key, 24)
    D = D_MODEL

    def nrm(k, shape, s):
        return jax.random.normal(k, shape, jnp.float32) * s

    return {
        "x": nrm(ks[0], (BATCH, SEQ, D), 1.0),
        "c": nrm(ks[1], (BATCH, D), 1.0),
        "ctx": nrm(ks[2], (BATCH, CTX_LEN, D), 1.0),
        "c_ctx": nrm(ks[3], (D,), 1.0),
        "w_mod": nrm(ks[4], (DEPTH, D, 6 * D), 0.5 * D ** -0.5),
        "b_mod": nrm(ks[5], (DEPTH, 6 * D), 0.01),
        "norm_mix_g": 1.0 + nrm(ks[6], (DEPTH, D), 0.02),
        "norm_ffn_g": 1.0 + nrm(ks[7], (DEPTH, D), 0.02),
        "w_in_even": nrm(ks[8], (N_EVEN, D, EVEN_IN), D ** -0.5),
        "conv_w": nrm(ks[9], (N_EVEN, CONV_K, CONV_WIDTH_2), CONV_K ** -0.5),
        "w_out_even": nrm(ks[10], (N_EVEN, EVEN_OUT, D), EVEN_OUT ** -0.5),
        "w_qkv": nrm(ks[11], (N_ODD, D, QKV_OUT), D ** -0.5),
        "q_norm_g": 1.0 + nrm(ks[12], (N_ODD, HEAD_DIM_2), 0.02),
        "k_norm_g": 1.0 + nrm(ks[13], (N_ODD, HEAD_DIM_2), 0.02),
        "sink_logit": nrm(ks[14], (N_ODD, N_HEADS_2), 1.0),
        "w_o": nrm(ks[15], (N_ODD, Q_DIM, D), Q_DIM ** -0.5),
        "w_router_g": nrm(ks[16], (DEPTH, D, N_GROUPS), D ** -0.5),
        "b_router_g": nrm(ks[17], (DEPTH, N_GROUPS), 0.01),
        "w_router_e": nrm(ks[18], (DEPTH, D, N_EXPERTS), D ** -0.5),
        "b_router_e": nrm(ks[19], (DEPTH, N_EXPERTS), 0.01),
        "w1": nrm(ks[20], (DEPTH, N_EXPERTS, D, D_FF_EXPERT), D ** -0.5),
        "w3": nrm(ks[21], (DEPTH, N_EXPERTS, D, D_FF_EXPERT), D ** -0.5),
        "w2": nrm(ks[22], (DEPTH, N_EXPERTS, D_FF_EXPERT, D), D_FF_EXPERT ** -0.5),
    }

def second_block(x, c, ctx, c_ctx, w_mod, b_mod, norm_mix_g, norm_ffn_g, w_in_even, conv_w, w_out_even,
              w_qkv, q_norm_g, k_norm_g, sink_logit, w_o, w_router_g, b_router_g, w_router_e, b_router_e,
              w1, w3, w2):
    B, L, D = x.shape
    Lc = ctx.shape[1]
    xl, xc = x, ctx
    for layer in range(DEPTH):
        last = layer == DEPTH - 1
        is_even = layer % 2 == 0
        j = layer // 2
        mod_l = (jax.nn.silu(c) @ w_mod[layer] + b_mod[layer])[:, None, :]
        mod_c = jax.nn.silu(c_ctx) @ w_mod[layer] + b_mod[layer]
        sh1_l, sc1_l, g1_l, sh2_l, sc2_l, g2_l = jnp.split(mod_l, 6, axis=-1)
        sh1_c, sc1_c, g1_c, sh2_c, sc2_c, g2_c = jnp.split(mod_c, 6, axis=-1)

        hl = modulate(rms_norm_2(xl, norm_mix_g[layer]), sh1_l, sc1_l)
        if is_even:
            yl = even_mixer(hl, w_in_even[j], conv_w[j], w_out_even[j])
            yc = None
            if not last:
                hc = modulate(rms_norm_2(xc, norm_mix_g[layer]), sh1_c, sc1_c)
                yc = even_mixer(hc, w_in_even[j], conv_w[j], w_out_even[j])
        else:
            hc = modulate(rms_norm_2(xc, norm_mix_g[layer]), sh1_c, sc1_c)
            yl, yc = window_attention(hl, hc, w_qkv[j], q_norm_g[j], k_norm_g[j], sink_logit[j], w_o[j],
                                      not last)
        xl = xl + g1_l * yl

        hl2 = modulate(rms_norm_2(xl, norm_ffn_g[layer]), sh2_l, sc2_l).reshape(B * L, D)
        moe_args = (w_router_g[layer], b_router_g[layer], w_router_e[layer], b_router_e[layer],
                    w1[layer], w3[layer], w2[layer])
        if last:
            xl = xl + g2_l * hier_moe(hl2, *moe_args).reshape(B, L, D)
        else:
            xc = xc + g1_c * yc
            hc2 = modulate(rms_norm_2(xc, norm_ffn_g[layer]), sh2_c, sc2_c).reshape(B * Lc, D)
            f = hier_moe(jnp.concatenate([hl2, hc2], axis=0), *moe_args)
            xl = xl + g2_l * f[:B * L].reshape(B, L, D)
            xc = xc + g2_c * f[B * L:].reshape(B, Lc, D)
    return xl


def setup_inputs(seed=0):
    out = dict(first_inputs(seed))
    for name, value in second_inputs(seed + 1).items():
        if name != "x":
            out[name + "_2"] = value
    return out


def reference(
    x, ffn1_norm, ffn1_w_gate, ffn1_w_up, ffn1_w_down, mix_norm, w_in, conv_dw, conv_dw_bias,
    conv_ln_gain, conv_ln_bias, pool_w, pool_scale, q_norm, k_norm, lambda_q1, lambda_k1,
    lambda_q2, lambda_k2, attn_subln, w_out, ffn2_norm, ffn2_w_gate, ffn2_w_up, ffn2_w_down,
    post_norm, c_2, ctx_2, c_ctx_2, w_mod_2, b_mod_2, norm_mix_g_2, norm_ffn_g_2, w_in_even_2,
    conv_w_2, w_out_even_2, w_qkv_2, q_norm_g_2, k_norm_g_2, sink_logit_2, w_o_2, w_router_g_2,
    b_router_g_2, w_router_e_2, b_router_e_2, w1_2, w3_2, w2_2,
):
    x = first_block(
        x, ffn1_norm, ffn1_w_gate, ffn1_w_up, ffn1_w_down, mix_norm, w_in, conv_dw,
        conv_dw_bias, conv_ln_gain, conv_ln_bias, pool_w, pool_scale, q_norm, k_norm, lambda_q1,
        lambda_k1, lambda_q2, lambda_k2, attn_subln, w_out, ffn2_norm, ffn2_w_gate, ffn2_w_up,
        ffn2_w_down, post_norm,
    )
    return second_block(
        x, c_2, ctx_2, c_ctx_2, w_mod_2, b_mod_2, norm_mix_g_2, norm_ffn_g_2, w_in_even_2,
        conv_w_2, w_out_even_2, w_qkv_2, q_norm_g_2, k_norm_g_2, sink_logit_2, w_o_2,
        w_router_g_2, b_router_g_2, w_router_e_2, b_router_e_2, w1_2, w3_2, w2_2,
    )


_drawn_inputs = setup_inputs


def setup_inputs(seed=0):
    import zlib

    import numpy as np

    out = dict(_drawn_inputs(seed))
    spreads = {}
    factors = {'ffn1_norm': 2.698,
     'conv_dw_bias': 2.738,
     'conv_ln_gain': 4.008,
     'conv_ln_bias': 4.471,
     'q_norm': 3.2,
     'k_norm': 3.308,
     'attn_subln': 3.243,
     'ffn2_norm': 3.976,
     'ctx_2': 2.675,
     'b_mod_2': 2.793,
     'norm_mix_g_2': 4.798,
     'norm_ffn_g_2': 12.941,
     'q_norm_g_2': 45.084,
     'k_norm_g_2': 51.369,
     'sink_logit_2': 8.0,
     'b_router_g_2': 34.945,
     'b_router_e_2': 50.732}
    for name, (base, spread) in spreads.items():
        noise = np.random.default_rng([zlib.crc32(name.encode()), seed]).standard_normal(out[name].shape)
        drawn = base * np.exp(spread * noise) if base else spread * noise
        out[name] = __import__('jax').numpy.asarray(drawn.astype(out[name].dtype))
    for name, factor in factors.items():
        out[name] = (out[name] * factor).astype(out[name].dtype)
    return out
```

```python
from contextlib import ExitStack

import concourse.bass as bass
import numpy as np
from concourse import mybir

ALU = mybir.AluOpType
ACT = mybir.ActivationFunctionType
X = mybir.AxisListType.X
F32 = mybir.dt.float32
U32 = mybir.dt.uint32
I32 = mybir.dt.int32

P = 128
D = 1024
KD = D // P
SEQ = 256
DEPTH = 2
PANELS = 6
PC = 512
FF = 2816
FF_CHUNKS = FF // P
FF_STEPS = -(-FF // PC)
EPS = 1e-6
HEADS = 4
HD = 64
CONV_W = 31
PAD = CONV_W // 2
EXPERTS = 32
GROUPS = 4
PER_GROUP = EXPERTS // GROUPS
NLOG = GROUPS + EXPERTS
POOL_WINDOWS = (2, 4, 8, 16)
TILES = (4, 2)
EXTRA = (8, 4)
BLOCKS = tuple(EXPERTS + e for e in EXTRA)
BLOCK_BASE = (0, BLOCKS[0])
HEADS2 = 16
KV2 = 4
BIG = 1e30
FF_ROWS = (8, 4)


def panel_plan():
    base, g = {}, 0
    stages = [("mod", 24)]
    for l in range(DEPTH):
        stages += [(f"ffn{2 * l}", 3 * FF_STEPS), (f"in{l}", 5), (f"out{l}", 2), (f"ffn{2 * l + 1}", 3 * FF_STEPS)]
    stages += [("even", 4), ("even_out", 2), ("moe0", 3 * BLOCKS[0]),
               ("odd", 3), ("odd_out", 2), ("moe1", 3 * BLOCKS[1])]
    for name, n in stages:
        base[name] = g
        g += n
    return base


def const_table():
    cols, at = [], {}

    def put(name, a):
        a = np.asarray(a, np.float32).reshape(P, -1)
        at[name] = (sum(c.shape[1] for c in cols), a.shape[1])
        cols.append(a)

    i = np.arange(P)
    put("ident", np.eye(P))
    put("tri", i[:, None] < i[None, :])
    put("iota", np.broadcast_to(i, (P, P)))
    put("tokid", i[:, None] + P * np.arange(4)[None, :])
    w = 2 * np.pi * (np.outer(i, i) % P) / P
    put("dft_c", np.cos(w))
    put("dft_ns", -np.sin(w))
    t = np.arange(SEQ)
    freq = (np.float32(10000.0) ** (-np.arange(16, dtype=np.float32) / np.float32(16))).astype(np.float32)
    pos = np.stack([t // 64, t % 64], -1).astype(np.float32)
    ang = (pos[:, :, None] * freq).astype(np.float32).astype(np.float64)
    for name, f in (("cos", np.cos), ("sin", np.sin)):
        put(name, f(ang).reshape(2, P, 32).transpose(1, 0, 2))
    at["resident"] = (0, sum(c.shape[1] for c in cols))
    w = 2 * np.pi * (np.outer(t, t) % SEQ) / SEQ
    s = 1 / np.sqrt(SEQ * P)
    put("dft_l", np.concatenate([np.cos(w) * s, np.sin(w) * s], 1).reshape(2, P, 2 * SEQ).transpose(1, 0, 2))
    dist = np.abs(t[:, None] - t[None, :])
    put("window", np.where(dist <= 128, 0.0, -BIG).reshape(2, P, SEQ).transpose(1, 0, 2))
    put("ndist", (-dist).reshape(2, P, SEQ).transpose(1, 0, 2))
    band = np.zeros((4, SEQ, SEQ))
    for g, wd in enumerate(POOL_WINDOWS):
        lo, hi = np.clip(t - wd // 2, 0, SEQ), np.clip(t + wd // 2, 0, SEQ)
        inside = (t[:, None] >= lo[None, :]) & (t[:, None] < hi[None, :])
        band[g] = inside / (hi - lo)[None, :] - np.eye(SEQ)
    put("band", band.reshape(4, 2, P, SEQ).transpose(2, 1, 0, 3))
    return np.ascontiguousarray(np.concatenate(cols, 1)), at


def build(nc, A, out):
    G0 = panel_plan()
    _, CA = const_table()
    lam_init = [0.8 - 0.6 * float(np.exp(-0.3 * l)) for l in range(DEPTH)]
    slopes = [float(np.exp2(np.float32(-8.0 * (h + 1) / HEADS))) for h in range(HEADS)]

    mod_dram = nc.dram_tensor("mod_rows", (2, 2 * 6 * D), F32, kind="Internal").ap()
    h_dram = nc.dram_tensor("router_rows", (4 * P, D), F32, kind="Internal").ap()
    y_dram = nc.dram_tensor("expert_rows", (BLOCKS[0] * P, D), F32, kind="Internal").ap()

    with ExitStack() as ctx:
        def sb(name, shape, dt=F32):
            return ctx.enter_context(nc.sbuf_tensor(name, shape, dt))

        def sem(name):
            return ctx.enter_context(nc.semaphore(name))

        ring = sb("ring", [P, PANELS, KD * PC])
        xres = sb("x_rows", [P, 4, D])
        W = sb("work", [P, 20480])
        gain = sb("gain_rows", [P, D])
        K = sb("consts", [P, CA["resident"][1]])
        ones = sb("ones", [P, P])
        ones_c = sb("ones_over_256", [P, P])
        router_w = sb("router_w", [P, DEPTH, KD, NLOG])
        router_b = sb("router_b", [P, DEPTH, NLOG])
        rows2 = sb("rows2", [P, 2 * HD + HEADS2])
        conv2_w = sb("conv2_w", [P, 4, 3])
        cond = sb("cond", [P, KD, 2])
        eps = sb("eps", [P, 1])
        ss = sb("sum_squares", [P, 64])
        std = sb("std", [P, 64])
        rs = sb("rstd", [P, 64])
        var = sb("variance", [P, 64])
        rt = sb("rstd_error", [P, 64])
        slot_id = sb("slot_of_token", [P, 4, 2], U32)
        gates = sb("gates", [P, 2, 4])
        table = sb("token_of_slot", [P, BLOCKS[0]], U32)
        table_col = sb("token_of_slot_col", [P, 2], U32)
        extra_id = sb("extra_expert", [P, 8], I32)
        ps = ctx.enter_context(nc.psum_tensor("ps", [P, 8, PC], F32))
        psf = ps[:, :, :].rearrange("p b c -> p (b c)")

        def k(name):
            a, n = CA[name]
            return K[:, a:a + n]

        def w(a, n):
            return W[:, a:a + n]

        ident, tri, iota = k("ident"), k("tri"), k("iota")
        R0, R1, R2, R3 = 0, 4096, 8192, 12288
        hrow = w(R0, 4096).rearrange("p (t d) -> p t d", t=4)

        hT1 = w(R0 + 2048, 2048)
        sg1 = w(R1, 1024).rearrange("p (b n) -> p b n", b=4)
        aT1 = w(R1 + 1024, 1024).rearrange("p (b n) -> p b n", b=4)
        yT1 = w(R1 + 2048, 2048).rearrange("p (k n) -> p k n", k=KD)
        zpad = w(R1, 2 * (SEQ + 2 * PAD)).rearrange("p (c n) -> p c n", c=2)
        conv_acc = w(R1 + 576, 512).rearrange("p (c n) -> p c n", c=2)
        sig = w(R1 + 1088, 512).rearrange("p (c n) -> p c n", c=2)
        up = w(R2, 512).rearrange("p (t n) -> p t n", t=2)
        dT = w(R2 + 512, 512).rearrange("p (c n) -> p c n", c=2)
        sqt = w(R2 + 1024, 1024)
        qn = w(R2 + 2048, 1024)
        kn = w(R2 + 3072, 1024)
        qT = w(R0, 1024).rearrange("p (h n) -> p h n", h=4)
        kT = w(R0 + 1024, 1024).rearrange("p (h n) -> p h n", h=4)
        ndist = w(R3, 512).rearrange("p (t n) -> p t n", t=2)
        band = w(R3 + 512, 2048).rearrange("p (t g n) -> p t g n", t=2, g=4)
        rows1 = w(R3 + 2560, 1024).rearrange("p (l n) -> p l n", l=2)
        pool_bd = w(R3 + 3584, 512).rearrange("p (l c n) -> p l c n", l=2, c=2)
        v1 = w(R3 + 4096, 1024).rearrange("p (t n) -> p t n", t=2)
        s1 = w(R3 + 5120, 1024).rearrange("p (b n) -> p b n", b=2)
        p1 = w(R3 + 6144, 1024).rearrange("p (b n) -> p b n", b=2)
        a1 = w(R3 + 7168, 512).rearrange("p (b n) -> p b n", b=2)
        at1 = w(R3 + 7680, 512).rearrange("p (b n) -> p b n", b=2)
        osq = w(R2 + 1024, 512)
        on = w(R2 + 1536, 512)
        cols1 = sb("cols1", [P, DEPTH, 2 * CONV_W + 8])
        lam = sb("lam", [P, 8])
        m1 = sb("row_stats", [P, 2, 8])

        modrow = W[0:2, 0:12288]
        hT2 = w(R1, 4096)
        yT2 = w(R2, 4096)
        sc_rows = w(R3, 2048).rearrange("p (s d) -> p s d", s=2)
        sh_rows = w(R3 + 2048, 2048).rearrange("p (s d) -> p s d", s=2)
        g_rows = w(R3 + 4096, 2048).rearrange("p (s d) -> p s d", s=2)
        a_rows = w(R0, 2048).rearrange("p (t n) -> p t n", t=4)
        pt = w(R0 + 2048, 1024).rearrange("p (b n) -> p b n", b=2)
        dft_l = w(R0 + 3072, 1024).rearrange("p (t n) -> p t n", t=2)
        bT = w(R3, 2048).rearrange("p (j n) -> p j n", j=4)
        cT = w(R3 + 2048, 2048).rearrange("p (j n) -> p j n", j=4)
        upad = w(R3 + 6144, 1032).rearrange("p (b s n) -> p b s n", b=2, s=2)
        prod = w(R3, 1024)
        q2 = w(R0, 2048).rearrange("p (t n) -> p t n", t=2)
        kdup = w(R0 + 2048, 2048).rearrange("p (t h c n) -> p t h c n", t=4, h=4, c=2)
        qT2 = w(R2 + 2048, 2048).rearrange("p (k n) -> p k n", k=8)
        yTo = w(R2, 2048).rearrange("p (k n) -> p k n", k=8)
        kT2 = w(R3, 2048).rearrange("p (h n) -> p h n", h=4)
        v2 = w(R3 + 2048, 1024).rearrange("p (t n) -> p t n", t=4)
        window = w(R3 + 3072, 512).rearrange("p (t n) -> p t n", t=2)
        rope_a = w(R3, 1024)
        rope_b = w(R3 + 1024, 1024)
        sq2 = w(R2, 2048)
        s2 = w(R1, 1024).rearrange("p (b n) -> p b n", b=2)
        p2 = w(R1 + 1024, 1024).rearrange("p (b n) -> p b n", b=2)
        pT2 = w(R1 + 2048, 1024).rearrange("p (b n) -> p b n", b=2)

        xg = w(R0, 2048).rearrange("p (b n) -> p b n", b=2)
        xgT = w(R0 + 2048, 2048).rearrange("p (b n) -> p b n", b=2)
        ysb = w(R1, 2048).rearrange("p (b n) -> p b n", b=2)
        sgm = w(R1 + 2048, 1024).rearrange("p (b j n) -> p b j n", b=2, j=4)
        aTm = w(R1 + 3072, 1024).rearrange("p (b j n) -> p b j n", b=2, j=4)
        yg = w(R0, 4096).rearrange("p (b c n) -> p b c n", b=2, c=2)

        def r(at, *shape):
            v = w(R2 + at, int(np.prod(shape)))
            return v if len(shape) == 1 else v.rearrange(
                {2: "p (a b) -> p a b", 3: "p (a b c) -> p a b c"}[len(shape)],
                **dict(zip("abc", shape)))

        r_logit = r(0, 4, NLOG)
        r_gexp = r(144, 4, GROUPS)
        r_goh = r(160, 4, GROUPS)
        r_gcand = r(176, 4, GROUPS)
        r_gneg = r(192, 4, GROUPS)
        r_em = r(256, 4, EXPERTS)
        r_em2 = r(384, 4, EXPERTS)
        r_cand = r(512, 4, EXPERTS)
        r_oh1 = r(640, 4, EXPERTS)
        r_oh2 = r(768, 4, EXPERTS)
        r_mem = r(896, 4, EXPERTS)
        r_slot = r(1024, 4, EXPERTS)
        r_tmp = r(1152, 4, EXPERTS)
        r_cnt = r(1280, EXPERTS)
        r_nx = r(1312, EXPERTS)
        r_t1 = r(1344, EXPERTS)
        r_xs = r(1376, EXPERTS)
        r_shift = r(1408, EXPERTS)
        r_ex = r(1440, 8, EXPERTS)
        r_ex2 = r(1696, 8, EXPERTS)
        r_exid = r(1952, 8)
        r_s = r(1960, 16, 4)
        r_sl = r(2032, 2, 4)
        r_sli = r(2040, 2, 4).bitcast(I32)
        r_blki = r(2048, 2, 4).bitcast(I32)
        r_ini = r(2056, 2, 4).bitcast(I32)
        r_blkf = r(2064, 2, 4)
        r_inf = r(2072, 2, 4)
        r_blk = r(2080, 8, 40)
        r_onehot = r(2400, 8, P)

        landed = [sem(f"panel_landed_{i}") for i in range(PANELS)]
        panel_done = sem("panel_done")
        x_landed = sem("x_landed")
        const_landed = sem("const_landed")
        cond_landed = sem("cond_landed")
        bmod_landed = sem("bmod_landed")
        ones_ready = sem("ones_ready")
        cond_ready = sem("cond_ready")
        mod_copied = sem("mod_copied")
        mod_stored = sem("mod_stored")
        gain_landed = sem("gain_landed")
        modb_landed = sem("mod_rows_landed")
        ms_ready = sem("mean_square_ready")
        std_ready = sem("std_ready")
        row_ready = sem("row_ready")
        tr_ready = sem("transposed_ready")
        hT_act = sem("hT_by_act")
        hT_dve = sem("hT_by_dve")
        gu_ready = sem("gate_up_ready")
        silu_ready = sem("silu_ready")
        act_ready = sem("activated_ready")
        x_ready = sem("residual_ready")
        sig_ready = sem("sigmoid_ready")
        z_ready = sem("glu_ready")
        conv_ready = sem("conv_ready")
        up_ready = sem("pool_rows_ready")
        dps_ready = sem("pool_diff_ready")
        dT_ready = sem("pool_diff_copied")
        pp_ready = sem("pool_product_ready")
        mean_ready = sem("mean_ready")
        xsq_ready = sem("centred_square_ready")
        var_ready = sem("variance_ready")
        lnstd_ready = sem("ln_std_ready")
        ln_ready = sem("ln_ready")
        yT_ready = sem("mixed_T_ready")
        sq_ready = sem("squares_ready")
        qks_ready = sem("qk_sums_ready")
        qkstd_ready = sem("qk_std_ready")
        qkn_ready = sem("qk_normed_ready")
        qkt_ready = sem("qk_transposed_ready")
        qkT_ready = sem("qkT_ready")
        v_ready = sem("v_ready")
        sc_ready = sem("scores_ready")
        s_ready = sem("scores_biased_ready")
        p_ready = sem("exp_ready")
        a_ready = sem("weights_ready")
        at_ready = sem("weights_transposed_ready")
        aT_ready = sem("weightsT_ready")
        o_ready = sem("attended_ready")
        osq_ready = sem("attended_square_ready")
        oss_ready = sem("attended_sums_ready")
        ostd_ready = sem("attended_std_ready")
        on_ready = sem("attended_normed_ready")
        ot_ready = sem("attended_transposed_ready")
        lam_ready = sem("lambda_dots_ready")
        lame_ready = sem("lambda_exp_ready")
        acopy = sem("fourier_rows_ready")
        bcopy = sem("b_gate_ready")
        ccopy = sem("c_gate_ready")
        dftl_landed = sem("dft_l_landed")
        pt_ready = sem("dft_seq_ready")
        ptc_ready = sem("dft_seq_copied")
        f_ready = sem("dft_chan_ready")
        fc_ready = sem("dft_chan_copied")
        conv2_ready = sem("short_conv_ready")
        q2_ready = sem("q2_ready")
        k2_ready = sem("k2_ready")
        v2_ready = sem("v2_ready")
        h_stored = sem("router_rows_stored")
        logit_ready = sem("logits_ready")
        gmax_ready = sem("group_max_ready")
        gexp_ready = sem("group_exp_ready")
        top_ready = sem("top_two_ready")
        texp_ready = sem("top_exp_ready")
        member_ready = sem("membership_ready")
        pos_ready = sem("positions_ready")
        onehot_ready = sem("slot_onehots_ready")
        tps_ready = sem("table_product_ready")
        table_ready = sem("table_ready")
        xg_landed = [sem(f"gathered_{i}") for i in range(2)]
        xgt_ready = sem("gathered_transposed")
        xgT_act = sem("gatheredT_by_act")
        xgT_dve = sem("gatheredT_by_dve")
        mgu_ready = sem("expert_gate_up_ready")
        msilu_ready = sem("expert_silu_ready")
        mact_ready = sem("expert_activated_ready")
        y_act = sem("expert_out_by_act")
        y_dve = sem("expert_out_by_dve")
        y_stored = [sem(f"expert_out_stored_{i}") for i in range(2)]
        yg_landed = [sem(f"expert_rows_landed_{i}") for i in range(2)]
        combined = sem("tile_combined")
        out_stored = sem("out_stored")

        NORMS = [2, 2, 2, 0, 2, 2, 2, 0, 4, 4, 4, 2]
        TILE0 = [sum(NORMS[:n]) for n in range(13)]
        BANK0 = [2 * t for t in TILE0]
        gain_src = []
        for l in range(DEPTH):
            gain_src += [A["ffn1_norm"][l], A["mix_norm"][l], A["ffn2_norm"][l], A["post_norm"][l]]
        for l in range(DEPTH):
            gain_src += [A["norm_mix_g_2"][l], A["norm_ffn_g_2"][l]]
        MODB = [6 * 16, 12 * 16, 17 * 16, 20 * 16]

        def slot(g):
            return ring[:, g % PANELS, :].rearrange("p (k n) -> p k n", k=KD)

        def slot_down(g):
            return ring[:, g % PANELS, :].rearrange("p (k n) -> p k n", k=4)

        def hT_wait(pe, n):
            pe.wait_ge(hT_act, BANK0[n + 1] // 2)
            pe.wait_ge(hT_dve, BANK0[n + 1] // 2)

        CONST_DMAS = 11

        block = ctx.enter_context(nc.Block())

        @block.sync
        def _(sp):
            def load(g, j, dst, src):
                if not isinstance(g, int) or g >= PANELS:
                    sp.wait_ge(panel_done, g - PANELS + 1)
                sp.dma_start(dst, src).then_inc(landed[j], 16)

            def wide(wt, c0, n=PC):
                return wt.rearrange("(k p) n -> p k n", p=P)[:, :, bass.ds(c0, n)]

            def down(wt, r0, n=4):
                return wt.rearrange("(k p) n -> p k n", p=P)[:, bass.ds(r0, n), :]

            def expert(wt, e):
                return wt.rearrange("e (k p) n -> e p k n", p=P)[bass.ds(e, 1)].rearrange("a p k n -> p (a k) n")

            sp.dma_start(xres[:, 0:2, :], A["x"][0].rearrange("(t p) d -> p t d", p=P)).then_inc(x_landed, 16)
            wmod = A["w_mod_2"].rearrange("l (k p) n -> l p k n", p=P)
            for l in range(DEPTH):
                if l == 0:
                    for j in range(6):
                        load(j, j, slot(j), wmod[l, :, :, PC * j:PC * (j + 1)])
                with sp.Fori(1 - l, 2) as i:
                    for j in range(6):
                        load(12 * l + 6 * i + j, j, slot(j), wmod[l][:, :, bass.ds(6 * PC * i + PC * j, PC)])

            def ffn(f, wg, wu, wd):
                g0 = G0[f"ffn{f}"]

                def step(s, j, n=PC):
                    load(g0 + 3 * s, (g0 + j) % PANELS, slot(g0 + j)[:, :, 0:n], wide(wg, s * PC, n))
                    load(g0 + 3 * s + 1, (g0 + j + 1) % PANELS, slot(g0 + j + 1)[:, :, 0:n], wide(wu, s * PC, n))
                    load(g0 + 3 * s + 2, (g0 + j + 2) % PANELS, slot_down(g0 + j + 2)[:, 0:n // P, :],
                         down(wd, s * 4, n // P))

                step(0, 0)
                with sp.Fori(0, 2) as i:
                    step(2 * i + 1, 3)
                    step(2 * i + 2, 0)
                step(FF_STEPS - 1, 3, FF - (FF_STEPS - 1) * PC)

            for l in range(DEPTH):
                ffn(2 * l, A["ffn1_w_gate"][l], A["ffn1_w_up"][l], A["ffn1_w_down"][l])
                for j, (c0, n) in enumerate([(0, 512), (512, 256), (768, 512), (1280, 512), (1792, 512)]):
                    g = G0[f"in{l}"] + j
                    load(g, g % PANELS, slot(g)[:, :, 0:n], wide(A["w_in"][l], c0, n))
                for j in range(2):
                    g = G0[f"out{l}"] + j
                    load(g, g % PANELS, slot(g), wide(A["w_out"][l], PC * j))
                ffn(2 * l + 1, A["ffn2_w_gate"][l], A["ffn2_w_up"][l], A["ffn2_w_down"][l])

            def panels(name, wt, cols):
                for j, c0 in enumerate(cols):
                    g = G0[name] + j
                    load(g, g % PANELS, slot(g), wide(wt, c0))

            def moe(l):
                g0 = G0[f"moe{l}"]
                w1, w3, w2 = (A[n][l] for n in ("w1_2", "w3_2", "w2_2"))

                def triple(b, j, e):
                    load(g0 + 3 * b, (g0 + j) % PANELS, slot(g0 + j), expert(w1, e))
                    load(g0 + 3 * b + 1, (g0 + j + 1) % PANELS, slot(g0 + j + 1), expert(w3, e))
                    load(g0 + 3 * b + 2, (g0 + j + 2) % PANELS, slot_down(g0 + j + 2), expert(w2, e))

                with sp.Fori(0, EXPERTS // 2) as i:
                    triple(2 * i, 0, 2 * i)
                    triple(2 * i + 1, 3, 2 * i + 1)
                sp.wait_ge(table_ready, l + 1)
                for n in range(EXTRA[l]):
                    e = sp.value_load(extra_id[0:1, n:n + 1], min_val=0, max_val=EXPERTS - 1)
                    triple(EXPERTS + n, 3 * (n % 2), e)

            panels("even", A["w_in_even_2"][0], [0, 512, 1024, 1536])
            panels("even_out", A["w_out_even_2"][0], [0, 512])
            moe(0)
            panels("odd", A["w_qkv_2"][0], [0, 512, 1024])
            panels("odd_out", A["w_o_2"][0], [0, 512])
            moe(1)

        @block.tensor
        def _(pe):
            def arrived(g, i6=0):
                pe.wait_ge(landed[g % PANELS], 16 * (g // PANELS + 1) + 16 * i6)

            def norm_T(n):
                nt = NORMS[n]
                pe.wait_ge(row_ready, TILE0[n + 1])
                for j in range(2 * nt):
                    for q in range(4):
                        kk, t = (2 * j + q // 2, q % 2) if nt == 2 else (j, q)
                        mm = pe.transpose(ps[:, j, q * P:(q + 1) * P], hrow[:, t, kk * P:(kk + 1) * P], ident)
                    mm.then_inc(tr_ready, 1)

            def rows_product(g, lhs, nt, out_at, c0=0, n=PC, tile_first=0):
                arrived(g)
                for t in range(nt):
                    for kk in range(KD):
                        mm = pe.matmul(out_at(t), lhs(kk, t), slot(g)[:, kk, c0:c0 + n],
                                       start=kk == 0, stop=kk == KD - 1)
                mm.then_inc(panel_done, 1)

            def mod_panels(i, first):
                for j in range(6):
                    arrived(j, i)
                    if not first:
                        pe.wait_ge(mod_copied, 6 * i + j - 5)
                    for kk in range(KD):
                        mm = pe.matmul(ps[0:2, j, :], cond[:, kk, :], slot(j)[:, kk, :],
                                       start=kk == 0, stop=kk == KD - 1)
                    mm.then_inc(panel_done, 1)

            pe.wait_ge(cond_ready, 1)
            mod_panels(0, True)
            with pe.Fori(1, 4) as i:
                mod_panels(i, False)
            pe.wait_ge(mod_copied, 24)
            pe.wait_ge(const_landed, 16 * CONST_DMAS)
            pe.wait_ge(ones_ready, 1)

            def ffn(f, n):
                g0 = G0[f"ffn{f}"]
                c0 = FF_CHUNKS * f
                hT_wait(pe, n)

                def gate_up(c, j, s_g, nch, i6=0, first=False):
                    if j == 0:
                        arrived(s_g, i6)
                        arrived(s_g + 1, i6)
                    if not first:
                        pe.wait_ge(act_ready, c0 + c - 3)
                    b = 4 + j % 4 if nch == 4 else 4 + j
                    for half in range(2):
                        for kk in range(KD):
                            mm = pe.matmul(ps[:, b, half * 256:half * 256 + 256],
                                           slot(s_g + half)[:, kk, j * P:(j + 1) * P],
                                           hT1[:, kk * 256:(kk + 1) * 256], start=kk == 0, stop=kk == KD - 1)
                        if half == 0 and j == nch - 1:
                            mm.then_inc(panel_done, 1)
                    mm.then_inc(gu_ready, 1)

                def ffn_down(c, j, s_g, nch, i6=0, start=False, stop=False):
                    if j == 0:
                        arrived(s_g + 2, i6)
                    pe.wait_ge(act_ready, c0 + c + 1)
                    for t in range(2):
                        for half in range(2):
                            mm = pe.matmul(ps[:, 2 * t + half, :], aT1[:, j % 4, t * P:(t + 1) * P],
                                           slot_down(s_g + 2)[:, j, half * PC:(half + 1) * PC],
                                           start=start, stop=stop)
                    if j >= nch - 2:
                        mm.then_inc(panel_done, 1)

                def step(s, jp, nch=4, i6=0, prev=True, pi6=0, last=False):
                    for j in range(nch):
                        c = 4 * s + j
                        gate_up(c, j, g0 + jp, nch, i6, first=isinstance(s, int) and s == 0)
                        if j > 0:
                            ffn_down(c - 1, j - 1, g0 + jp, nch, i6, start=isinstance(s, int) and s == 0 and j == 1)
                        elif prev:
                            ffn_down(c - 1, 3, g0 + (jp + 3) % 6 + (0 if jp == 3 else 0), 4, pi6)
                    if last:
                        ffn_down(c, nch - 1, g0 + jp, nch, i6, stop=True)

                step(0, 0, prev=False)
                with pe.Fori(0, 2) as i:
                    step(2 * i + 1, 3, i6=i, pi6=i)
                    step(2 * i + 2, 0, i6=i + 1, pi6=i)
                step(FF_STEPS - 1, 3, nch=2, i6=2, pi6=2, last=True)

            def mix1(l):
                n = 4 * l + 1
                g = G0[f"in{l}"]
                hT = lambda kk, t: hT1[:, kk * 256 + t * P:kk * 256 + (t + 1) * P]
                hT_wait(pe, n)
                arrived(g)
                for m in range(4):
                    for kk in range(KD):
                        mm = pe.matmul(ps[:, m // 2, (m % 2) * 256:(m % 2) * 256 + 256],
                                       slot(g)[:, kk, m * P:(m + 1) * P], hT1[:, kk * 256:(kk + 1) * 256],
                                       start=kk == 0, stop=kk == KD - 1)
                mm.then_inc(panel_done, 1)
                rows_product(g + 1, hT, 2, lambda t: ps[:, 2, t * 256:(t + 1) * 256], n=256)
                rows_product(g + 2, hT, 2, lambda t: ps[:, 3 + t, :])
                rows_product(g + 3, hT, 2, lambda t: ps[:, 5 + t, :])
                pe.wait_ge(up_ready, l + 1)
                for grp in range(4):
                    r = 64 * (grp % 2)
                    for t in range(2):
                        mm = pe.matmul(ps[r:r + 64, 2, (grp // 2) * 256:(grp // 2) * 256 + 256],
                                       up[:, t, grp * 64:(grp + 1) * 64], band[:, t, grp, :],
                                       start=t == 0, stop=t == 1)
                mm.then_inc(dps_ready, 1)
                pe.wait_ge(z_ready, l + 1)
                rows_product(g + 4, hT, 2, lambda t: ps[:, (7, 0)[t], :])
                pe.wait_ge(dT_ready, l + 1)
                for c in range(2):
                    mm = pe.matmul(ps[:, 2, c * 256:(c + 1) * 256], pool_bd[:, l, c, :], dT[:, c, :],
                                   start=True, stop=True)
                mm.then_inc(pp_ready, 1)
                pe.wait_ge(conv_ready, l + 1)
                for c in range(2):
                    mm = pe.matmul(ps[:, 1, 0:256], ones_c[:, :], conv_acc[:, c, :], start=c == 0, stop=c == 1)
                mm.then_inc(mean_ready, 1)
                for i, src in enumerate((qn, kn)):
                    pe.wait_ge(qkn_ready, 2 * l + i + 1)
                    for t in range(2):
                        for h in range(4):
                            mm = pe.transpose(ps[:, 3 + 2 * i + t, h * P:(h + 1) * P],
                                              src[:, t * 512 + h * P:t * 512 + (h + 1) * P], ident)
                    mm.then_inc(qkt_ready, 1)
                pe.wait_ge(xsq_ready, l + 1)
                for c in range(2):
                    mm = pe.matmul(ps[:, 1, 256:512], ones_c[:, :], sig[:, c, :], start=c == 0, stop=c == 1)
                mm.then_inc(var_ready, 1)
                pe.wait_ge(qkT_ready, 2 * l + 2)
                pe.wait_ge(v_ready, l + 1)
                pe.wait_ge(ln_ready, l + 1)

                def scores(i):
                    qt, h = divmod(i, 4)
                    if i >= 2:
                        pe.wait_ge(s_ready, 8 * l + i - 1)
                    for c in range(2):
                        mm = pe.matmul(ps[:, 3 + 2 * (i % 2) + c, 0:256],
                                       qT[64 * c:64 * c + 64, h, qt * P:(qt + 1) * P],
                                       kT[64 * c:64 * c + 64, h, :], start=True, stop=True)
                    mm.then_inc(sc_ready, 1)

                def attend(i):
                    qt, h = divmod(i, 4)
                    pe.wait_ge(a_ready, 8 * l + i + 1)
                    for t in range(2):
                        mm = pe.transpose(ps[:, 1, (i % 2) * 256 + t * P:(i % 2) * 256 + (t + 1) * P], a1[:, i % 2, t * P:(t + 1) * P], ident)
                    mm.then_inc(at_ready, 1)
                    pe.wait_ge(aT_ready, 8 * l + i + 1)
                    for t in range(2):
                        mm = pe.matmul(ps[:, (7, 0)[qt], h * P:(h + 1) * P], at1[:, i % 2, t * P:(t + 1) * P],
                                       v1[:, t, h * P:(h + 1) * P], start=t == 0, stop=t == 1)
                    mm.then_inc(o_ready, 1)

                def attended_T(qt):
                    pe.wait_ge(yT_ready, 5 * l + 2 + 2 * qt)
                    pe.wait_ge(on_ready, 2 * l + qt + 1)
                    for h in range(4):
                        mm = pe.transpose(ps[:, 2, h * P:(h + 1) * P], on[:, h * P:(h + 1) * P], ident)
                    mm.then_inc(ot_ready, 1)

                for i in range(9):
                    if i < 8:
                        scores(i)
                    if i >= 1:
                        attend(i - 1)
                    if i == 5:
                        attended_T(0)
                attended_T(1)
                pe.wait_ge(yT_ready, 5 * l + 5)
                for half in range(2):
                    rows_product(G0[f"out{l}"] + half, lambda kk, t: yT1[:, kk, t * P:(t + 1) * P], 2,
                                 lambda t: ps[:, 2 * t + half, :])

            for l in range(DEPTH):
                norm_T(4 * l)
                ffn(2 * l, 4 * l)
                norm_T(4 * l + 1)
                mix1(l)
                norm_T(4 * l + 2)
                ffn(2 * l + 1, 4 * l + 2)

            hT4 = lambda kk, t: hT2[:, kk * 512 + t * P:kk * 512 + (t + 1) * P]
            hT2t = lambda kk, t: hT2[:, kk * 256 + t * P:kk * 256 + (t + 1) * P]

            def even():
                g = G0["even"]
                norm_T(8)
                hT_wait(pe, 8)
                rows_product(g, hT4, 4, lambda t: ps[:, t, :])

                def chans(gg, b0):
                    arrived(gg)
                    for m in range(4):
                        for kk in range(KD):
                            mm = pe.matmul(ps[:, b0 + m, :], slot(gg)[:, kk, m * P:(m + 1) * P],
                                           hT2[:, kk * 512:(kk + 1) * 512], start=kk == 0, stop=kk == KD - 1)
                    mm.then_inc(panel_done, 1)

                chans(g + 1, 4)
                pe.wait_ge(acopy, 4)
                chans(g + 2, 0)
                pe.wait_ge(bcopy, 4)
                chans(g + 3, 4)
                pe.wait_ge(ccopy, 4)
                pe.wait_ge(dftl_landed, 16)

                def along_seq(i):
                    s, grp = divmod(i, 4)
                    if i >= 2:
                        pe.wait_ge(ptc_ready, i - 1)
                    for t in range(2):
                        mm = pe.matmul(ps[:, i % 2, :], a_rows[:, 2 * s + t, grp * P:(grp + 1) * P], dft_l[:, t, :],
                                       start=t == 0, stop=t == 1)
                    mm.then_inc(pt_ready, 1)

                def along_chan(i):
                    pe.wait_ge(ptc_ready, i + 1)
                    if i >= 2:
                        pe.wait_ge(fc_ready, i - 1)
                    pe.matmul(ps[:, 2 + i % 2, 0:256], k("dft_c"), pt[:, i % 2, 0:256], start=True, stop=False)
                    pe.matmul(ps[:, 2 + i % 2, 0:256], k("dft_ns"), pt[:, i % 2, 256:512],
                              start=False, stop=True).then_inc(f_ready, 1)

                for i in range(9):
                    if i < 8:
                        along_seq(i)
                    if i >= 1:
                        along_chan(i - 1)
                pe.wait_ge(fc_ready, 8)
                pe.wait_ge(conv2_ready, 4)
                for half in range(2):
                    rows_product(G0["even_out"] + half, lambda kk, t: yT2[:, kk * 512 + t * P:kk * 512 + (t + 1) * P],
                                 4, lambda t: ps[:, 2 * t + half, :])

            def moe(m):
                nt, n = TILES[m], 9 + 2 * m
                nb, b0, g0 = BLOCKS[m], BLOCK_BASE[m], G0[f"moe{m}"]
                norm_T(n)
                hT_wait(pe, n)
                lhs = hT4 if nt == 4 else hT2t
                for t in range(nt):
                    for kk in range(KD):
                        mm = pe.matmul(ps[:, 0, t * NLOG:(t + 1) * NLOG], lhs(kk, t), router_w[:, m, kk, :],
                                       start=kk == 0, stop=kk == KD - 1)
                mm.then_inc(logit_ready, 1)
                pe.wait_ge(member_ready, m + 1)
                for t in range(nt + 1):
                    for u in range(min(t + 1, nt)):
                        mm = pe.matmul(ps[:, 1, t * 32:(t + 1) * 32], tri if u == t else ones[:, :], r_mem[:, u, :],
                                       start=u == 0, stop=u == min(t, nt - 1))
                mm.then_inc(pos_ready, 1)
                pe.wait_ge(onehot_ready, m + 1)
                for i in range(2 * nt):
                    mm = pe.matmul(ps[:, 2, 0:nb], r_onehot[:, i, :], r_blk[:, i, 0:nb], start=i == 0, stop=i == 2 * nt - 1)
                mm.then_inc(tps_ready, 1)
                pe.wait_ge(table_ready, m + 1)

                def turn(b, par):
                    pe.wait_ge(xg_landed[par], 8 * b0 + 8 * (b - par) + 16)
                    for kk in range(KD):
                        mm = pe.transpose(psf[:, kk * P:(kk + 1) * P], xg[:, par, kk * P:(kk + 1) * P], ident)
                    mm.then_inc(xgt_ready, 1)

                def expert(b, par, i6, turn_next=True):
                    pe.wait_ge(xgT_act, b0 + b + 1)
                    pe.wait_ge(xgT_dve, b0 + b + 1)
                    g = g0 + 3 * par
                    arrived(g, i6)
                    arrived(g + 1, i6)
                    for j in range(4):
                        for half in range(2):
                            at = half * P
                            for kk in range(KD):
                                mm = pe.matmul(ps[:, 2 + j, at:at + P], slot(g + half)[:, kk, j * P:(j + 1) * P],
                                               xgT[:, par, kk * P:(kk + 1) * P], start=kk == 0, stop=kk == KD - 1)
                            if half == 0 and j == 3:
                                mm.then_inc(panel_done, 1)
                        mm.then_inc(mgu_ready, 1)
                    if turn_next:
                        turn(b + 1, 1 - par)
                    arrived(g + 2, i6)
                    if not (isinstance(b, int) and b0 + b == 0):
                        pe.wait_ge(y_act, b0 + b)
                        pe.wait_ge(y_dve, b0 + b)
                    pe.wait_ge(mact_ready, 4 * (b0 + b) + 4)
                    for half in range(2):
                        for j in range(4):
                            mm = pe.matmul(ps[:, 6 + half, :], aTm[:, par, j, :],
                                           slot_down(g + 2)[:, j, half * PC:(half + 1) * PC],
                                           start=j == 0, stop=j == 3)
                        mm.then_inc(panel_done, 1)

                turn(0, 0)
                expert(0, 0, 0)
                expert(1, 1, 0)
                with pe.Fori(1, nb // 2 - 1) as i:
                    expert(2 * i, 0, i)
                    expert(2 * i + 1, 1, i)
                expert(nb - 2, 0, nb // 2 - 1)
                expert(nb - 1, 1, nb // 2 - 1, turn_next=False)

            def odd():
                g = G0["odd"]
                norm_T(10)
                hT_wait(pe, 10)
                for half in range(2):
                    rows_product(g + half, hT4, 2, lambda t: ps[:, 2 * t + half, :])
                rows_product(g + 2, hT4, 4, lambda t: ps[:, 4 + t, :])
                pe.wait_ge(q2_ready, 1)
                for b in range(4):
                    t, j = divmod(b, 2)
                    for c in range(4):
                        mm = pe.transpose(ps[:, b, c * P:(c + 1) * P],
                                          q2[:, t, (4 * j + c) * P:(4 * j + c + 1) * P], ident)
                    mm.then_inc(qkt_ready, 1)
                pe.wait_ge(k2_ready, 1)
                pe.wait_ge(v2_ready, 4)
                for h in range(4):
                    for t in range(4):
                        mm = pe.transpose(ps[:, 4 + h, t * P:(t + 1) * P],
                                          kdup[:, t, h, :, :].rearrange("p c n -> p (c n)"), ident)
                    mm.then_inc(qkt_ready, 1)
                pe.wait_ge(qkT_ready, 4 + 8)

                def scores(i):
                    h, qt = divmod(i, 2)
                    r = 64 * (h % 2)
                    if i >= 2:
                        pe.wait_ge(s_ready, 16 + i - 1)
                    pe.matmul(ps[:, i % 2, :], qT2[r:r + 64, h // 2, qt * P:(qt + 1) * P],
                              kT2[r:r + 64, h // 4, :], start=True, stop=True).then_inc(sc_ready, 1)

                def attend(i):
                    h, qt = divmod(i, 2)
                    r = 64 * (h % 2)
                    pe.wait_ge(a_ready, 16 + i + 1)
                    for t in range(4):
                        mm = pe.transpose(ps[:, 2 + i % 2, t * P:(t + 1) * P], p2[:, i % 2, t * P:(t + 1) * P], ident)
                    mm.then_inc(at_ready, 1)

                def values(i):
                    h, qt = divmod(i, 2)
                    r = 64 * (h % 2)
                    pe.wait_ge(aT_ready, 16 + i + 1)
                    c = h // 2
                    for t in range(4):
                        mm = pe.matmul(ps[r:r + 64, 4 + c // 2, (c % 2) * 256 + qt * P:(c % 2) * 256 + (qt + 1) * P],
                                       v2[:, t, (h // 4) * 64:(h // 4 + 1) * 64], pT2[:, i % 2, t * P:(t + 1) * P],
                                       start=t == 0, stop=t == 3)
                    mm.then_inc(o_ready, 1)

                for i in range(34):
                    if i < 32:
                        scores(i)
                    if 1 <= i < 33:
                        attend(i - 1)
                    if i >= 2:
                        values(i - 2)
                pe.wait_ge(yT_ready, 10 + 4)
                for half in range(2):
                    rows_product(G0["odd_out"] + half, lambda kk, t: yTo[:, kk, t * P:(t + 1) * P], 2,
                                 lambda t: ps[:, 2 * t + half, :])

            even()
            moe(0)
            odd()
            moe(1)

        @block.scalar
        def _(act):
            def load(dst, src, s):
                act.dma_start(dst, src).then_inc(s, 16)

            def consts(name):
                a, n = CA[name]
                return A["consts"][:, a:a + n]

            load(cond[:, :, :], A["cond_cols"], cond_landed)
            load(modrow, A["b_mod_2"].rearrange("l v -> (l v)").partition_broadcast(2), bmod_landed)
            load(K[:, :], consts("resident"), const_landed)
            load(w(R3, 512), consts("ndist"), const_landed)
            load(w(R3 + 512, 2048), consts("band"), const_landed)
            load(w(R3 + 2560, 1024), A["rows1"].partition_broadcast(P), const_landed)
            act.wait_ge(ones_ready, 1)
            for half in range(2):
                load(pool_bd[64 * half:64 * half + 64, :, :, 64 * half:64 * half + 64].rearrange("p l c n -> p (l c) n"),
                     A["pool_w"].rearrange("l (c h) i o -> h i (l c) o", h=2)[half], const_landed)
            load(cols1[:, :, :], A["cols1"], const_landed)
            load(router_w[:, :, :, :], A["router_w"], const_landed)
            load(router_b[:, :, :].rearrange("p l n -> p (l n)"), A["router_b"].partition_broadcast(P), const_landed)
            load(rows2[:, :], A["rows2"].partition_broadcast(P), const_landed)
            load(conv2_w[:, :, :], A["conv2_cols"], const_landed)
            load(gain[:, :], gain_src[0].partition_broadcast(P), gain_landed)

            act.wait_ge(cond_landed, 16)
            act.activation(cond[:, :, :], cond[:, :, :], ACT.Silu).then_inc(cond_ready, 1)
            act.wait_ge(mod_copied, 24)
            act.dma_start(mod_dram, modrow).then_inc(mod_stored, 16)

            def norm(n):
                act.wait_ge(ms_ready, n + 1)
                nt = {8: 4, 9: 4, 10: 4}.get(n, 2)
                act.activation(std[:, 0:nt], ss[:, 0:nt], ACT.Sqrt, bias=eps[:, 0:1]).then_inc(std_ready, 1)
                if n in (3, 7):
                    act.wait_ge(x_ready, 4 if n == 3 else 8)
                dst = hT1 if n < 8 else hT2
                for j in range(0, 2 * NORMS[n], 2):
                    act.wait_ge(tr_ready, BANK0[n] + j + 1)
                    act.copy(dst[:, j * PC:(j + 1) * PC], ps[:, j, :]).then_inc(hT_act, 1)
                if n + 1 < len(gain_src):
                    load(gain[:, :], gain_src[n + 1].partition_broadcast(P), gain_landed)

            def ffn(f):
                def chunk(c, j):
                    act.wait_ge(gu_ready, FF_CHUNKS * f + c + 1)
                    act.activation(sg1[:, j, :], ps[:, 4 + j, 0:256], ACT.Tanh, scale=0.5).then_inc(silu_ready, 1)

                with act.Fori(0, 5) as i:
                    for j in range(4):
                        chunk(4 * i + j, j)
                for j in range(2):
                    chunk(20 + j, j)

            def mix1(l):
                g = G0[f"in{l}"]
                act.wait_ge(panel_done, g + 1)
                act.activation(sig, ps[:, 1, :].rearrange("p (c n) -> p c n", c=2), ACT.Tanh,
                               scale=0.5).then_inc(sig_ready, 1)
                act.wait_ge(panel_done, g + 2)
                act.copy(w(R2, 512), ps[:, 2, :]).then_inc(up_ready, 1)
                act.wait_ge(panel_done, g + 3)
                act.activation(sqt, psf[:, 3 * PC:5 * PC], ACT.Square).then_inc(sq_ready, 1)
                act.wait_ge(qks_ready, 2 * l + 1)
                act.activation(std[:, 0:16], ss[:, 0:16], ACT.Sqrt, bias=eps[:, 0:1], scale=1 / HD).then_inc(qkstd_ready, 1)
                act.wait_ge(panel_done, g + 4)
                act.activation(sqt, psf[:, 5 * PC:7 * PC], ACT.Square).then_inc(sq_ready, 1)
                act.wait_ge(qks_ready, 2 * l + 2)
                act.activation(std[:, 0:16], ss[:, 0:16], ACT.Sqrt, bias=eps[:, 0:1], scale=1 / HD).then_inc(qkstd_ready, 1)
                act.wait_ge(dps_ready, l + 1)
                act.copy(w(R2 + 512, 512), ps[:, 2, :]).then_inc(dT_ready, 1)
                act.wait_ge(panel_done, g + 5)
                act.copy(v1[:, 0, :], ps[:, 7, :])
                act.copy(v1[:, 1, :], ps[:, 0, :]).then_inc(v_ready, 1)
                act.wait_ge(pp_ready, l + 1)
                for c in range(2):
                    act.activation(yT1[:, 2 + c, :], ps[:, 2, c * 256:(c + 1) * 256], ACT.Copy,
                                   scale=cols1[:, l, 2 * CONV_W + 6 + c:2 * CONV_W + 7 + c]).then_inc(yT_ready, 1)
                for i in range(2):
                    act.wait_ge(qkt_ready, 2 * l + i + 1)
                    for t in range(2):
                        cp = act.copy((qT, kT)[i][:, :, t * P:(t + 1) * P],
                                      ps[:, 3 + 2 * i + t, :].rearrange("p (h n) -> p h n", h=4))
                    cp.then_inc(qkT_ready, 1)
                act.wait_ge(var_ready, l + 1)
                act.activation(sig[:, 0, :], ps[:, 1, 256:512], ACT.Sqrt, bias=eps[:, 0:1]).then_inc(lnstd_ready, 1)
                act.wait_ge(ln_ready, l + 1)
                for c in range(2):
                    cc = 2 * CONV_W + 2
                    cp = act.activation(yT1[:, c, :], conv_acc[:, c, :], ACT.Silu,
                                        scale=cols1[:, l, cc + c:cc + c + 1],
                                        bias=cols1[:, l, cc + 2 + c:cc + 3 + c])
                cp.then_inc(yT_ready, 1)
                act.wait_ge(lam_ready, l + 1)
                act.activation(lam[:, 2:4], lam[:, 0:2], ACT.Exp).then_inc(lame_ready, 1)

                def exps(i):
                    act.wait_ge(s_ready, 8 * l + i + 1)
                    for c in range(2):
                        e = act.activation(p1[:, i % 2, c * 256:(c + 1) * 256], s1[:, i % 2, c * 256:(c + 1) * 256],
                                           ACT.Exp, bias=m1[:, i % 2, c:c + 1], accum_out=m1[:, i % 2, 2 + c:3 + c])
                    e.then_inc(p_ready, 1)

                def weights_T(i):
                    act.wait_ge(at_ready, 8 * l + i + 1)
                    act.copy(at1[:, i % 2, :], ps[:, 1, (i % 2) * 256:(i % 2) * 256 + 256]).then_inc(aT_ready, 1)

                def sub_norm(qt):
                    act.wait_ge(o_ready, 8 * l + 4 * qt + 4)
                    act.activation(osq, ps[:, (7, 0)[qt], :], ACT.Square).then_inc(osq_ready, 1)
                    act.wait_ge(oss_ready, 2 * l + qt + 1)
                    act.activation(std[:, 32:36], ss[:, 32:36], ACT.Sqrt, bias=eps[:, 0:1], scale=1 / P).then_inc(ostd_ready, 1)
                    act.wait_ge(ot_ready, 2 * l + qt + 1)
                    act.copy(yT1[:, 4:8, qt * P:(qt + 1) * P],
                             ps[:, 2, :].rearrange("p (h n) -> p h n", h=4)).then_inc(yT_ready, 1)

                for i in range(9):
                    if i < 8:
                        exps(i)
                    if i >= 1:
                        weights_T(i - 1)
                    if i == 5:
                        sub_norm(0)
                sub_norm(1)

            for l in range(DEPTH):
                norm(4 * l)
                ffn(2 * l)
                norm(4 * l + 1)
                mix1(l)
                norm(4 * l + 2)
                ffn(2 * l + 1)
                norm(4 * l + 3)

            def mod_rows(l, v, dst, streams):
                for s in streams:
                    at = (6 * l + v) * D
                    load(dst[:, s, :], mod_dram[s, at:at + D].partition_broadcast(P), modb_landed)

            def even():
                load(xres[:, 2:4, :], A["ctx_2"][0].rearrange("(t p) d -> p t d", p=P), x_landed)
                act.wait_ge(mod_stored, 16)
                mod_rows(0, 1, sc_rows, (0, 1))
                mod_rows(0, 0, sh_rows, (0, 1))
                mod_rows(0, 2, g_rows, (0, 1))
                norm(8)
                act.wait_ge(tr_ready, BANK0[9])
                load(w(R0 + 3072, 1024), consts("dft_l"), dftl_landed)
                g = G0["even"]
                act.wait_ge(panel_done, g + 1)
                for t in range(4):
                    act.copy(a_rows[:, t, :], ps[:, t, :]).then_inc(acopy, 1)
                act.wait_ge(panel_done, g + 3)
                for m in range(4):
                    act.copy(cT[:, m, :], ps[:, m, :]).then_inc(ccopy, 1)

                def seq_copy(i):
                    act.wait_ge(pt_ready, i + 1)
                    act.copy(pt[:, i % 2, :], ps[:, i % 2, :]).then_inc(ptc_ready, 1)

                def chan_copy(i):
                    s, grp = divmod(i, 4)
                    act.wait_ge(f_ready, i + 1)
                    act.copy(yT2[:, grp * 512 + s * 256:grp * 512 + s * 256 + 256], ps[:, 2 + i % 2, 0:256]).then_inc(fc_ready, 1)

                for i in range(9):
                    if i < 8:
                        seq_copy(i)
                    if i >= 1:
                        chan_copy(i - 1)

            def moe(m):
                nt, n, nb, b0, g0 = TILES[m], 9 + 2 * m, BLOCKS[m], BLOCK_BASE[m], G0[f"moe{m}"]
                streams = (0, 1)[:nt // 2]
                act.wait_ge(x_ready, 9 + 2 * m)
                mod_rows(m, 4, sc_rows, streams)
                mod_rows(m, 3, sh_rows, streams)
                mod_rows(m, 5, g_rows, streams)
                norm(n)
                for t in range(nt):
                    load(h_dram[t * P:(t + 1) * P, :], hrow[:, t, :], h_stored)
                act.wait_ge(gmax_ready, m + 1)
                act.activation(r_gexp[:, 0:nt, :], r_gcand[:, 0:nt, :], ACT.Exp).then_inc(gexp_ready, 1)
                act.wait_ge(top_ready, m + 1)
                act.activation(r_s[:, 5, 0:nt], r_s[:, 4, 0:nt], ACT.Exp).then_inc(texp_ready, 1)

                def out_rows(b, par, first=False):
                    act.wait_ge(panel_done, g0 + 3 * b + 3)
                    if not first:
                        act.wait_ge(y_stored[par], 8 * (b0 + b - par))
                    act.copy(ysb[:, par, 0:PC], ps[:, 6, :]).then_inc(y_act, 1)
                    act.wait_ge(y_act, b0 + b + 1)
                    act.wait_ge(y_dve, b0 + b + 1)
                    act.dma_start(y_dram.rearrange("(b p) d -> b p d", p=P)[bass.ds(b, 1)].rearrange("a p d -> p (a d)"),
                                  ysb[:, par, :]).then_inc(y_stored[par], 16)

                def expert(b, par, prev=True, first=False):
                    act.wait_ge(xgt_ready, b0 + b + 1)
                    act.copy(xgT[:, par, 0:PC], ps[:, 0, :]).then_inc(xgT_act, 1)
                    if prev:
                        out_rows(b - 1, 1 - par, first=first)
                    for j in range(4):
                        act.wait_ge(mgu_ready, 4 * (b0 + b) + j + 1)
                        act.activation(sgm[:, par, j, :], ps[:, 2 + j, 0:P],
                                       ACT.Tanh, scale=0.5).then_inc(msilu_ready, 1)

                expert(0, 0, prev=False)
                expert(1, 1, first=m == 0)
                expert(2, 0, first=m == 0)
                expert(3, 1)
                with act.Fori(2, nb // 2) as i:
                    expert(2 * i, 0)
                    expert(2 * i + 1, 1)
                out_rows(nb - 1, 1)

            def odd():
                act.wait_ge(x_ready, 10)
                mod_rows(1, 1, sc_rows, (0, 1))
                mod_rows(1, 0, sh_rows, (0, 1))
                mod_rows(1, 2, g_rows, (0,))
                norm(10)
                act.wait_ge(row_ready, TILE0[11])
                load(w(R3 + 3072, 512), consts("window"), dftl_landed)
                g = G0["odd"]
                act.wait_ge(panel_done, g + 2)
                act.activation(sq2, psf[:, 0:4 * PC], ACT.Square).then_inc(sq_ready, 1)
                act.wait_ge(qks_ready, 5)
                act.activation(std[:, 0:32], ss[:, 0:32], ACT.Sqrt, bias=eps[:, 0:1], scale=1 / HD).then_inc(qkstd_ready, 1)
                act.wait_ge(panel_done, g + 3)
                act.activation(sq2[:, 0:1024].rearrange("p (t n) -> p t n", t=4), ps[:, 4:8, 0:256],
                               ACT.Square).then_inc(sq_ready, 1)
                for t in range(4):
                    act.copy(v2[:, t, :], ps[:, 4 + t, 256:512]).then_inc(v2_ready, 1)
                act.wait_ge(qks_ready, 6)
                act.activation(std[:, 0:16], ss[:, 0:16], ACT.Sqrt, bias=eps[:, 0:1], scale=1 / HD).then_inc(qkstd_ready, 1)
                for b in range(4):
                    t, j = divmod(b, 2)
                    act.wait_ge(qkt_ready, 4 + b + 1)
                    act.copy(qT2[:, 4 * j:4 * j + 4, t * P:(t + 1) * P],
                             ps[:, b, :].rearrange("p (h n) -> p h n", h=4)).then_inc(qkT_ready, 1)
                for h in range(4):
                    act.wait_ge(qkt_ready, 8 + h + 1)
                    act.copy(kT2[:, h, :], ps[:, 4 + h, :]).then_inc(qkT_ready, 1)

                def exps(i):
                    h = i // 2
                    act.wait_ge(s_ready, 16 + i + 1)
                    act.activation(m1[:, i % 2, 2:3], rows2[:, 2 * HD + h:2 * HD + h + 1], ACT.Exp,
                                   bias=m1[:, i % 2, 1:2])
                    act.activation(p2[:, i % 2, :], s2[:, i % 2, :], ACT.Exp, bias=m1[:, i % 2, 1:2],
                                   accum_out=m1[:, i % 2, 3:4]).then_inc(p_ready, 1)

                def weights_T(i):
                    act.wait_ge(at_ready, 16 + i + 1)
                    act.copy(pT2[:, i % 2, :], ps[:, 2 + i % 2, :]).then_inc(aT_ready, 1)

                for i in range(33):
                    if i < 32:
                        exps(i)
                    if i >= 1:
                        weights_T(i - 1)
                act.wait_ge(o_ready, 16 + 32)
                for b in range(4):
                    act.copy(w(R2 + b * PC, PC), ps[:, 4 + b, :]).then_inc(yT_ready, 1)

            even()
            moe(0)
            odd()
            moe(1)
            for t in range(2):
                act.wait_ge(combined, 4 + t + 1)
                act.dma_start(out[0, t * P:(t + 1) * P, :], xres[:, t, :]).then_inc(out_stored, 16)
            act.wait_ge(out_stored, 32)

        @block.vector
        def _(dve):
            def spread(v, shape):
                return v.unsqueeze(len(shape) - 1).to_broadcast(shape)

            def newton(r, v, t):
                dve.tensor_tensor(t, r, r, ALU.mult)
                dve.drain()
                dve.tensor_tensor(t, t, v, ALU.mult)
                dve.drain()
                dve.tensor_scalar(t, t, -0.5, 1.5, ALU.mult, ALU.add)
                dve.drain()
                dve.tensor_tensor(r, r, t, ALU.mult)

            def silu_times(dst, tanh, g, u):
                dve.scalar_tensor_tensor(tanh, tanh, 1.0, g, ALU.add, ALU.mult)
                dve.drain()
                return dve.scalar_tensor_tensor(dst, tanh, 0.5, u, ALU.mult, ALU.mult)

            def rstd(a, b, scale, ready, count):
                dve.tensor_scalar(var[:, a:b], ss[:, a:b], scale, EPS, ALU.mult, ALU.add)
                dve.wait_ge(ready, count)
                dve.reciprocal(rs[:, a:b], std[:, a:b])
                dve.drain()
                newton(rs[:, a:b], var[:, a:b], rt[:, a:b])
                dve.drain()

            dve.memset(eps[:, :], EPS)
            dve.memset(ones_c[:, :], 1 / 256)
            dve.memset(w(R3 + 3584, 512), 0.0)
            dve.memset(ones[:, :], 1.0).then_inc(ones_ready, 1)

            def mod_panels(i, first):
                for j in range(6):
                    dve.wait_ge(panel_done, 6 * i + j + 1)
                    at = bass.ds(6 * PC * i + j * PC, PC)
                    dve.tensor_tensor(modrow[:, at], modrow[:, at], ps[0:2, j, :], ALU.add).then_inc(mod_copied, 1)

            dve.wait_ge(bmod_landed, 16)
            with dve.Fori(0, 4) as i:
                mod_panels(i, False)
            dve.wait_ge(mod_stored, 16)
            dve.wait_ge(const_landed, 16 * CONST_DMAS)
            dve.wait_ge(x_landed, 16)

            def norm(n, nt, modulated=False, rows_out=True):
                for t in range(nt):
                    dve.tensor_tensor_reduce(hrow[:, t, :], xres[:, t, :], xres[:, t, :], 1 / D, 0.0,
                                             ALU.mult, ALU.add, ss[:, t:t + 1])
                dve.drain().then_inc(ms_ready, 1)
                dve.wait_ge(gain_landed, 16 * (n + 1))
                if modulated:
                    dve.wait_ge(modb_landed, MODB[n - 8])
                    for s in range(nt // 2):
                        dve.scalar_tensor_tensor(sc_rows[:, s, :], sc_rows[:, s, :], 1.0, gain[:, :], ALU.add, ALU.mult)
                rstd(0, nt, 1.0, std_ready, n + 1)
                for t in range(nt):
                    dst = hrow[:, t, :] if rows_out else xres[:, t, :]
                    if modulated:
                        dve.scalar_tensor_tensor(dst, xres[:, t, :], rs[:, t:t + 1], sc_rows[:, t // 2, :], ALU.mult, ALU.mult)
                        dve.drain()
                        dve.tensor_tensor(dst, dst, sh_rows[:, t // 2, :], ALU.add).then_inc(row_ready, 1)
                    else:
                        h = dve.scalar_tensor_tensor(dst, xres[:, t, :], rs[:, t:t + 1], gain[:, :], ALU.mult, ALU.mult)
                        if rows_out:
                            h.then_inc(row_ready, 1)
                if not rows_out:
                    dve.drain().then_inc(x_ready, 1)

            def hT_odd(n):
                dst = hT1 if n < 8 else hT2
                for j in range(1, 2 * NORMS[n], 2):
                    dve.wait_ge(tr_ready, BANK0[n] + j + 1)
                    dve.tensor_copy(dst[:, j * PC:(j + 1) * PC], ps[:, j, :]).then_inc(hT_dve, 1)

            def residual(last_panel, scale):
                dve.wait_ge(panel_done, last_panel)
                for t in range(2):
                    dve.scalar_tensor_tensor(xres[:, t, :], psf[:, 2 * t * PC:(2 * t + 2) * PC], scale,
                                             xres[:, t, :], ALU.mult, ALU.add)
                dve.drain().then_inc(x_ready, 1)

            def ffn(f):
                def chunk(c, j):
                    dve.wait_ge(silu_ready, FF_CHUNKS * f + c + 1)
                    silu_times(aT1[:, j, :], sg1[:, j, :], ps[:, 4 + j, 0:256], ps[:, 4 + j, 256:512]).then_inc(act_ready, 1)

                with dve.Fori(0, 5) as i:
                    for j in range(4):
                        chunk(4 * i + j, j)
                for j in range(2):
                    chunk(20 + j, j)
                residual(G0[f"ffn{f}"] + 3 * FF_STEPS, 0.5)

            def head_norm(l, i, src, dst, nh, gain_row, scale, spread_gain, count):
                dve.wait_ge(sq_ready, count)
                dve.tensor_reduce(ss[:, 0:nh], sqt.rearrange("p (h n) -> p h n", n=HD), X, ALU.add).then_inc(qks_ready, 1)
                dve.drain()
                rstd(0, nh, 1 / HD, qkstd_ready, count)
                d3 = dst.rearrange("p (h n) -> p h n", n=HD)
                dve.tensor_tensor(d3, src.rearrange("p (h n) -> p h n", n=HD), spread(rs[:, 0:nh], [P, nh, HD]), ALU.mult)
                dve.drain()
                dve.scalar_tensor_tensor(d3, d3, scale, gain_row.unsqueeze(1).to_broadcast([P, nh, HD]),
                                         ALU.mult, ALU.mult).then_inc(qkn_ready, 1)

            def mix1(l):
                dve.memset(zpad[:, :, 0:PAD], 0.0)
                dve.memset(zpad[:, :, PAD + SEQ:], 0.0)
                dve.wait_ge(sig_ready, l + 1)
                dve.tensor_scalar(sig, sig, 0.5, 0.5, ALU.mult, ALU.add)
                dve.drain()
                dve.tensor_tensor(zpad[:, :, PAD:PAD + SEQ], ps[:, 0, :].rearrange("p (c n) -> p c n", c=2), sig,
                                  ALU.mult).then_inc(z_ready, 1)
                dve.drain()
                for j in range(CONV_W):
                    for c in range(2):
                        wj = cols1[:, l, c * CONV_W + j:c * CONV_W + j + 1]
                        if j == 0:
                            op = dve.tensor_scalar(conv_acc[:, c, :], zpad[:, c, 0:SEQ], wj,
                                                   cols1[:, l, 2 * CONV_W + c:2 * CONV_W + c + 1], ALU.mult, ALU.add)
                        else:
                            op = dve.scalar_tensor_tensor(conv_acc[:, c, :], zpad[:, c, j:j + SEQ], wj,
                                                          conv_acc[:, c, :], ALU.mult, ALU.add)
                    if j < CONV_W - 1:
                        dve.drain()
                dve.drain().then_inc(conv_ready, 1)
                r1 = rows1[:, l, :]
                head_norm(l, 0, psf[:, 3 * PC:5 * PC], qn, 16, r1[:, 0:HD], HD ** -0.5, False, 2 * l + 1)
                dve.drain()
                head_norm(l, 1, psf[:, 5 * PC:7 * PC], kn, 16, r1[:, HD:2 * HD], 1.0, False, 2 * l + 2)
                dve.tensor_tensor_reduce(s1[:, 0, 0:HD], r1[:, 128:192], r1[:, 192:256], 1.0, 0.0,
                                         ALU.mult, ALU.add, lam[:, 0:1])
                dve.tensor_tensor_reduce(s1[:, 0, HD:2 * HD], r1[:, 256:320], r1[:, 320:384], 1.0, 0.0,
                                         ALU.mult, ALU.add, lam[:, 1:2])
                dve.drain().then_inc(lam_ready, 1)
                dve.wait_ge(mean_ready, l + 1)
                dve.tensor_tensor(conv_acc, conv_acc, ps[:, 1, 0:256].unsqueeze(1).to_broadcast([P, 2, 256]), ALU.subtract)
                dve.drain()
                dve.tensor_tensor(sig, conv_acc, conv_acc, ALU.mult).then_inc(xsq_ready, 1)
                dve.wait_ge(lnstd_ready, l + 1)
                dve.tensor_scalar(up[:, 0, :], ps[:, 1, 256:512], EPS, None, ALU.add)
                dve.reciprocal(sig[:, 1, :], sig[:, 0, :])
                dve.drain()
                newton(sig[:, 1, :], up[:, 0, :], up[:, 1, :])
                dve.drain()
                dve.tensor_tensor(conv_acc, conv_acc, sig[:, 1, :].unsqueeze(1).to_broadcast([P, 2, 256]),
                                  ALU.mult).then_inc(ln_ready, 1)
                dve.wait_ge(lame_ready, l + 1)
                dve.tensor_tensor(lam[:, 4:5], lam[:, 3:4], lam[:, 2:3], ALU.subtract)
                dve.drain()
                dve.tensor_scalar(lam[:, 5:6], lam[:, 4:5], -lam_init[l], None, ALU.add)
                dve.drain()

                def bias_and_max(i):
                    qt, h = divmod(i, 4)
                    dve.wait_ge(sc_ready, 8 * l + i + 1)
                    dve.scalar_tensor_tensor(s1[:, i % 2, :].rearrange("p (c n) -> p c n", c=2),
                                             ndist[:, qt, :].unsqueeze(1).to_broadcast([P, 2, SEQ]), slopes[h],
                                             ps[:, 3 + 2 * (i % 2):5 + 2 * (i % 2), 0:256], ALU.mult, ALU.add)
                    dve.drain()
                    dve.tensor_reduce(m1[:, i % 2, 0:2], s1[:, i % 2, :].rearrange("p (c n) -> p c n", c=2), X,
                                      ALU.max, negate=True).then_inc(s_ready, 1)

                def weights(i):
                    b = i % 2
                    dve.wait_ge(p_ready, 8 * l + i + 1)
                    dve.reciprocal(m1[:, b, 4:6], m1[:, b, 2:4])
                    dve.drain()
                    dve.tensor_tensor(m1[:, b, 6:7], m1[:, b, 5:6], lam[:, 5:6], ALU.mult)
                    dve.tensor_scalar(a1[:, b, :], p1[:, b, 0:256], m1[:, b, 4:5], None, ALU.mult)
                    dve.drain()
                    dve.scalar_tensor_tensor(a1[:, b, :], p1[:, b, 256:512], m1[:, b, 6:7], a1[:, b, :],
                                             ALU.mult, ALU.add).then_inc(a_ready, 1)

                def sub_norm(qt):
                    dve.wait_ge(osq_ready, 2 * l + qt + 1)
                    dve.tensor_reduce(ss[:, 32:36], osq.rearrange("p (h n) -> p h n", h=4), X, ALU.add).then_inc(oss_ready, 1)
                    dve.drain()
                    rstd(32, 36, 1 / P, ostd_ready, 2 * l + qt + 1)
                    if qt == 1:
                        dve.wait_ge(ot_ready, 2 * l + 1)
                    o3 = on.rearrange("p (h n) -> p h n", h=4)
                    dve.tensor_tensor(o3, ps[:, (7, 0)[qt], :].rearrange("p (h n) -> p h n", h=4),
                                      spread(rs[:, 32:36], [P, 4, P]), ALU.mult)
                    dve.drain()
                    dve.scalar_tensor_tensor(o3, o3, 1.0 - lam_init[l],
                                             r1[:, 384:512].unsqueeze(1).to_broadcast([P, 4, P]),
                                             ALU.mult, ALU.mult).then_inc(on_ready, 1)

                for i in range(9):
                    if i < 8:
                        bias_and_max(i)
                    if i >= 1:
                        weights(i - 1)
                    if i == 5:
                        sub_norm(0)
                sub_norm(1)
                residual(G0[f"out{l}"] + 2, 1.0)

            for l in range(DEPTH):
                norm(4 * l, 2)
                hT_odd(4 * l)
                ffn(2 * l)
                norm(4 * l + 1, 2)
                hT_odd(4 * l + 1)
                mix1(l)
                norm(4 * l + 2, 2)
                hT_odd(4 * l + 2)
                ffn(2 * l + 1)
                norm(4 * l + 3, 2, rows_out=False)

            def gated_residual(last_panel, nt):
                dve.wait_ge(panel_done, last_panel)
                for t in range(nt):
                    dve.tensor_tensor(prod, psf[:, 2 * t * PC:(2 * t + 2) * PC], g_rows[:, t // 2, :], ALU.mult)
                    dve.drain()
                    dve.tensor_tensor(xres[:, t, :], xres[:, t, :], prod, ALU.add)
                    dve.drain()
                dve.drain().then_inc(x_ready, 1)

            def even():
                g = G0["even"]
                dve.wait_ge(x_landed, 32)
                norm(8, 4, modulated=True)
                hT_odd(8)
                dve.memset(upad[:, :, :, 0:1], 0.0)
                dve.memset(upad[:, :, :, SEQ + 1:], 0.0)
                dve.wait_ge(panel_done, g + 2)
                for m in range(4):
                    dve.tensor_copy(bT[:, m, :], ps[:, 4 + m, :]).then_inc(bcopy, 1)
                dve.wait_ge(ccopy, 4)
                dve.wait_ge(panel_done, g + 4)
                dve.drain()
                for j in range(4):
                    u = upad[:, j % 2, :, :]
                    y = yT2[:, (4 + j) * 512:(5 + j) * 512].rearrange("p (s n) -> p s n", s=2)
                    s3 = lambda v: v.rearrange("p (s n) -> p s n", s=2)
                    dve.tensor_tensor(u[:, :, 1:SEQ + 1], s3(cT[:, j, :]), s3(ps[:, 4 + j, :]), ALU.mult)
                    dve.drain()
                    dve.tensor_scalar(y, u[:, :, 0:SEQ], conv2_w[:, j, 0:1], None, ALU.mult)
                    for tap in (1, 2):
                        dve.drain()
                        dve.scalar_tensor_tensor(y, u[:, :, tap:tap + SEQ], conv2_w[:, j, tap:tap + 1], y, ALU.mult, ALU.add)
                    dve.drain()
                    dve.tensor_tensor(y, y, s3(bT[:, j, :]), ALU.mult).then_inc(conv2_ready, 1)
                gated_residual(G0["even_out"] + 2, 4)

            def first_max(v, nt, width, mx, eq, cand, oh):
                iw = iota[:, 0:width].unsqueeze(1).to_broadcast([P, nt, width])
                dve.tensor_reduce(mx, v, X, ALU.max)
                dve.drain()
                dve.tensor_tensor(eq, v, spread(mx, [P, nt, width]), ALU.is_equal)
                dve.drain()
                dve.scalar_tensor_tensor(cand, eq, -1000.0, iw, ALU.mult, ALU.add)
                dve.drain()
                dve.tensor_reduce(r_s[:, 15, 0:nt], cand, X, ALU.min)
                dve.drain()
                dve.tensor_tensor(oh, cand, spread(r_s[:, 15, 0:nt], [P, nt, width]), ALU.is_equal)
                dve.drain()

            def moe(m):
                nt, n, nb, b0, g0, nx = TILES[m], 9 + 2 * m, BLOCKS[m], BLOCK_BASE[m], G0[f"moe{m}"], EXTRA[m]
                norm(n, nt, modulated=True)
                hT_odd(n)
                S = lambda i: r_s[:, i, 0:nt]
                lg = r_logit[:, 0:nt, :]
                dve.wait_ge(logit_ready, m + 1)
                dve.tensor_tensor(lg, ps[:, 0, 0:nt * NLOG].rearrange("p (t n) -> p t n", t=nt),
                                  router_b[:, m, :].unsqueeze(1).to_broadcast([P, nt, NLOG]), ALU.add)
                dve.drain()
                goh = r_goh[:, 0:nt, :]
                first_max(lg[:, :, 0:GROUPS], nt, GROUPS, S(0), r_gneg[:, 0:nt, :], r_gcand[:, 0:nt, :], goh)
                dve.tensor_tensor(r_gcand[:, 0:nt, :], lg[:, :, 0:GROUPS], spread(S(0), [P, nt, GROUPS]),
                                  ALU.subtract).then_inc(gmax_ready, 1)
                dve.tensor_scalar(r_gneg[:, 0:nt, :], goh, BIG, -BIG, ALU.mult, ALU.add)
                dve.drain()
                em, em2 = r_em[:, 0:nt, :], r_em2[:, 0:nt, :]
                oh1, oh2, cand = r_oh1[:, 0:nt, :], r_oh2[:, 0:nt, :], r_cand[:, 0:nt, :]
                for t in range(nt):
                    dve.tensor_tensor(r_em[:, t, :].rearrange("p (a b) -> p a b", a=GROUPS),
                                      r_logit[:, t, GROUPS:].rearrange("p (a b) -> p a b", a=GROUPS),
                                      spread(r_gneg[:, t, :], [P, GROUPS, PER_GROUP]), ALU.add)
                dve.drain()
                first_max(em, nt, EXPERTS, S(1), em2, cand, oh1)
                dve.scalar_tensor_tensor(em2, oh1, -3 * BIG, em, ALU.mult, ALU.add)
                dve.drain()
                first_max(em2, nt, EXPERTS, S(2), r_tmp[:, 0:nt, :], cand, oh2)
                dve.tensor_tensor(S(4), S(2), S(1), ALU.subtract).then_inc(top_ready, 1)
                dve.tensor_tensor(r_mem[:, 0:nt, :], oh1, oh2, ALU.add).then_inc(member_ready, 1)
                dve.wait_ge(gexp_ready, m + 1)
                dve.tensor_reduce(S(6), r_gexp[:, 0:nt, :], X, ALU.add)
                dve.wait_ge(texp_ready, m + 1)
                dve.tensor_scalar(S(7), S(5), 1.0, None, ALU.add)
                dve.drain()
                dve.tensor_tensor(S(8), S(6), S(7), ALU.mult)
                dve.drain()
                dve.reciprocal(gates[:, 0, 0:nt], S(8))
                dve.drain()
                dve.tensor_tensor(gates[:, 1, 0:nt], gates[:, 0, 0:nt], S(5), ALU.mult)
                dve.wait_ge(pos_ready, m + 1)
                pos = r_tmp[:, 0:nt, :]
                dve.tensor_copy(pos, ps[:, 1, 0:nt * 32].rearrange("p (t n) -> p t n", t=nt))
                dve.tensor_copy(r_cnt, ps[:, 1, nt * 32:nt * 32 + 32])
                dve.drain()
                dve.tensor_scalar(r_nx, r_cnt, 128.0, None, ALU.is_gt)
                for thr in (256.0, 384.0):
                    dve.drain()
                    dve.scalar_tensor_tensor(r_nx, r_cnt, thr, r_nx, ALU.is_gt, ALU.add)
                dve.drain()
                dve.tensor_copy(r_t1, r_nx)
                dve.drain()
                src, dst = r_t1, r_xs
                for sh in (1, 2, 4, 8, 16):
                    dve.tensor_copy(dst[:, 0:sh], src[:, 0:sh])
                    dve.tensor_tensor(dst[:, sh:], src[:, sh:], src[:, 0:EXPERTS - sh], ALU.add)
                    dve.drain()
                    src, dst = dst, src
                incl = src
                excl = dst
                dve.tensor_tensor(excl, incl, r_nx, ALU.subtract)
                dve.drain()
                dve.tensor_tensor(r_shift, excl, iota[:, 0:32], ALU.subtract)
                dve.drain()
                dve.tensor_scalar(r_shift, r_shift, float(EXPERTS - 1), 128.0, ALU.add, ALU.mult)
                dve.drain()
                bc = lambda v: v.unsqueeze(1).to_broadcast([P, nt, EXPERTS])
                sl = r_slot[:, 0:nt, :]
                dve.scalar_tensor_tensor(sl, pos, 128.0, bc(r_shift), ALU.is_ge, ALU.mult)
                dve.drain()
                dve.tensor_tensor(sl, sl, pos, ALU.add)
                dve.drain()
                dve.scalar_tensor_tensor(sl, bc(iota[:, 0:32]), 128.0, sl, ALU.mult, ALU.add)
                dve.drain()
                for kk, oh in enumerate((oh1, oh2)):
                    dve.tensor_tensor(cand, oh, sl, ALU.mult)
                    dve.drain()
                    dve.tensor_reduce(r_sl[:, kk, 0:nt], cand, X, ALU.add)
                    dve.drain()
                for kk in range(2):
                    dve.tensor_copy(r_sli[:, kk, 0:nt], r_sl[:, kk, 0:nt])
                    dve.tensor_copy(slot_id[:, 0:nt, kk], r_sl[:, kk, 0:nt])
                dve.drain()
                for kk in range(2):
                    dve.tensor_scalar(r_blki[:, kk, 0:nt], r_sli[:, kk, 0:nt], 7, None, ALU.logical_shift_right)
                    dve.tensor_scalar(r_ini[:, kk, 0:nt], r_sli[:, kk, 0:nt], 127, None, ALU.bitwise_and)
                dve.drain()
                for kk in range(2):
                    dve.tensor_copy(r_blkf[:, kk, 0:nt], r_blki[:, kk, 0:nt])
                    dve.tensor_copy(r_inf[:, kk, 0:nt], r_ini[:, kk, 0:nt])
                dve.drain()
                for kk in range(2):
                    for t in range(nt):
                        i = kk * nt + t
                        dve.tensor_scalar(r_onehot[:, i, :], iota, r_inf[:, kk, t:t + 1], None, ALU.is_equal)
                        dve.tensor_scalar(r_blk[:, i, 0:nb], iota[:, 0:nb], r_blkf[:, kk, t:t + 1],
                                          k("tokid")[:, t:t + 1], ALU.is_equal, ALU.mult)
                dve.drain().then_inc(onehot_ready, 1)
                ix = spread(iota[:, 0:nx], [P, nx, EXPERTS])
                ex, ex2 = r_ex[:, 0:nx, :], r_ex2[:, 0:nx, :]
                bx = lambda v: v.unsqueeze(1).to_broadcast([P, nx, EXPERTS])
                dve.tensor_tensor(ex, ix, bx(excl), ALU.is_ge)
                dve.tensor_tensor(ex2, ix, bx(incl), ALU.is_lt)
                dve.drain()
                dve.tensor_tensor(ex, ex, ex2, ALU.mult)
                dve.drain()
                dve.tensor_tensor(ex, ex, bx(iota[:, 0:32]), ALU.mult)
                dve.drain()
                dve.tensor_reduce(r_exid[:, 0:nx], ex, X, ALU.add)
                dve.drain()
                dve.tensor_copy(extra_id[:, 0:nx], r_exid[:, 0:nx])
                dve.wait_ge(tps_ready, m + 1)
                dve.tensor_copy(table[:, 0:nb], ps[:, 2, 0:nb])
                dve.drain().then_inc(table_ready, 1)

                def out_rows(b, par, first=False):
                    dve.wait_ge(panel_done, g0 + 3 * b + 3)
                    if not first:
                        dve.wait_ge(y_stored[par], 8 * (b0 + b - par))
                    dve.tensor_copy(ysb[:, par, PC:2 * PC], ps[:, 7, :]).then_inc(y_dve, 1)

                def expert(b, par, prev=True, first=False):
                    dve.wait_ge(xgt_ready, b0 + b + 1)
                    dve.tensor_copy(xgT[:, par, PC:2 * PC], ps[:, 1, :]).then_inc(xgT_dve, 1)
                    if prev:
                        out_rows(b - 1, 1 - par, first=first)
                    for j in range(4):
                        dve.wait_ge(msilu_ready, 4 * (b0 + b) + j + 1)
                        silu_times(aTm[:, par, j, :], sgm[:, par, j, :], ps[:, 2 + j, 0:P],
                                   ps[:, 2 + j, P:2 * P]).then_inc(mact_ready, 1)

                expert(0, 0, prev=False)
                expert(1, 1, first=m == 0)
                expert(2, 0, first=m == 0)
                expert(3, 1)
                with dve.Fori(2, nb // 2) as i:
                    expert(2 * i, 0)
                    expert(2 * i + 1, 1)
                out_rows(nb - 1, 1)
                for t in range(nt):
                    y1, y2 = yg[:, t % 2, 0, :], yg[:, t % 2, 1, :]
                    dve.wait_ge(yg_landed[t % 2], 32 * (t // 2 + 1) + (64 if m else 0))
                    dve.tensor_scalar(y1, y1, gates[:, 0, t:t + 1], None, ALU.mult)
                    dve.drain()
                    dve.scalar_tensor_tensor(y1, y2, gates[:, 1, t:t + 1], y1, ALU.mult, ALU.add)
                    dve.drain()
                    dve.tensor_tensor(y1, y1, g_rows[:, t // 2, :], ALU.mult)
                    dve.drain()
                    dve.tensor_tensor(xres[:, t, :], xres[:, t, :], y1, ALU.add)
                    dve.drain().then_inc(combined, 1)
                dve.drain().then_inc(x_ready, 1)

            def rope(rows, nh, t):
                v = rows.rearrange("p (h x) -> p h x", h=nh)
                cos = k("cos")[:, t * 32:(t + 1) * 32].rearrange("p (a n) -> p a n", a=2)
                sin = k("sin")[:, t * 32:(t + 1) * 32].rearrange("p (a n) -> p a n", a=2)
                A4 = rope_a.rearrange("p (c a h n) -> p c a h n", c=2, a=2, h=16)
                B4 = rope_b.rearrange("p (c a h n) -> p c a h n", c=2, a=2, h=16)
                for a in range(2):
                    c = cos[:, a, :].unsqueeze(1).to_broadcast([P, nh, 16])
                    s = sin[:, a, :].unsqueeze(1).to_broadcast([P, nh, 16])
                    x1, x2 = v[:, :, 32 * a:32 * a + 16], v[:, :, 32 * a + 16:32 * a + 32]
                    dve.tensor_tensor(A4[:, 0, a, 0:nh, :], x1, c, ALU.mult)
                    dve.tensor_tensor(A4[:, 1, a, 0:nh, :], x2, s, ALU.mult)
                    dve.tensor_tensor(B4[:, 0, a, 0:nh, :], x1, s, ALU.mult)
                    dve.tensor_tensor(B4[:, 1, a, 0:nh, :], x2, c, ALU.mult)
                dve.drain()
                for a in range(2):
                    x1, x2 = v[:, :, 32 * a:32 * a + 16], v[:, :, 32 * a + 16:32 * a + 32]
                    dve.tensor_tensor(x1, A4[:, 0, a, 0:nh, :], A4[:, 1, a, 0:nh, :], ALU.subtract)
                    dve.tensor_tensor(x2, B4[:, 0, a, 0:nh, :], B4[:, 1, a, 0:nh, :], ALU.add)
                dve.drain()

            def odd():
                norm(10, 4, modulated=True)
                hT_odd(10)
                dve.wait_ge(sq_ready, 5)
                dve.tensor_reduce(ss[:, 0:32], sq2.rearrange("p (h n) -> p h n", n=HD), X, ALU.add).then_inc(qks_ready, 1)
                dve.drain()
                rstd(0, 32, 1 / HD, qkstd_ready, 5)
                q3 = w(R0, 2048).rearrange("p (h n) -> p h n", n=HD)
                dve.tensor_tensor(q3, psf[:, 0:2048].rearrange("p (h n) -> p h n", n=HD), spread(rs[:, 0:32], [P, 32, HD]), ALU.mult)
                dve.drain()
                dve.scalar_tensor_tensor(q3, q3, HD ** -0.5, rows2[:, 0:HD].unsqueeze(1).to_broadcast([P, 32, HD]),
                                         ALU.mult, ALU.mult)
                dve.drain()
                for t in range(2):
                    rope(q2[:, t, :], 16, t)
                dve.drain().then_inc(q2_ready, 1)
                dve.wait_ge(sq_ready, 6)
                dve.tensor_reduce(ss[:, 0:16], sq2[:, 0:1024].rearrange("p (h n) -> p h n", n=HD), X, ALU.add).then_inc(qks_ready, 1)
                dve.drain()
                rstd(0, 16, 1 / HD, qkstd_ready, 6)
                kf = sq2[:, 1024:2048]
                for t in range(4):
                    dve.tensor_tensor(kf[:, t * 256:(t + 1) * 256].rearrange("p (h n) -> p h n", n=HD),
                                      ps[:, 4 + t, 0:256].rearrange("p (h n) -> p h n", n=HD),
                                      spread(rs[:, 4 * t:4 * t + 4], [P, 4, HD]), ALU.mult)
                dve.drain()
                k3 = kf.rearrange("p (h n) -> p h n", n=HD)
                dve.tensor_tensor(k3, k3, rows2[:, HD:2 * HD].unsqueeze(1).to_broadcast([P, 16, HD]), ALU.mult)
                dve.drain()
                for t in range(2):
                    rope(kf[:, t * 256:(t + 1) * 256], 4, t)
                for t in range(4):
                    for c in range(2):
                        dve.tensor_copy(kdup[:, t, :, c, :], kf[:, t * 256:(t + 1) * 256].rearrange("p (h n) -> p h n", n=HD))
                dve.drain().then_inc(k2_ready, 1)
                dve.wait_ge(dftl_landed, 32)
                dve.wait_ge(qkT_ready, 12)

                def bias_and_max(i):
                    h, qt = divmod(i, 2)
                    b = i % 2
                    dve.wait_ge(sc_ready, 16 + i + 1)
                    dve.tensor_tensor(s2[:, b, 0:256], ps[:, b, 0:256], window[:, qt, :], ALU.add)
                    dve.tensor_copy(s2[:, b, 256:512], ps[:, b, 256:512])
                    dve.drain()
                    dve.tensor_reduce(m1[:, b, 0:1], s2[:, b, :], X, ALU.max)
                    dve.drain()
                    dve.tensor_scalar(m1[:, b, 1:2], m1[:, b, 0:1], rows2[:, 2 * HD + h:2 * HD + h + 1], -1.0,
                                      ALU.max, ALU.mult).then_inc(s_ready, 1)

                def weights(i):
                    b = i % 2
                    dve.wait_ge(p_ready, 16 + i + 1)
                    dve.tensor_tensor(m1[:, b, 4:5], m1[:, b, 2:3], m1[:, b, 3:4], ALU.add)
                    dve.drain()
                    dve.reciprocal(m1[:, b, 5:6], m1[:, b, 4:5])
                    dve.drain()
                    dve.tensor_scalar(p2[:, b, :], p2[:, b, :], m1[:, b, 5:6], None, ALU.mult).then_inc(a_ready, 1)

                for i in range(33):
                    if i < 32:
                        bias_and_max(i)
                    if i >= 1:
                        weights(i - 1)
                gated_residual(G0["odd_out"] + 2, 2)

            even()
            moe(0)
            odd()
            moe(1)

        @block.gpsimd
        def _(pool):
            def moe(m):
                nt, nb, b0 = TILES[m], BLOCKS[m], BLOCK_BASE[m]
                pool.wait_ge(table_ready, m + 1)
                pool.wait_ge(h_stored, 64 if m == 0 else 96)

                def gather(b, par, first=False):
                    if not first:
                        pool.wait_ge(xgt_ready, b0 + b - 1)
                    pool.tensor_copy(table_col[:, par:par + 1], table[:, bass.ds(b, 1)])
                    pool.drain()
                    pool.indirect_dma_start(out=xg[:, par, :], out_offset=None, in_=h_dram,
                                            in_offset=bass.IndirectOffsetOnAxis(ap=table_col[:, par:par + 1], axis=0)
                                            ).then_inc(xg_landed[par], 16)

                gather(0, 0, True)
                gather(1, 1, True)
                with pool.Fori(1, nb // 2) as i:
                    gather(2 * i, 0)
                    gather(2 * i + 1, 1)
                for par in range(2):
                    pool.wait_ge(y_stored[par], 8 * (b0 + nb))
                for t in range(nt):
                    if t >= 2:
                        pool.wait_ge(combined, t - 1)
                    for kk in range(2):
                        pool.indirect_dma_start(out=yg[:, t % 2, kk, :], out_offset=None, in_=y_dram,
                                                in_offset=bass.IndirectOffsetOnAxis(ap=slot_id[:, t, kk:kk + 1], axis=0)
                                                ).then_inc(yg_landed[t % 2], 16)

            moe(0)
            moe(1)


INPUTS = ["x", "ffn1_norm", "ffn1_w_gate", "ffn1_w_up", "ffn1_w_down", "mix_norm", "w_in", "pool_w", "w_out",
          "ffn2_norm", "ffn2_w_gate", "ffn2_w_up", "ffn2_w_down", "post_norm", "ctx_2", "w_mod_2", "b_mod_2",
          "norm_mix_g_2", "norm_ffn_g_2", "w_in_even_2", "w_out_even_2", "w_qkv_2", "w_o_2", "w1_2", "w3_2", "w2_2"]


def kernel(**inputs):
    import concourse.bacc as bacc
    from concourse.bass_utils import run_bass_kernel_spmd

    a = {n: np.ascontiguousarray(inputs[n]) for n in INPUTS}
    I = {n: np.asarray(v) for n, v in inputs.items()}

    def cols(v):
        return v.reshape(v.shape[0], -1, P).transpose(0, 2, 1)

    L = DEPTH
    taps = I["conv_dw"].reshape(L, CONV_W, 2, P).transpose(0, 3, 2, 1).reshape(L, P, 2 * CONV_W)
    a["cols1"] = np.ascontiguousarray(np.concatenate(
        [taps, cols(I["conv_dw_bias"]), cols(I["conv_ln_gain"]), cols(I["conv_ln_bias"]), cols(I["pool_scale"])],
        axis=2).transpose(1, 0, 2))
    a["rows1"] = np.ascontiguousarray(np.concatenate(
        [I["q_norm"], I["k_norm"], I["lambda_q1"], I["lambda_k1"], I["lambda_q2"], I["lambda_k2"],
         I["attn_subln"]], axis=1).reshape(-1))
    a["rows2"] = np.ascontiguousarray(np.concatenate(
        [I["q_norm_g_2"][0], I["k_norm_g_2"][0], I["sink_logit_2"][0]]))
    a["cond_cols"] = np.ascontiguousarray(
        np.stack([I["c_2"][0], I["c_ctx_2"]]).reshape(2, KD, P).transpose(2, 1, 0))
    a["router_w"] = np.ascontiguousarray(
        np.concatenate([I["w_router_g_2"], I["w_router_e_2"]], axis=2).reshape(L, KD, P, NLOG).transpose(2, 0, 1, 3))
    a["router_b"] = np.ascontiguousarray(
        np.concatenate([I["b_router_g_2"], I["b_router_e_2"]], axis=1).reshape(-1))
    a["conv2_cols"] = np.ascontiguousarray(I["conv_w_2"][0].reshape(3, 4, P).transpose(2, 1, 0))
    a["consts"] = const_table()[0]

    nc = bacc.Bacc("TRN2", target_bir_lowering=False, num_devices=1)
    arrays = {f"in_{n}": v for n, v in a.items()}
    aps = {n: nc.dram_tensor(f"in_{n}", v.shape, mybir.dt.from_np(v.dtype), kind="ExternalInput").ap()
           for n, v in a.items()}
    out = nc.dram_tensor("out", (1, SEQ, D), F32, kind="ExternalOutput").ap()
    build(nc, aps, out)
    r = run_bass_kernel_spmd(nc, [arrays], core_ids=[0])
    return r.results[0]["out"]
```

```python
from contextlib import ExitStack

import concourse.bass as bass
import numpy as np
from concourse import mybir

ALU = mybir.AluOpType
ACT = mybir.ActivationFunctionType
X = mybir.AxisListType.X
F32 = mybir.dt.float32
F32R = mybir.dt.float32r
U32 = mybir.dt.uint32
I32 = mybir.dt.int32

P = 128
D = 1024
KD = D // P
SEQ = 256
DEPTH = 2
RAW = 4
RAW_UP = 6
SPLIT = 3
PC = 256
BANK = 512
AT = 2048
T_COLS = AT + 512 + KD * PC
FF = 2816
FF_UNITS = FF // PC
EPS = 1e-6
HEADS = 4
HD = 64
CONV_W = 31
PAD = CONV_W // 2
EXPERTS = 32
GROUPS = 4
PER_GROUP = EXPERTS // GROUPS
NLOG = GROUPS + EXPERTS
POOL_WINDOWS = (2, 4, 8, 16)
TILES = (4, 2)
EXTRA = (8, 4)
BLOCKS = tuple(EXPERTS + e for e in EXTRA)
BLOCK_BASE = (0, BLOCKS[0])
HEADS2 = 16
BIG = 1e30


def panel_plan():
    base, g = {}, 0
    stages = [("mod", 48)]
    for l in range(DEPTH):
        stages += [(f"ffn{2 * l}", 3 * FF_UNITS), (f"in{l}", 9), (f"out{l}", 4), (f"ffn{2 * l + 1}", 3 * FF_UNITS)]
    stages += [("even", 8), ("even_out", 4), ("moe0", 6 * EXPERTS), ("extra0", 6 * EXTRA[0]),
               ("odd", 6), ("odd_out", 4), ("moe1", 6 * EXPERTS), ("extra1", 6 * EXTRA[1])]
    for name, n in stages:
        base[name] = g
        g += n
    return base


def const_table():
    cols, at = [], {}

    def put(name, a):
        a = np.asarray(a, np.float32).reshape(P, -1)
        at[name] = (sum(c.shape[1] for c in cols), a.shape[1])
        cols.append(a)

    i = np.arange(P)
    put("ident", np.eye(P))
    put("tri", i[:, None] < i[None, :])
    put("iota", np.broadcast_to(i, (P, P)))
    put("tokid", i[:, None] + P * np.arange(4)[None, :])
    w = 2 * np.pi * (np.outer(i, i) % P) / P
    put("dft_c", np.cos(w))
    put("dft_ns", -np.sin(w))
    t = np.arange(SEQ)
    freq = (np.float32(10000.0) ** (-np.arange(16, dtype=np.float32) / np.float32(16))).astype(np.float32)
    pos = np.stack([t // 64, t % 64], -1).astype(np.float32)
    ang = (pos[:, :, None] * freq).astype(np.float32).astype(np.float64)
    for name, f in (("cos", np.cos), ("sin", np.sin)):
        put(name, f(ang).reshape(2, P, 32).transpose(1, 0, 2))
    at["resident"] = (0, sum(c.shape[1] for c in cols))
    w = 2 * np.pi * (np.outer(t, t) % SEQ) / SEQ
    s = 1 / np.sqrt(SEQ * P)
    put("dft_l", np.concatenate([np.cos(w) * s, np.sin(w) * s], 1).reshape(2, P, 2 * SEQ).transpose(1, 0, 2))
    dist = np.abs(t[:, None] - t[None, :])
    put("window", np.where(dist <= 128, 0.0, -BIG).reshape(2, P, SEQ).transpose(1, 0, 2))
    put("ndist", (-dist).reshape(2, P, SEQ).transpose(1, 0, 2))
    band = np.zeros((4, SEQ, SEQ))
    for g, wd in enumerate(POOL_WINDOWS):
        lo, hi = np.clip(t - wd // 2, 0, SEQ), np.clip(t + wd // 2, 0, SEQ)
        inside = (t[:, None] >= lo[None, :]) & (t[:, None] < hi[None, :])
        band[g] = inside / (hi - lo)[None, :] - np.eye(SEQ)
    put("band", band.reshape(4, 2, P, SEQ).transpose(2, 1, 0, 3))
    return np.ascontiguousarray(np.concatenate(cols, 1)), at


def build(nc, A, out):
    G0 = panel_plan()
    _, CA = const_table()
    lam_init = [0.8 - 0.6 * float(np.exp(-0.3 * l)) for l in range(DEPTH)]
    slopes = [float(np.exp2(np.float32(-8.0 * (h + 1) / HEADS))) for h in range(HEADS)]

    mod_dram = nc.dram_tensor("mod_rows", (2, 2 * 6 * D), F32, kind="Internal").ap()
    h_dram = nc.dram_tensor("router_rows", (4 * P, D), F32, kind="Internal").ap()
    y_dram = nc.dram_tensor("expert_rows", (BLOCKS[0] * P, D), F32, kind="Internal").ap()

    R0, R1, R2, R3 = 0, 4096, 4096 + 3072, 4096 + 3072 + 3456

    with ExitStack() as ctx:
        def sb(name, shape, dt=F32):
            return ctx.enter_context(nc.sbuf_tensor(name, shape, dt))

        def sem(name):
            return ctx.enter_context(nc.semaphore(name))

        raw = sb("raw", [P, RAW, KD * PC])
        w_hi = sb("w_hi", [P, SPLIT, KD * PC], F32R)
        w_lo = sb("w_lo", [P, SPLIT, KD * PC], F32R)
        t_hi = sb("t_hi", [P, T_COLS], F32R)
        t_lo = sb("t_lo", [P, T_COLS], F32R)
        xres = sb("x_rows", [P, 4, D])
        W = sb("work", [P, R3 + 6144])
        K = sb("consts", [P, CA["resident"][1]])
        ones = sb("ones", [P, P])
        ones_c = sb("ones_over_256", [P, P])
        router_w = sb("router_w", [P, DEPTH, KD, NLOG])
        router_b = sb("router_b", [P, DEPTH, NLOG])
        rows2 = sb("rows2", [P, 2 * HD + HEADS2])
        conv2_w = sb("conv2_w", [P, 4, 3])
        cond = sb("cond", [P, KD, 2])
        extra_used = sb("extra_blocks", [1, 8], I32)
        eps = sb("eps", [P, 1])
        ss = sb("sum_squares", [P, 64])
        std = sb("std", [P, 64])
        rs = sb("rstd", [P, 64])
        var = sb("variance", [P, 64])
        rt = sb("rstd_error", [P, 64])
        slot_id = sb("slot_of_token", [P, 4, 2], U32)
        gates = sb("gates", [P, 2, 4])
        table = sb("token_of_slot", [P, BLOCKS[0]], U32)
        table_col = sb("token_of_slot_col", [P, 2], U32)
        extra_id = sb("extra_expert", [P, 8], I32)
        ps = ctx.enter_context(nc.psum_tensor("ps", [P, 8, BANK], F32))
        psf = ps[:, :, :].rearrange("p b c -> p (b c)")

        def k(name):
            a, n = CA[name]
            return K[:, a:a + n]

        def w(a, n):
            return W[:, a:a + n]

        ident, tri, iota = k("ident"), k("tri"), k("iota")
        hrow = w(R0, 4096).rearrange("p (t d) -> p t d", t=4)

        def gain(n):
            return w(R3 + 1024 if n < 7 else R1 + 1024 if n == 7 else R1 + 2048, D)

        sg1 = w(R1, 1024).rearrange("p (b n) -> p b n", b=4)
        zpad = w(R1, 2 * (SEQ + 2 * PAD)).rearrange("p (c n) -> p c n", c=2)
        conv_acc = w(R1 + 576, 512).rearrange("p (c n) -> p c n", c=2)
        sig = w(R1 + 1088, 512).rearrange("p (c n) -> p c n", c=2)
        ystage = w(R1 + 1600, 1024)
        up = w(R2, 512).rearrange("p (t n) -> p t n", t=2)
        dT = w(R2 + 512, 512).rearrange("p (c n) -> p c n", c=2)
        sqt = w(R2 + 1024, 1024)
        qn = w(R2 + 2048, 1024)
        kn = w(R3, 1024)
        qT = w(R0, 1024).rearrange("p (h n) -> p h n", h=4)
        kT = w(R0 + 1024, 1024).rearrange("p (h n) -> p h n", h=4)
        ndist = w(R3 + 2048, 512).rearrange("p (t n) -> p t n", t=2)
        band = xres[:, 2:4, :].rearrange("p a b -> p (a b)").rearrange("p (t g n) -> p t g n", t=2, g=4)
        rows1 = w(R3 + 2560, 1024).rearrange("p (l n) -> p l n", l=2)
        pool_bd = w(R3 + 3584, 512).rearrange("p (l c n) -> p l c n", l=2, c=2)
        v1 = w(R3 + 4096, 1024).rearrange("p (t n) -> p t n", t=2)
        s1 = w(R3 + 5120, 1024).rearrange("p (b n) -> p b n", b=2)
        p1 = w(R0 + 2048, 1024).rearrange("p (b n) -> p b n", b=2)
        a1 = w(R0 + 3072, 512).rearrange("p (b n) -> p b n", b=2)
        at1 = w(R0 + 3584, 512).rearrange("p (b n) -> p b n", b=2)
        osq = w(R2 + 1024, 512)
        on = w(R2 + 1536, 512)
        cols1 = sb("cols1", [P, DEPTH, 2 * CONV_W + 8])
        lam = sb("lam", [P, 8])
        m1 = sb("row_stats", [P, 2, 8])

        modrow = W[0:2, 0:12288]
        sc_rows = w(R3, 2048).rearrange("p (s d) -> p s d", s=2)
        sh_rows = w(R3 + 2048, 2048).rearrange("p (s d) -> p s d", s=2)
        g_rows = w(R3 + 4096, 2048).rearrange("p (s d) -> p s d", s=2)
        a_rows = w(R0, 2048).rearrange("p (t n) -> p t n", t=4)
        pt = w(R0 + 2048, 1024).rearrange("p (b n) -> p b n", b=2)
        dft_l = w(R0 + 3072, 1024).rearrange("p (t n) -> p t n", t=2)
        bT = w(R3, 2048).rearrange("p (j n) -> p j n", j=4)
        cT = w(R3 + 2048, 2048).rearrange("p (j n) -> p j n", j=4)
        upad = w(R1, 1032).rearrange("p (b s n) -> p b s n", b=2, s=2)
        conv2_y = w(R1 + 1040, 1024).rearrange("p (b n) -> p b n", b=2)
        prod = w(R2, 1024)
        q2 = w(R0, 2048).rearrange("p (t n) -> p t n", t=2)
        kdup = w(R0 + 2048, 2048).rearrange("p (t h c n) -> p t h c n", t=4, h=4, c=2)
        qT2 = xres[:, 2:4, :].rearrange("p a b -> p (a b)").rearrange("p (k n) -> p k n", k=8)
        kT2 = w(R3, 2048).rearrange("p (h n) -> p h n", h=4)
        v2 = w(R3 + 2048, 1024).rearrange("p (t n) -> p t n", t=4)
        window = w(R3 + 3072, 512).rearrange("p (t n) -> p t n", t=2)
        rope_a = w(R3, 1024)
        rope_b = w(R3 + 1024, 1024)
        sq2 = w(R2, 2048)
        s2 = w(R1, 1024).rearrange("p (b n) -> p b n", b=2)
        p2 = w(R1 + 1024, 1024).rearrange("p (b n) -> p b n", b=2)
        pT2 = w(R1 + 2048, 1024).rearrange("p (b n) -> p b n", b=2)

        xg = w(R0, 2048).rearrange("p (b n) -> p b n", b=2)
        ysb = w(R1, 2048).rearrange("p (b n) -> p b n", b=2)
        sgm = w(R1 + 2048, 512).rearrange("p (b n) -> p b n", b=2)
        am = w(R1 + 2560, 512).rearrange("p (b n) -> p b n", b=2)
        yg = [w(a, 2048).rearrange("p (c n) -> p c n", c=2) for a in (R0, R0 + 2048, R1, R2)]

        def r(at, *shape):
            v = w(R2 + at, int(np.prod(shape)))
            return v if len(shape) == 1 else v.rearrange(
                {2: "p (a b) -> p a b", 3: "p (a b c) -> p a b c"}[len(shape)],
                **dict(zip("abc", shape)))

        r_logit = r(0, 4, NLOG)
        r_gexp = r(144, 4, GROUPS)
        r_goh = r(160, 4, GROUPS)
        r_gcand = r(176, 4, GROUPS)
        r_gneg = r(192, 4, GROUPS)
        r_em = r(256, 4, EXPERTS)
        r_em2 = r(384, 4, EXPERTS)
        r_cand = r(512, 4, EXPERTS)
        r_oh1 = r(640, 4, EXPERTS)
        r_oh2 = r(768, 4, EXPERTS)
        r_mem = r(896, 4, EXPERTS)
        r_slot = r(1024, 4, EXPERTS)
        r_tmp = r(1152, 4, EXPERTS)
        r_cnt = r(1280, EXPERTS)
        r_nx = r(1312, EXPERTS)
        r_t1 = r(1344, EXPERTS)
        r_xs = r(1376, EXPERTS)
        r_shift = r(1408, EXPERTS)
        r_ex = r(1440, 8, EXPERTS)
        r_ex2 = r(1696, 8, EXPERTS)
        r_exid = r(1952, 8)
        r_s = r(1960, 16, 4)
        r_sl = r(2032, 2, 4)
        r_sli = r(2040, 2, 4).bitcast(I32)
        r_blki = r(2048, 2, 4).bitcast(I32)
        r_ini = r(2056, 2, 4).bitcast(I32)
        r_blkf = r(2064, 2, 4)
        r_inf = r(2072, 2, 4)
        r_blk = r(2080, 8, 40)
        r_onehot = r(2400, 8, P)

        landed = [sem(f"raw_landed_{i}") for i in range(RAW)]
        expert_landed = [sem(f"expert_raw_landed_{i}") for i in range(RAW_UP)]
        w_hi_ready = sem("w_hi_ready")
        w_ready = sem("w_ready")
        panel_done = sem("panel_done")
        x_landed = sem("x_landed")
        const_landed = sem("const_landed")
        cond_landed = sem("cond_landed")
        bmod_landed = sem("bmod_landed")
        ones_ready = sem("ones_ready")
        cond_ready = sem("cond_ready")
        mod_copied = sem("mod_copied")
        mod_stored = sem("mod_stored")
        gain_landed = sem("gain_landed")
        modb_landed = sem("mod_rows_landed")
        gate_landed = sem("gate_rows_landed")
        ms_ready = sem("mean_square_ready")
        std_ready = sem("std_ready")
        row_ready = sem("row_ready")
        tr_ready = sem("transposed_ready")
        hT_hi = sem("hT_hi_ready")
        hT_lo = sem("hT_ready")
        silu_ready = sem("silu_ready")
        act_ready = sem("activated_ready")
        x_ready = sem("residual_ready")
        sig_ready = sem("sigmoid_ready")
        z_ready = sem("glu_ready")
        conv_ready = sem("conv_ready")
        up_ready = sem("pool_rows_ready")
        dps_ready = sem("pool_diff_ready")
        dT_ready = sem("pool_diff_copied")
        pp_ready = sem("pool_product_ready")
        mean_ready = sem("mean_ready")
        xsq_ready = sem("centred_square_ready")
        var_ready = sem("variance_ready")
        lnstd_ready = sem("ln_std_ready")
        ln_ready = sem("ln_ready")
        pooled_ready = sem("pooled_ready")
        ys_hi = sem("conv_pool_T_hi")
        ys_lo = sem("conv_pool_T_ready")
        ao_hi = sem("attended_T_hi")
        ao_lo = sem("attended_T_ready")
        sq_ready = sem("squares_ready")
        qks_ready = sem("qk_sums_ready")
        qkstd_ready = sem("qk_std_ready")
        qkn_ready = sem("qk_normed_ready")
        qkt_ready = sem("qk_transposed_ready")
        qkT_ready = sem("qkT_ready")
        v_ready = sem("v_ready")
        sc_ready = sem("scores_ready")
        s_ready = sem("scores_biased_ready")
        p_ready = sem("exp_ready")
        a_ready = sem("weights_ready")
        at_ready = sem("weights_transposed_ready")
        aT_ready = sem("weightsT_ready")
        o_ready = sem("attended_ready")
        osq_ready = sem("attended_square_ready")
        oss_ready = sem("attended_sums_ready")
        ostd_ready = sem("attended_std_ready")
        on_ready = sem("attended_normed_ready")
        ot_ready = sem("attended_transposed_ready")
        lam_ready = sem("lambda_dots_ready")
        lame_ready = sem("lambda_exp_ready")
        acopy = sem("fourier_rows_ready")
        bcopy = sem("b_gate_ready")
        ccopy = sem("c_gate_ready")
        dftl_landed = sem("dft_l_landed")
        pt_ready = sem("dft_seq_ready")
        ptc_ready = sem("dft_seq_copied")
        f_ready = sem("dft_chan_ready")
        fc_hi = sem("dft_chan_hi")
        fc_lo = sem("dft_chan_split")
        conv2_ready = sem("short_conv_ready")
        q2_ready = sem("q2_ready")
        k2_ready = sem("k2_ready")
        v2_ready = sem("v2_ready")
        h_stored = sem("router_rows_stored")
        logit_ready = sem("logits_ready")
        gmax_ready = sem("group_max_ready")
        gexp_ready = sem("group_exp_ready")
        top_ready = sem("top_two_ready")
        texp_ready = sem("top_exp_ready")
        member_ready = sem("membership_ready")
        pos_ready = sem("positions_ready")
        onehot_ready = sem("slot_onehots_ready")
        tps_ready = sem("table_product_ready")
        table_ready = sem("table_ready")
        xg_landed = [[sem(f"gathered_{m}_{i}") for i in range(2)] for m in range(DEPTH)]
        xgt_ready = sem("gathered_transposed")
        xgT_hi = sem("gatheredT_hi")
        xgT_lo = sem("gatheredT_ready")
        mtanh_ready = sem("expert_tanh_ready")
        mat_ready = sem("expert_activated_transposed")
        maT_hi = sem("expert_activatedT_hi")
        maT_lo = sem("expert_activatedT_ready")
        mact_ready = sem("expert_activated_ready")
        y_act = sem("expert_out_by_act")
        y_dve = sem("expert_out_by_dve")
        y_stored = [sem(f"expert_out_stored_{i}") for i in range(2)]
        yg_landed = [sem(f"expert_rows_landed_{i}") for i in range(4)]
        y1_ready = sem("first_expert_weighted")
        extra_filled = sem("extra_rows_filled")
        combined = sem("tile_combined")
        out_stored = sem("out_stored")

        NORMS = [2, 2, 2, 0, 2, 2, 2, 0, 4, 4, 4, 2]
        TILE0 = [sum(NORMS[:n]) for n in range(13)]
        BANK0 = [2 * t for t in TILE0]
        gain_src = []
        for l in range(DEPTH):
            gain_src += [A["ffn1_norm"][l], A["mix_norm"][l], A["ffn2_norm"][l], A["post_norm"][l]]
        for l in range(DEPTH):
            gain_src += [A["norm_mix_g_2"][l], A["norm_ffn_g_2"][l]]
        MODB = [16 * c for c in (5, 10, 15, 18)]
        GATE = [16 * c for c in (2, 4, 5, 6)]

        def expert_layer(p):
            for m, end in ((0, G0["odd"]), (1, 1 << 30)):
                if G0[f"moe{m}"] <= p < end:
                    return m

        def slot(p):
            m = expert_layer(p)
            if m is not None:
                p0 = G0[f"moe{m}"]
                x = (p - p0) % (SPLIT + 1)
                if x == SPLIT:
                    return T(AT + 512, KD * PC)
                p = p0 + x
            return w_hi[:, p % SPLIT, :], w_lo[:, p % SPLIT, :]

        def raw_slot(p):
            m = expert_layer(p)
            if m is None:
                skipped = (6 * EXPERTS + 6 * EXTRA[0]) // RAW if p >= G0["odd"] else 0
                return raw[:, p % RAW, :], landed[p % RAW], 16 * (p // RAW + 1 - skipped)
            y = p - G0[f"moe{m}"]
            x = y % RAW_UP
            at = raw[:, (p - y + x) % RAW, :] if x < RAW else w(R3 + (x - RAW) * KD * PC, KD * PC)
            return at, expert_landed[x], 16 * (BLOCK_BASE[m] + y // RAW_UP + 1)

        def hi3(pair):
            return [v.rearrange("p (k n) -> p k n", k=KD) for v in pair]

        def hi3_down(pair):
            return [v.rearrange("p (k n) -> p k n", k=2) for v in pair]

        def T(a, n):
            return t_hi[:, a:a + n], t_lo[:, a:a + n]

        CONST_DMAS = 11

        block = ctx.enter_context(nc.Block())

        @block.sync
        def _(sp):
            def load(p, j, src, down=False):
                m = expert_layer(j)
                if m is None or j < G0[f"moe{m}"] + RAW:
                    if j >= RAW:
                        sp.wait_ge(w_ready, p - RAW + 1)
                elif j < G0[f"moe{m}"] + RAW_UP:
                    sp.wait_ge(row_ready, TILE0[10 + 2 * m])
                else:
                    sp.wait_ge(w_ready, p - RAW_UP + 1)
                dst, landed_in, _ = raw_slot(j)
                sp.dma_start(dst.rearrange("p (k n) -> p k n", k=2 if down else KD), src).then_inc(landed_in, 16)

            def cols(wt, c0):
                return wt.rearrange("(k p) n -> p k n", p=P)[:, :, bass.ds(c0, PC)]

            def rows(wt, k0):
                return wt.rearrange("(k p) n -> p k n", p=P)[:, bass.ds(k0, 2), :]

            sp.dma_start(xres[:, 0:2, :], A["x"][0].rearrange("(t p) d -> p t d", p=P)).then_inc(x_landed, 16)
            wmod = [A["w_mod_2"][l] for l in range(DEPTH)]

            for l in range(DEPTH):
                if l == 0:
                    for j in range(12):
                        load(j, j, cols(wmod[0], PC * j))
                with sp.Fori(1 - l, 2) as i:
                    for j in range(12):
                        load(24 * l + 12 * i + j, 12 + j, cols(wmod[l], 12 * PC * i + PC * j))

            def ffn(f, wg, wu, wd):
                p0 = G0[f"ffn{f}"]

                def unit(u, j):
                    load(p0 + 3 * u - 1, p0 + j, cols(wg, u * PC))
                    load(p0 + 3 * u, p0 + j + 1, cols(wu, u * PC))
                    load(p0 + 3 * u + 1, p0 + j + 2, rows(wd, u * 2 - 2), True)

                load(p0, p0, cols(wg, 0))
                load(p0 + 1, p0 + 1, cols(wu, 0))
                with sp.Fori(0, 2) as i:
                    for v in range(4):
                        unit(4 * i + 1 + v, 3 * v + 2)
                unit(9, 26)
                unit(10, 29)
                load(p0 + 32, p0 + 32, rows(wd, 20), True)

            def panels(name, wt, starts):
                for j, c0 in enumerate(starts):
                    p = G0[name] + j
                    load(p, p, cols(wt, c0))

            for l in range(DEPTH):
                ffn(2 * l, A["ffn1_w_gate"][l], A["ffn1_w_up"][l], A["ffn1_w_down"][l])
                panels(f"in{l}", A["w_in"][l], range(0, 9 * PC, PC))
                panels(f"out{l}", A["w_out"][l], range(0, 4 * PC, PC))
                ffn(2 * l + 1, A["ffn2_w_gate"][l], A["ffn2_w_up"][l], A["ffn2_w_down"][l])

            def moe(m):
                p0 = G0[f"moe{m}"]
                w1, w3, w2 = (A[n][m].rearrange("e a b -> (e a) b") for n in ("w1_2", "w3_2", "w2_2"))

                def up(wt, e, half):
                    return wt.rearrange("(k p) n -> p k n", p=P)[:, bass.ds(e * KD, KD), half * PC:(half + 1) * PC]

                def dn(e, half):
                    return rows(w2, e * 4 + 2 * half)

                def unit(e, half, p, j, e_prev):
                    load(p, j, up(w1, e, half))
                    load(p + 1, j + 1, up(w3, e, half))
                    load(p + 2, j + 2, dn(e_prev, 1 - half), True)

                load(p0, p0, up(w1, 0, 0))
                load(p0 + 1, p0 + 1, up(w3, 0, 0))

                def two_experts(i, j, units=(1, 2, 3, 4)):
                    for v in units:
                        unit(2 * i + v // 2, v % 2, p0 + 12 * i + 3 * v - 1, j + 3 * v - 1, 2 * i + (v - 1) // 2)

                two_experts(0, p0)
                with sp.Fori(1, EXPERTS // 2 - 1) as i:
                    two_experts(i, p0 + 12)
                two_experts(EXPERTS // 2 - 1, p0 + 6 * EXPERTS - 12, (1, 2, 3))
                load(p0 + 6 * EXPERTS - 1, p0 + 6 * EXPERTS - 1, dn(EXPERTS - 1, 1), True)

                q0 = G0[f"extra{m}"]
                sp.wait_ge(table_ready, m + 1)
                used = sp.value_load(extra_used[0:1, 0:1], min_val=0, max_val=EXTRA[m])
                with sp.Fori(0, EXTRA[m] // 2) as i:
                    for v in range(2):
                        q = q0 + 12 * i + 6 * v
                        js = [q0 + 6 * v + x for x in range(6)]
                        with sp.If(used > 2 * i + v):
                            e = sp.value_load(extra_id[0:1, bass.ds(2 * i + v, 1)], min_val=0, max_val=EXPERTS - 1)
                            load(q, js[0], up(w1, e, 0))
                            load(q + 1, js[1], up(w3, e, 0))
                            load(q + 2, js[2], up(w1, e, 1))
                            load(q + 3, js[3], up(w3, e, 1))
                            load(q + 4, js[4], dn(e, 0), True)
                            load(q + 5, js[5], dn(e, 1), True)
                        with sp.Else():
                            for x in range(6):
                                _, landed_in, count = raw_slot(js[x])
                                sp.wait_ge(landed_in, count - 16 + 32 * i)
                                sp.sem_inc(landed_in, 16)

            panels("even", A["w_in_even_2"][0], range(0, 8 * PC, PC))
            panels("even_out", A["w_out_even_2"][0], range(0, 4 * PC, PC))
            moe(0)
            panels("odd", A["w_qkv_2"][0], range(0, 6 * PC, PC))
            panels("odd_out", A["w_o_2"][0], range(0, 4 * PC, PC))
            moe(1)

        @block.tensor
        def _(pe):
            def product(dst, a, b, start, stop):
                pe.matmul(dst, a[0], b[0], start=start, stop=False)
                pe.matmul(dst, a[0], b[1], start=False, stop=False)
                return pe.matmul(dst, a[1], b[0], start=False, stop=stop)

            def at(pair, *idx):
                return [v[idx] for v in pair]

            def norm_T(n):
                nt = NORMS[n]
                pe.wait_ge(row_ready, TILE0[n + 1])
                for j in range(2 * nt):
                    for q in range(4):
                        kk, t = (2 * j + q // 2, q % 2) if nt == 2 else (j, q)
                        mm = pe.transpose(ps[:, j, q * P:(q + 1) * P], hrow[:, t, kk * P:(kk + 1) * P], ident)
                    mm.then_inc(tr_ready, 1)

            def rows_product(p, lhs, nt, out_at):
                pe.wait_ge(w_ready, p + 1)
                wt = hi3(slot(p))
                for t in range(nt):
                    for kk in range(KD):
                        mm = product(out_at(t), lhs(kk, t), at(wt, slice(None), kk, slice(None)), kk == 0, kk == KD - 1)
                mm.then_inc(panel_done, 1)

            def mod_panels(i, first):
                for j in range(12):
                    pe.wait_ge(w_ready, 12 * i + j + 1)
                    if not first or j >= 6:
                        pe.wait_ge(mod_copied, 12 * i + j - 5)
                    for kk in range(KD):
                        mm = product(ps[:, j % 6, 0:PC], T(kk * P, P), at(hi3(slot(j)), slice(None), kk, slice(None)),
                                     kk == 0, kk == KD - 1)
                    mm.then_inc(panel_done, 1)

            pe.wait_ge(cond_ready, 2)
            mod_panels(0, True)
            with pe.Fori(1, 4) as i:
                mod_panels(i, False)
            pe.wait_ge(mod_copied, 48)
            pe.wait_ge(const_landed, 16 * CONST_DMAS)
            pe.wait_ge(ones_ready, 1)

            def ffn(f, n):
                p0 = G0[f"ffn{f}"]
                pe.wait_ge(hT_lo, BANK0[n + 1])

                def gate_up(u, j, par):
                    for half in range(2):
                        p = p0 + (3 * u - 1 if j else 0) + half
                        pe.wait_ge(w_ready, p + 1)
                        wt = hi3(slot(p0 + j + half))
                        for c in range(2):
                            for kk in range(KD):
                                mm = product(ps[:, 4 + 2 * par + c, half * PC:(half + 1) * PC],
                                             at(wt, slice(None), kk, slice(c * P, (c + 1) * P)),
                                             T(kk * 256, 256), kk == 0, kk == KD - 1)
                        mm.then_inc(panel_done, 1)

                def ffn_down(u, p, j, par, start=False, stop=False):
                    pe.wait_ge(w_ready, p + 1)
                    pe.wait_ge(act_ready, FF_UNITS * f + u + 1)
                    wt = hi3_down(slot(p0 + j))
                    for c in range(2):
                        for t in range(2):
                            for half in range(2):
                                mm = product(ps[:, 2 * t + half, :], T(AT + (2 * par + c) * 256 + t * P, P),
                                             at(wt, slice(None), c, slice(half * BANK, (half + 1) * BANK)),
                                             start and c == 0, stop and c == 1)
                    mm.then_inc(panel_done, 1)

                gate_up(0, 0, 0)
                gate_up(1, 2, 1)
                ffn_down(0, p0 + 4, 4, 0, start=True)
                with pe.Fori(0, 4) as i:
                    for v in range(2):
                        u = 2 * i + 2 + v
                        gate_up(u, 5 + 3 * v, v)
                        ffn_down(u - 1, p0 + 3 * u + 1, 7 + 3 * v, 1 - v)
                gate_up(10, 29, 0)
                ffn_down(9, p0 + 31, 31, 1)
                ffn_down(10, p0 + 32, 32, 0, stop=True)

            def mix1(l):
                n = 4 * l + 1
                p = G0[f"in{l}"]
                hT = lambda kk, t: T(kk * 256 + t * P, P)
                pe.wait_ge(hT_lo, BANK0[n + 1])
                for b in range(2):
                    pe.wait_ge(w_ready, p + b + 1)
                    for c in range(2):
                        for kk in range(KD):
                            mm = product(ps[:, b, c * 256:(c + 1) * 256],
                                         at(hi3(slot(p + b)), slice(None), kk, slice(c * P, (c + 1) * P)),
                                         T(kk * 256, 256), kk == 0, kk == KD - 1)
                    mm.then_inc(panel_done, 1)
                rows_product(p + 2, hT, 2, lambda t: ps[:, 2, t * 256:(t + 1) * 256])
                for half in range(2):
                    rows_product(p + 3 + half, hT, 2, lambda t: ps[:, 3 + t, half * 256:half * 256 + 256])
                for half in range(2):
                    rows_product(p + 5 + half, hT, 2, lambda t: ps[:, 5 + t, half * 256:half * 256 + 256])
                pe.wait_ge(up_ready, l + 1)
                for grp in range(4):
                    r = 64 * (grp % 2)
                    for t in range(2):
                        mm = pe.matmul(ps[r:r + 64, 2, (grp // 2) * 256:(grp // 2) * 256 + 256],
                                       up[:, t, grp * 64:(grp + 1) * 64], band[:, t, grp, :],
                                       start=t == 0, stop=t == 1)
                mm.then_inc(dps_ready, 1)
                pe.wait_ge(z_ready, l + 1)
                for half in range(2):
                    rows_product(p + 7 + half, hT, 2, lambda t: ps[:, (7, 0)[t], half * 256:half * 256 + 256])
                pe.wait_ge(dT_ready, l + 1)
                for c in range(2):
                    mm = pe.matmul(ps[:, 2, c * 256:(c + 1) * 256], pool_bd[:, l, c, :], dT[:, c, :],
                                   start=True, stop=True)
                mm.then_inc(pp_ready, 1)
                for i, src in enumerate((qn, kn)):
                    pe.wait_ge(qkn_ready, 2 * l + i + 1)
                    for t in range(2):
                        for h in range(4):
                            mm = pe.transpose(ps[:, 3 + 2 * i + t, h * P:(h + 1) * P],
                                              src[:, t * 512 + h * P:t * 512 + (h + 1) * P], ident)
                    mm.then_inc(qkt_ready, 1)
                pe.wait_ge(qkT_ready, 2 * l + 2)
                pe.wait_ge(v_ready, l + 1)

                def mean():
                    pe.wait_ge(pooled_ready, l + 1)
                    pe.wait_ge(conv_ready, l + 1)
                    for c in range(2):
                        mm = pe.matmul(ps[:, 2, 0:256], ones_c[:, :], conv_acc[:, c, :], start=c == 0, stop=c == 1)
                    mm.then_inc(mean_ready, 1)

                def variance():
                    pe.wait_ge(xsq_ready, l + 1)
                    for c in range(2):
                        mm = pe.matmul(ps[:, 2, 256:512], ones_c[:, :], sig[:, c, :], start=c == 0, stop=c == 1)
                    mm.then_inc(var_ready, 1)

                def scores(i):
                    qt, h = divmod(i, 4)
                    if i >= 2:
                        pe.wait_ge(s_ready, 8 * l + i - 1)
                    for c in range(2):
                        mm = pe.matmul(ps[:, 3 + 2 * (i % 2) + c, 0:256],
                                       qT[64 * c:64 * c + 64, h, qt * P:(qt + 1) * P],
                                       kT[64 * c:64 * c + 64, h, :], start=True, stop=True)
                    mm.then_inc(sc_ready, 1)

                def attend(i):
                    qt, h = divmod(i, 4)
                    pe.wait_ge(a_ready, 8 * l + i + 1)
                    for t in range(2):
                        mm = pe.transpose(ps[:, 1, (i % 2) * 256 + t * P:(i % 2) * 256 + (t + 1) * P],
                                          a1[:, i % 2, t * P:(t + 1) * P], ident)
                    mm.then_inc(at_ready, 1)
                    pe.wait_ge(aT_ready, 8 * l + i + 1)
                    for t in range(2):
                        mm = pe.matmul(ps[:, (7, 0)[qt], h * P:(h + 1) * P], at1[:, i % 2, t * P:(t + 1) * P],
                                       v1[:, t, h * P:(h + 1) * P], start=t == 0, stop=t == 1)
                    mm.then_inc(o_ready, 1)

                def attended_T(qt):
                    if qt == 0:
                        pe.wait_ge(ln_ready, l + 1)
                    else:
                        pe.wait_ge(ao_lo, 2 * l + 1)
                    pe.wait_ge(on_ready, 2 * l + qt + 1)
                    for h in range(4):
                        mm = pe.transpose(ps[:, 2, h * P:(h + 1) * P], on[:, h * P:(h + 1) * P], ident)
                    mm.then_inc(ot_ready, 1)

                scores(0)
                for i in range(9):
                    if i + 1 < 8:
                        scores(i + 1)
                    if i >= 1:
                        attend(i - 1)
                    if i == 5:
                        mean()
                    if i == 6:
                        variance()
                    if i == 7:
                        attended_T(0)
                attended_T(1)
                pe.wait_ge(ys_lo, l + 1)
                pe.wait_ge(ao_lo, 2 * l + 2)
                for q in range(4):
                    rows_product(G0[f"out{l}"] + q, lambda kk, t: T(2048 + kk * 256 + t * P, P), 2,
                                 lambda t: ps[:, 2 * t + q // 2, (q % 2) * 256:(q % 2) * 256 + 256])

            for l in range(DEPTH):
                norm_T(4 * l)
                ffn(2 * l, 4 * l)
                norm_T(4 * l + 1)
                mix1(l)
                norm_T(4 * l + 2)
                ffn(2 * l + 1, 4 * l + 2)

            hT4 = lambda kk, t: T(kk * 512 + t * P, P)
            hT2t = lambda kk, t: T(kk * 256 + t * P, P)

            def even():
                p = G0["even"]
                norm_T(8)
                pe.wait_ge(hT_lo, BANK0[9])
                for half in range(2):
                    rows_product(p + half, hT4, 4, lambda t: ps[:, t, half * 256:half * 256 + 256])

                def chans(pp, b0):
                    pe.wait_ge(w_ready, pp + 1)
                    for c in range(2):
                        for kk in range(KD):
                            mm = product(ps[:, b0 + c, :], at(hi3(slot(pp)), slice(None), kk, slice(c * P, (c + 1) * P)),
                                         T(kk * 512, 512), kk == 0, kk == KD - 1)
                    mm.then_inc(panel_done, 1)

                chans(p + 2, 4)
                chans(p + 3, 6)
                pe.wait_ge(acopy, 4)
                chans(p + 4, 0)
                chans(p + 5, 2)
                pe.wait_ge(bcopy, 4)
                chans(p + 6, 4)
                chans(p + 7, 6)
                pe.wait_ge(ccopy, 4)
                pe.wait_ge(dftl_landed, 16)

                def along_seq(i):
                    s, grp = divmod(i, 4)
                    if i >= 2:
                        pe.wait_ge(ptc_ready, i - 1)
                    for t in range(2):
                        mm = pe.matmul(ps[:, i % 2, :], a_rows[:, 2 * s + t, grp * P:(grp + 1) * P], dft_l[:, t, :],
                                       start=t == 0, stop=t == 1)
                    mm.then_inc(pt_ready, 1)

                def along_chan(i):
                    pe.wait_ge(ptc_ready, i + 1)
                    if i >= 2:
                        pe.wait_ge(fc_lo, i - 1)
                    pe.matmul(ps[:, 2 + i % 2, 0:256], k("dft_c"), pt[:, i % 2, 0:256], start=True, stop=False)
                    pe.matmul(ps[:, 2 + i % 2, 0:256], k("dft_ns"), pt[:, i % 2, 256:512],
                              start=False, stop=True).then_inc(f_ready, 1)

                for i in range(9):
                    if i < 8:
                        along_seq(i)
                    if i >= 1:
                        along_chan(i - 1)
                pe.wait_ge(fc_lo, 8)
                pe.wait_ge(conv2_ready, 4)
                for q in range(4):
                    rows_product(G0["even_out"] + q, lambda kk, t: T(kk * 512 + t * P, P),
                                 4, lambda t: ps[:, 2 * t + q // 2, (q % 2) * 256:(q % 2) * 256 + 256])

            def moe(m):
                nt, n = TILES[m], 9 + 2 * m
                nb, b0, p0, q0 = BLOCKS[m], BLOCK_BASE[m], G0[f"moe{m}"], G0[f"extra{m}"]
                norm_T(n)
                pe.wait_ge(hT_lo, BANK0[n + 1])
                lhs = hT4 if nt == 4 else hT2t
                for t in range(nt):
                    for part in range(2):
                        for kk in range(KD):
                            mm = pe.matmul(ps[:, 0, t * NLOG:(t + 1) * NLOG], lhs(kk, t)[part].bitcast(F32),
                                           router_w[:, m, kk, :], start=kk == 0 and part == 0,
                                           stop=kk == KD - 1 and part == 1)
                mm.then_inc(logit_ready, 1)
                pe.wait_ge(member_ready, m + 1)
                for t in range(nt + 1):
                    for u in range(min(t + 1, nt)):
                        mm = pe.matmul(ps[:, 1, t * 32:(t + 1) * 32], tri if u == t else ones[:, :], r_mem[:, u, :],
                                       start=u == 0, stop=u == min(t, nt - 1))
                mm.then_inc(pos_ready, 1)
                pe.wait_ge(onehot_ready, m + 1)
                for i in range(2 * nt):
                    mm = pe.matmul(ps[:, 2, 0:nb], r_onehot[:, i, :], r_blk[:, i, 0:nb], start=i == 0, stop=i == 2 * nt - 1)
                mm.then_inc(tps_ready, 1)
                pe.wait_ge(table_ready, m + 1)

                def turn(b, par):
                    pe.wait_ge(xg_landed[m][par], 8 * (b - par) + 16)
                    for kk in range(KD):
                        mm = pe.transpose(psf[:, kk * P:(kk + 1) * P], xg[:, par, kk * P:(kk + 1) * P], ident)
                    mm.then_inc(xgt_ready, 1)

                def wide(p, j, par, half, which):
                    pe.wait_ge(w_ready, p + 1)
                    wt = hi3(slot(j))
                    for kk in range(KD):
                        mm = product(ps[:, 2 + half, which * PC:(which + 1) * PC], T(par * 1024 + kk * P, P),
                                     at(wt, slice(None), kk, slice(None)), kk == 0, kk == KD - 1)
                    mm.then_inc(panel_done, 1)

                def turn_act(b, half):
                    pe.wait_ge(mact_ready, 2 * (b0 + b) + half + 1)
                    for c in range(2):
                        mm = pe.transpose(ps[:, 4 + half, c * P:(c + 1) * P], am[:, half, c * P:(c + 1) * P], ident)
                    mm.then_inc(mat_ready, 1)

                def moe_down(p, j, b, half, first=False):
                    pe.wait_ge(w_ready, p + 1)
                    pe.wait_ge(maT_lo, 2 * (b0 + b) + half + 1)
                    if half == 0 and not first:
                        pe.wait_ge(y_act, b0 + b)
                        pe.wait_ge(y_dve, b0 + b)
                    wt = hi3_down(slot(j))
                    for c in range(2):
                        for h in range(2):
                            mm = product(ps[:, 6 + h, :], T(AT + half * 256 + c * P, P),
                                         at(wt, slice(None), c, slice(h * BANK, (h + 1) * BANK)),
                                         half == 0 and c == 0, half == 1 and c == 1)
                    mm.then_inc(panel_done, 1)

                def block_of(b, par, p, j, first=False, last=False):
                    pe.wait_ge(xgT_lo, 2 * (b0 + b) + 2)
                    if first:
                        wide(p0, p0, 0, 0, 0)
                        wide(p0 + 1, p0 + 1, 0, 0, 1)
                    else:
                        wide(p - 1, j - 1, par, 0, 0)
                        turn_act(b - 1, 1)
                        wide(p, j, par, 0, 1)
                        moe_down(p + 1, j + 1, b - 1, 1)
                    wide(p + 2, j + 2, par, 1, 0)
                    turn_act(b, 0)
                    if not last:
                        turn(b + 1, 1 - par)
                    wide(p + 3, j + 3, par, 1, 1)
                    moe_down(p + 4, j + 4, b, 0, first=first and b0 == 0)

                turn(0, 0)
                block_of(0, 0, p0, p0, first=True)
                block_of(1, 1, p0 + 6, p0 + 6)
                with pe.Fori(1, EXPERTS // 2 - 1) as i:
                    for v in range(2):
                        block_of(2 * i + v, v, p0 + 12 * i + 6 * v, p0 + 12 + 6 * v)
                for b in (EXPERTS - 2, EXPERTS - 1):
                    block_of(b, b % 2, p0 + 6 * b, p0 + 6 * b, last=b == EXPERTS - 1)
                turn_act(EXPERTS - 1, 1)
                moe_down(p0 + 6 * EXPERTS - 1, p0 + 6 * EXPERTS - 1, EXPERTS - 1, 1)

                used = pe.value_load(extra_used[0:1, 0:1], min_val=0, max_val=EXTRA[m])
                with pe.Fori(0, EXTRA[m] // 2) as i:
                    for v in range(2):
                        b, q, j = EXPERTS + 2 * i + v, q0 + 12 * i + 6 * v, q0 + 6 * v
                        with pe.If(used > 2 * i + v):
                            turn(b, v)
                            pe.wait_ge(xgT_lo, 2 * (b0 + b) + 2)
                            wide(q, j, v, 0, 0)
                            wide(q + 1, j + 1, v, 0, 1)
                            wide(q + 2, j + 2, v, 1, 0)
                            turn_act(b, 0)
                            wide(q + 3, j + 3, v, 1, 1)
                            moe_down(q + 4, j + 4, b, 0)
                            turn_act(b, 1)
                            moe_down(q + 5, j + 5, b, 1)
                        with pe.Else():
                            pe.drain()
                            pe.sem_inc(panel_done, 6)
                            pe.sem_inc(xgt_ready, 1)
                            pe.sem_inc(mat_ready, 2)

            def odd():
                p = G0["odd"]
                norm_T(10)
                pe.wait_ge(hT_lo, BANK0[11])
                for q in range(4):
                    rows_product(p + q, hT4, 2, lambda t: ps[:, 2 * t + q // 2, (q % 2) * 256:(q % 2) * 256 + 256])
                for q in range(2):
                    rows_product(p + 4 + q, hT4, 4, lambda t: ps[:, 4 + t, q * 256:q * 256 + 256])
                pe.wait_ge(q2_ready, 1)
                for b in range(4):
                    t, j = divmod(b, 2)
                    for c in range(4):
                        mm = pe.transpose(ps[:, b, c * P:(c + 1) * P],
                                          q2[:, t, (4 * j + c) * P:(4 * j + c + 1) * P], ident)
                    mm.then_inc(qkt_ready, 1)
                pe.wait_ge(k2_ready, 1)
                pe.wait_ge(v2_ready, 4)
                for h in range(4):
                    for t in range(4):
                        mm = pe.transpose(ps[:, 4 + h, t * P:(t + 1) * P],
                                          kdup[:, t, h, :, :].rearrange("p c n -> p (c n)"), ident)
                    mm.then_inc(qkt_ready, 1)
                pe.wait_ge(qkT_ready, 4 + 8)

                def scores(i):
                    h, qt = divmod(i, 2)
                    r = 64 * (h % 2)
                    if i >= 2:
                        pe.wait_ge(s_ready, 16 + i - 1)
                    pe.matmul(ps[:, i % 2, :], qT2[r:r + 64, h // 2, qt * P:(qt + 1) * P],
                              kT2[r:r + 64, h // 4, :], start=True, stop=True).then_inc(sc_ready, 1)

                def attend(i):
                    pe.wait_ge(a_ready, 16 + i + 1)
                    for t in range(4):
                        mm = pe.transpose(ps[:, 2 + i % 2, t * P:(t + 1) * P], p2[:, i % 2, t * P:(t + 1) * P], ident)
                    mm.then_inc(at_ready, 1)

                def values(i):
                    h, qt = divmod(i, 2)
                    r = 64 * (h % 2)
                    pe.wait_ge(aT_ready, 16 + i + 1)
                    c = h // 2
                    for t in range(4):
                        mm = pe.matmul(ps[r:r + 64, 4 + c // 2, (c % 2) * 256 + qt * P:(c % 2) * 256 + (qt + 1) * P],
                                       v2[:, t, (h // 4) * 64:(h // 4 + 1) * 64], pT2[:, i % 2, t * P:(t + 1) * P],
                                       start=t == 0, stop=t == 3)
                    mm.then_inc(o_ready, 1)

                scores(0)
                for i in range(34):
                    if i + 1 < 32:
                        scores(i + 1)
                    if 1 <= i < 33:
                        attend(i - 1)
                    if i >= 2:
                        values(i - 2)
                pe.wait_ge(ao_lo, 4 + 4)
                for q in range(4):
                    rows_product(G0["odd_out"] + q, lambda kk, t: T(kk * 256 + t * P, P), 2,
                                 lambda t: ps[:, 2 * t + q // 2, (q % 2) * 256:(q % 2) * 256 + 256])

            even()
            moe(0)
            odd()
            moe(1)

        @block.scalar
        def _(act):
            def load(dst, src, s):
                act.dma_start(dst, src).then_inc(s, 16)

            def consts(name):
                a, n = CA[name]
                return A["consts"][:, a:a + n]

            def split(p, j=None, i12=0):
                j = p if j is None else j
                m = expert_layer(j)
                src, landed_in, count = raw_slot(j)
                act.wait_ge(landed_in, count + (16 * 12 // (RAW if m is None else RAW_UP)) * i12)
                if m is not None and j >= G0[f"moe{m}"] + SPLIT:
                    act.wait_ge(panel_done, p - SPLIT)
                elif not isinstance(p, int) or p >= SPLIT:
                    act.wait_ge(panel_done, p - SPLIT + 1)
                act.copy(slot(j)[0], src).then_inc(w_hi_ready, 1)

            load(cond[:, :, :], A["cond_cols"], cond_landed)
            load(modrow, A["b_mod_2"].rearrange("l v -> (l v)").partition_broadcast(2), bmod_landed)
            load(K[:, :], consts("resident"), const_landed)
            load(w(R3 + 2048, 512), consts("ndist"), const_landed)
            load(xres[:, 2:4, :].rearrange("p a b -> p (a b)"), consts("band"), const_landed)
            load(w(R3 + 2560, 1024), A["rows1"].partition_broadcast(P), const_landed)
            act.wait_ge(ones_ready, 1)
            for half in range(2):
                load(pool_bd[64 * half:64 * half + 64, :, :, 64 * half:64 * half + 64].rearrange("p l c n -> p (l c) n"),
                     A["pool_w"].rearrange("l (c h) i o -> h i (l c) o", h=2)[half], const_landed)
            load(cols1[:, :, :], A["cols1"], const_landed)
            load(router_w[:, :, :, :], A["router_w"], const_landed)
            load(router_b[:, :, :].rearrange("p l n -> p (l n)"), A["router_b"].partition_broadcast(P), const_landed)
            load(rows2[:, :], A["rows2"].partition_broadcast(P), const_landed)
            load(conv2_w[:, :, :], A["conv2_cols"], const_landed)

            act.wait_ge(cond_landed, 16)
            act.activation(cond[:, :, :], cond[:, :, :], ACT.Silu)
            act.drain()
            act.copy(t_hi[:, 0:1024].rearrange("p (k n) -> p k n", k=KD)[:, :, 0:2], cond[:, :, :]).then_inc(cond_ready, 1)
            for j in range(12):
                split(j)
            with act.Fori(1, 4) as i:
                for j in range(12):
                    split(12 * i + j, j, i)
            split(48)
            split(49)
            act.wait_ge(mod_copied, 48)
            act.dma_start(mod_dram, modrow).then_inc(mod_stored, 16)
            act.wait_ge(mod_stored, 16)
            load(gain(0), gain_src[0].partition_broadcast(P), gain_landed)
            act.dma_start(y_dram[EXPERTS * P:, :], A["w_out"][0][0:EXTRA[0] * P, :]).then_inc(extra_filled, 16)

            def norm(n, mid=None):
                nt = {8: 4, 9: 4, 10: 4}.get(n, 2)
                act.activation(std[:, 63:64], eps[:, 0:1], ACT.Sqrt)
                if n in (0, 8):
                    act.wait_ge(x_landed, 16 if n == 0 else 32)
                if n:
                    act.wait_ge(x_ready, n)
                for t in range(nt // 2, nt):
                    act.activation(hrow[:, t, :], xres[:, t, :], ACT.Square, scale=D ** -0.5, accum_out=ss[:, t:t + 1])
                act.drain()
                act.wait_ge(ms_ready, n + 1)
                act.activation(std[:, 0:nt], ss[:, 0:nt], ACT.Sqrt, bias=eps[:, 0:1]).then_inc(std_ready, 1)
                if n in (3, 7):
                    act.wait_ge(x_ready, 4 if n == 3 else 8)
                if mid is not None:
                    split(mid)
                for j in range(2 * NORMS[n]):
                    act.wait_ge(tr_ready, BANK0[n] + j + 1)
                    act.copy(t_hi[:, j * BANK:(j + 1) * BANK], ps[:, j, :]).then_inc(hT_hi, 1)
                if n < 7:
                    load(gain(n + 1), gain_src[n + 1].partition_broadcast(P), gain_landed)

            def ffn(f):
                p0 = G0[f"ffn{f}"]

                def unit(u, par, i=0, v=0):
                    split(p0 + 3 * u + 2, p0 + 3 * v + 2, i)
                    act.wait_ge(panel_done, p0 + 3 * u + 1 if v else p0 + 2)
                    act.activation(sg1[:, 2 * par:2 * par + 2, :], ps[:, 4 + 2 * par:6 + 2 * par, 0:256], ACT.Tanh,
                                   scale=0.5).then_inc(silu_ready, 1)
                    if v < 10:
                        split(p0 + 3 * u + 3, p0 + 3 * v + 3, i)
                        split(p0 + 3 * u + 4, p0 + 3 * v + 4, i)

                unit(0, 0)
                with act.Fori(0, 2) as i:
                    for v in range(1, 5):
                        unit(4 * i + v, v % 2, i, v)
                unit(9, 1, v=9)
                unit(10, 0, v=10)
                split(p0 + 33)
                split(p0 + 34)

            def mix1(l):
                p = G0[f"in{l}"]
                split(p + 3)
                act.wait_ge(panel_done, p + 2)
                act.activation(sig, ps[:, 1, :].rearrange("p (c n) -> p c n", c=2), ACT.Tanh,
                               scale=0.5).then_inc(sig_ready, 1)
                split(p + 4)
                act.wait_ge(panel_done, p + 3)
                act.copy(w(R2, 512), ps[:, 2, :]).then_inc(up_ready, 1)
                split(p + 5)
                split(p + 6)
                act.wait_ge(panel_done, p + 5)
                act.activation(sqt, psf[:, 3 * BANK:5 * BANK], ACT.Square).then_inc(sq_ready, 1)
                split(p + 7)
                act.wait_ge(qks_ready, 2 * l + 1)
                act.activation(std[:, 0:16], ss[:, 0:16], ACT.Sqrt, bias=eps[:, 0:1], scale=1 / HD).then_inc(qkstd_ready, 1)
                split(p + 8)
                act.wait_ge(panel_done, p + 7)
                act.activation(sqt, psf[:, 5 * BANK:7 * BANK], ACT.Square).then_inc(sq_ready, 1)
                act.wait_ge(dps_ready, l + 1)
                act.copy(w(R2 + 512, 512), ps[:, 2, :]).then_inc(dT_ready, 1)
                split(p + 9)
                act.wait_ge(qks_ready, 2 * l + 2)
                act.activation(std[:, 0:16], ss[:, 0:16], ACT.Sqrt, bias=eps[:, 0:1], scale=1 / HD).then_inc(qkstd_ready, 1)
                split(p + 10)
                act.wait_ge(panel_done, p + 9)
                act.copy(v1[:, 0, :], ps[:, 7, :])
                act.copy(v1[:, 1, :], ps[:, 0, :]).then_inc(v_ready, 1)
                split(p + 11)
                act.wait_ge(pp_ready, l + 1)
                for c in range(2):
                    cp = act.activation(ystage[:, (2 + c) * 256:(3 + c) * 256], ps[:, 2, c * 256:(c + 1) * 256], ACT.Copy,
                                        scale=cols1[:, l, 2 * CONV_W + 6 + c:2 * CONV_W + 7 + c])
                cp.then_inc(pooled_ready, 1)
                for i in range(2):
                    act.wait_ge(qkt_ready, 2 * l + i + 1)
                    for t in range(2):
                        cp = act.copy((qT, kT)[i][:, :, t * P:(t + 1) * P],
                                      ps[:, 3 + 2 * i + t, :].rearrange("p (h n) -> p h n", h=4))
                    cp.then_inc(qkT_ready, 1)
                act.wait_ge(lam_ready, l + 1)
                act.activation(lam[:, 2:4], lam[:, 0:2], ACT.Exp).then_inc(lame_ready, 1)

                def exps(i):
                    act.wait_ge(s_ready, 8 * l + i + 1)
                    for c in range(2):
                        e = act.activation(p1[:, i % 2, c * 256:(c + 1) * 256], s1[:, i % 2, c * 256:(c + 1) * 256],
                                           ACT.Exp, bias=m1[:, i % 2, c:c + 1], accum_out=m1[:, i % 2, 2 + c:3 + c])
                    e.then_inc(p_ready, 1)

                def weights_T(i):
                    act.wait_ge(at_ready, 8 * l + i + 1)
                    act.copy(at1[:, i % 2, :], ps[:, 1, (i % 2) * 256:(i % 2) * 256 + 256]).then_inc(aT_ready, 1)

                def sub_norm(qt):
                    act.wait_ge(o_ready, 8 * l + 4 * qt + 4)
                    act.activation(osq, ps[:, (7, 0)[qt], :], ACT.Square).then_inc(osq_ready, 1)
                    act.wait_ge(oss_ready, 2 * l + qt + 1)
                    act.activation(std[:, 32:36], ss[:, 32:36], ACT.Sqrt, bias=eps[:, 0:1], scale=1 / P).then_inc(ostd_ready, 1)
                    act.wait_ge(ot_ready, 2 * l + qt + 1)
                    act.copy(t_hi[:, 2048 + 1024:4096].rearrange("p (h n) -> p h n", h=4)[:, :, qt * P:(qt + 1) * P],
                             ps[:, 2, :].rearrange("p (h n) -> p h n", h=4)).then_inc(ao_hi, 1)

                for i in range(9):
                    if i < 8:
                        exps(i)
                    if i >= 1:
                        weights_T(i - 1)
                    if i == 6:
                        act.wait_ge(var_ready, l + 1)
                        act.activation(sig[:, 0, :], ps[:, 2, 256:512], ACT.Sqrt, bias=eps[:, 0:1]).then_inc(lnstd_ready, 1)
                    if i == 7:
                        sub_norm(0)
                    if i == 8:
                        act.wait_ge(ln_ready, l + 1)
                        for c in range(2):
                            cc = 2 * CONV_W + 2
                            act.activation(ystage[:, c * 256:(c + 1) * 256], conv_acc[:, c, :], ACT.Silu,
                                           scale=cols1[:, l, cc + c:cc + c + 1],
                                           bias=cols1[:, l, cc + 2 + c:cc + 3 + c])
                        act.drain()
                        act.copy(t_hi[:, 2048:3072], ystage).then_inc(ys_hi, 1)
                sub_norm(1)
                split(p + 12)
                split(p + 13)

            def spread_rows(l, v, dst, streams, landed_in):
                for s in streams:
                    a = (6 * l + v) * D
                    load(dst[:, s, :], mod_dram[s, a:a + D].partition_broadcast(P), landed_in)

            def norm_rows(n):
                l, v = divmod(n - 8, 2)
                streams = (0, 1)[:NORMS[n] // 2]
                load(gain(n), gain_src[n].partition_broadcast(P), modb_landed)
                spread_rows(l, 3 * v + 1, sc_rows, streams, modb_landed)
                spread_rows(l, 3 * v, sh_rows, streams, modb_landed)

            for l in range(DEPTH):
                norm(4 * l)
                ffn(2 * l)
                norm(4 * l + 1, mid=G0[f"in{l}"] + 2)
                mix1(l)
                norm(4 * l + 2, mid=G0[f"ffn{2 * l + 1}"] + 1)
                if l == 1:
                    load(xres[:, 2:4, :], A["ctx_2"][0].rearrange("(t p) d -> p t d", p=P), x_landed)
                    norm_rows(8)
                    spread_rows(0, 2, g_rows, (0, 1), gate_landed)
                ffn(2 * l + 1)
                norm(4 * l + 3)

            def even():
                p = G0["even"]
                norm(8, mid=p + 2)
                act.wait_ge(tr_ready, BANK0[9])
                load(w(R0 + 3072, 1024), consts("dft_l"), dftl_landed)
                split(p + 3)
                split(p + 4)
                act.wait_ge(panel_done, p + 2)
                for t in range(4):
                    act.copy(a_rows[:, t, :], ps[:, t, :]).then_inc(acopy, 1)
                split(p + 5)
                split(p + 6)
                split(p + 7)
                act.wait_ge(panel_done, p + 6)
                for m in range(4):
                    act.copy(cT[:, m, :], ps[:, m, :]).then_inc(ccopy, 1)
                split(p + 8)
                split(p + 9)
                split(p + 10)

                def seq_copy(i):
                    act.wait_ge(pt_ready, i + 1)
                    act.copy(pt[:, i % 2, :], ps[:, i % 2, :]).then_inc(ptc_ready, 1)

                def chan_copy(i):
                    s, grp = divmod(i, 4)
                    act.wait_ge(f_ready, i + 1)
                    act.copy(t_hi[:, grp * 512 + s * 256:grp * 512 + s * 256 + 256], ps[:, 2 + i % 2, 0:256]).then_inc(fc_hi, 1)

                for i in range(9):
                    if i < 8:
                        seq_copy(i)
                    if i >= 1:
                        chan_copy(i - 1)
                act.wait_ge(conv2_ready, 4)
                norm_rows(9)
                split(p + 11)
                split(p + 12)

            def moe(m):
                nt, n = TILES[m], 9 + 2 * m
                b0, p0, q0 = BLOCK_BASE[m], G0[f"moe{m}"], G0[f"extra{m}"]
                streams = (0, 1)[:nt // 2]
                act.wait_ge(x_ready, 9 + 2 * m)
                spread_rows(m, 5, g_rows, streams, gate_landed)
                norm(n, mid=p0 + 1)
                for t in range(nt):
                    load(h_dram[t * P:(t + 1) * P, :], hrow[:, t, :], h_stored)
                act.wait_ge(gmax_ready, m + 1)
                act.activation(r_gexp[:, 0:nt, :], r_gcand[:, 0:nt, :], ACT.Exp).then_inc(gexp_ready, 1)
                act.wait_ge(top_ready, m + 1)
                act.activation(r_s[:, 5, 0:nt], r_s[:, 4, 0:nt], ACT.Exp).then_inc(texp_ready, 1)

                def rows_hi(b, par):
                    act.wait_ge(xgt_ready, b0 + b + 1)
                    for h in range(2):
                        act.copy(t_hi[:, par * 1024 + h * BANK:par * 1024 + (h + 1) * BANK], ps[:, h, :]).then_inc(xgT_hi, 1)

                def tanh(b, half, done):
                    act.wait_ge(panel_done, done)
                    act.activation(sgm[:, half, :], ps[:, 2 + half, 0:256], ACT.Tanh, scale=0.5).then_inc(mtanh_ready, 1)

                def act_hi(b, half):
                    act.wait_ge(mat_ready, 2 * (b0 + b) + half + 1)
                    act.copy(t_hi[:, AT + half * 256:AT + half * 256 + 256], ps[:, 4 + half, 0:256]).then_inc(maT_hi, 1)

                def out_rows(b, par, done, first=False):
                    act.wait_ge(panel_done, done)
                    if not first:
                        act.wait_ge(y_stored[par], 8 * (b0 + b - par))
                    act.copy(ysb[:, par, 0:BANK], ps[:, 6, :]).then_inc(y_act, 1)
                    act.wait_ge(y_act, b0 + b + 1)
                    act.wait_ge(y_dve, b0 + b + 1)
                    act.dma_start(y_dram.rearrange("(b p) d -> b p d", p=P)[bass.ds(b, 1)].rearrange("a p d -> p (a d)"),
                                  ysb[:, par, :]).then_inc(y_stored[par], 16)

                def block_of(b, par, p, j, i=0, prev=True, first=False, last=False):
                    split(p + 3, j + 3, i)
                    tanh(b, 0, p + 1 if prev else p + 2)
                    split(p + 4, j + 4, i)
                    if prev:
                        out_rows(b - 1, 1 - par, p + 2, first=first)
                    split(p + 5, j + 5, i)
                    act_hi(b, 0)
                    if not last:
                        rows_hi(b + 1, 1 - par)
                        split(p + 6, j + 6, i)
                    tanh(b, 1, p + 4)
                    if not last:
                        split(p + 7, j + 7, i)
                        split(p + 8, j + 8, i)
                    act_hi(b, 1)

                split(p0 + 2)
                rows_hi(0, 0)
                block_of(0, 0, p0, p0, prev=False)
                block_of(1, 1, p0 + 6, p0 + 6, first=m == 0)
                block_of(2, 0, p0 + 12, p0 + 12, first=m == 0)
                block_of(3, 1, p0 + 18, p0 + 18)
                with act.Fori(2, EXPERTS // 2 - 1) as i:
                    for v in range(2):
                        block_of(2 * i + v, v, p0 + 12 * i + 6 * v, p0 + 6 * v, i)
                for b in (EXPERTS - 2, EXPERTS - 1):
                    block_of(b, b % 2, p0 + 6 * b, p0 + 6 * b, last=b == EXPERTS - 1)
                out_rows(EXPERTS - 1, 1, p0 + 6 * EXPERTS)

                act.wait_ge(extra_filled, 16)
                used = act.value_load(extra_used[0:1, 0:1], min_val=0, max_val=EXTRA[m])
                with act.Fori(0, EXTRA[m] // 2) as i:
                    for v in range(2):
                        b, q, j = EXPERTS + 2 * i + v, q0 + 12 * i + 6 * v, q0 + 6 * v
                        with act.If(used > 2 * i + v):
                            split(q, j, i)
                            split(q + 1, j + 1, i)
                            rows_hi(b, v)
                            split(q + 2, j + 2, i)
                            tanh(b, 0, q + 2)
                            split(q + 3, j + 3, i)
                            act_hi(b, 0)
                            split(q + 4, j + 4, i)
                            tanh(b, 1, q + 4)
                            split(q + 5, j + 5, i)
                            act_hi(b, 1)
                            out_rows(b, v, q + 6)
                        with act.Else():
                            act.drain()
                            act.sem_inc(w_hi_ready, 6)
                            act.sem_inc(xgT_hi, 2)
                            act.sem_inc(mtanh_ready, 2)
                            act.sem_inc(maT_hi, 2)
                            act.sem_inc(y_act, 1)
                            act.wait_ge(y_stored[v], 8 * (b0 + b - v))
                            act.sem_inc(y_stored[v], 16)
                if m == 0:
                    act.wait_ge(w_ready, G0["odd"])
                    norm_rows(10)
                    split(G0["odd"])
                    split(G0["odd"] + 1)
                for t in range(nt):
                    act.wait_ge(yg_landed[t], 32 * (m + 1))
                    y1 = yg[t][:, 0, :]
                    act.activation(y1, y1, ACT.Copy, scale=gates[:, 0, t:t + 1]).then_inc(y1_ready, 1)

            def odd():
                p = G0["odd"]
                act.wait_ge(x_ready, 10)
                spread_rows(1, 2, g_rows, (0,), gate_landed)
                norm(10, mid=p + 2)
                act.wait_ge(row_ready, TILE0[11])
                load(w(R3 + 3072, 512), consts("window"), dftl_landed)
                split(p + 3)
                split(p + 4)
                split(p + 5)
                act.wait_ge(panel_done, p + 4)
                act.activation(sq2, psf[:, 0:4 * BANK], ACT.Square).then_inc(sq_ready, 1)
                split(p + 6)
                split(p + 7)
                act.wait_ge(qks_ready, 5)
                act.activation(std[:, 0:32], ss[:, 0:32], ACT.Sqrt, bias=eps[:, 0:1], scale=1 / HD).then_inc(qkstd_ready, 1)
                act.wait_ge(panel_done, p + 6)
                act.activation(sq2[:, 0:1024].rearrange("p (t n) -> p t n", t=4), ps[:, 4:8, 0:256],
                               ACT.Square).then_inc(sq_ready, 1)
                for t in range(4):
                    act.copy(v2[:, t, :], ps[:, 4 + t, 256:512]).then_inc(v2_ready, 1)
                split(p + 8)
                act.wait_ge(qks_ready, 6)
                act.activation(std[:, 0:16], ss[:, 0:16], ACT.Sqrt, bias=eps[:, 0:1], scale=1 / HD).then_inc(qkstd_ready, 1)
                for b in range(4):
                    t, j = divmod(b, 2)
                    act.wait_ge(qkt_ready, 4 + b + 1)
                    act.copy(qT2[:, 4 * j:4 * j + 4, t * P:(t + 1) * P],
                             ps[:, b, :].rearrange("p (h n) -> p h n", h=4)).then_inc(qkT_ready, 1)
                for h in range(4):
                    act.wait_ge(qkt_ready, 8 + h + 1)
                    act.copy(kT2[:, h, :], ps[:, 4 + h, :]).then_inc(qkT_ready, 1)

                def exps(i):
                    h = i // 2
                    act.wait_ge(s_ready, 16 + i + 1)
                    act.activation(m1[:, i % 2, 2:3], rows2[:, 2 * HD + h:2 * HD + h + 1], ACT.Exp,
                                   bias=m1[:, i % 2, 1:2])
                    act.activation(p2[:, i % 2, :], s2[:, i % 2, :], ACT.Exp, bias=m1[:, i % 2, 1:2],
                                   accum_out=m1[:, i % 2, 3:4]).then_inc(p_ready, 1)

                def weights_T(i):
                    act.wait_ge(at_ready, 16 + i + 1)
                    act.copy(pT2[:, i % 2, :], ps[:, 2 + i % 2, :]).then_inc(aT_ready, 1)

                for i in range(33):
                    if i < 32:
                        exps(i)
                    if i >= 1:
                        weights_T(i - 1)
                act.wait_ge(o_ready, 16 + 32)
                norm_rows(11)
                for b in range(4):
                    act.copy(t_hi[:, b * BANK:(b + 1) * BANK], ps[:, 4 + b, :]).then_inc(ao_hi, 1)
                split(p + 9)
                split(p + 10)

            even()
            moe(0)
            odd()
            moe(1)
            for t in range(2):
                act.wait_ge(combined, 4 + t + 1)
                act.dma_start(out[0, t * P:(t + 1) * P, :], xres[:, t, :]).then_inc(out_stored, 16)
            act.wait_ge(out_stored, 32)

        @block.vector
        def _(dve):
            def spread(v, shape):
                return v.unsqueeze(len(shape) - 1).to_broadcast(shape)

            def rest(dst, src, hi):
                return dve.tensor_tensor(dst, src, hi.bitcast(F32), ALU.subtract)

            def split(p, j=None):
                j = p if j is None else j
                dve.wait_ge(w_hi_ready, p + 1)
                hi, lo = slot(j)
                rest(lo, raw_slot(j)[0], hi).then_inc(w_ready, 1)

            def newton(r, v, t):
                dve.tensor_tensor(t, r, r, ALU.mult)
                dve.drain()
                dve.tensor_tensor(t, t, v, ALU.mult)
                dve.drain()
                dve.tensor_scalar(t, t, -0.5, 1.5, ALU.mult, ALU.add)
                dve.drain()
                dve.tensor_tensor(r, r, t, ALU.mult)

            def silu_times(dst, tanh, g, u):
                dve.scalar_tensor_tensor(tanh, tanh, 1.0, g, ALU.add, ALU.mult)
                dve.drain()
                return dve.scalar_tensor_tensor(dst, tanh, 0.5, u, ALU.mult, ALU.mult)

            def rstd(a, b, scale, ready, count):
                dve.wait_ge(ready, count)
                dve.tensor_scalar(var[:, a:b], ss[:, a:b], scale, EPS, ALU.mult, ALU.add)
                dve.reciprocal(rs[:, a:b], std[:, a:b])
                dve.drain()
                newton(rs[:, a:b], var[:, a:b], rt[:, a:b])
                dve.drain()

            dve.memset(eps[:, :], EPS)
            dve.memset(ones_c[:, :], 1 / 256)
            dve.memset(w(R3 + 3584, 512), 0.0)
            dve.memset(t_hi[:, 0:1024].bitcast(F32), 0.0)
            dve.memset(t_lo[:, 0:1024].bitcast(F32), 0.0)
            dve.memset(ones[:, :], 1.0).then_inc(ones_ready, 1)

            def mod_add(p, j):
                dve.wait_ge(panel_done, p + 1)
                a = bass.ds(p * PC, PC)
                dve.tensor_tensor(modrow[:, a], modrow[:, a], ps[0:2, j % 6, 0:PC], ALU.add).then_inc(mod_copied, 1)

            dve.wait_ge(cond_ready, 1)
            rest(t_lo[:, 0:1024].rearrange("p (k n) -> p k n", k=KD)[:, :, 0:2], cond[:, :, :],
                 t_hi[:, 0:1024].rearrange("p (k n) -> p k n", k=KD)[:, :, 0:2]).then_inc(cond_ready, 1)
            dve.wait_ge(bmod_landed, 16)
            for j in range(12):
                split(j)
                if j >= 2:
                    mod_add(j - 2, j - 2)
            with dve.Fori(1, 4) as i:
                for j in range(12):
                    split(12 * i + j, j)
                    mod_add(12 * i + j - 2, (j - 2) % 12)
            split(48)
            mod_add(46, 46)
            split(49)
            mod_add(47, 47)
            dve.wait_ge(mod_stored, 16)
            dve.wait_ge(const_landed, 16 * CONST_DMAS)
            dve.wait_ge(x_landed, 16)

            def norm(n, nt, modulated=False, rows_out=True):
                for t in range(nt // 2):
                    dve.tensor_tensor_reduce(hrow[:, t, :], xres[:, t, :], xres[:, t, :], 1 / D, 0.0,
                                             ALU.mult, ALU.add, ss[:, t:t + 1])
                dve.drain().then_inc(ms_ready, 1)
                if n < 8:
                    dve.wait_ge(gain_landed, 16 * (n + 1))
                if modulated:
                    dve.wait_ge(modb_landed, MODB[n - 8])
                    for s in range(nt // 2):
                        dve.scalar_tensor_tensor(sc_rows[:, s, :], sc_rows[:, s, :], 1.0, gain(n), ALU.add, ALU.mult)
                rstd(0, nt, 1.0, std_ready, n + 1)
                for t in range(nt):
                    dst = hrow[:, t, :] if rows_out else xres[:, t, :]
                    if modulated:
                        dve.scalar_tensor_tensor(dst, xres[:, t, :], rs[:, t:t + 1], sc_rows[:, t // 2, :], ALU.mult, ALU.mult)
                        dve.drain()
                        dve.tensor_tensor(dst, dst, sh_rows[:, t // 2, :], ALU.add).then_inc(row_ready, 1)
                    else:
                        h = dve.scalar_tensor_tensor(dst, xres[:, t, :], rs[:, t:t + 1], gain(n), ALU.mult, ALU.mult)
                        if rows_out:
                            h.then_inc(row_ready, 1)
                if not rows_out:
                    dve.drain().then_inc(x_ready, 1)

            def hT_rest(n, mid=None):
                if mid is not None:
                    split(mid)
                for j in range(2 * NORMS[n]):
                    dve.wait_ge(hT_hi, BANK0[n] + j + 1)
                    a = slice(j * BANK, (j + 1) * BANK)
                    rest(t_lo[:, a], ps[:, j, :], t_hi[:, a]).then_inc(hT_lo, 1)

            def residual(last_panel, scale):
                dve.wait_ge(panel_done, last_panel)
                for t in range(2):
                    dve.scalar_tensor_tensor(xres[:, t, :], psf[:, 2 * t * BANK:(2 * t + 2) * BANK], scale,
                                             xres[:, t, :], ALU.mult, ALU.add)
                dve.drain().then_inc(x_ready, 1)

            def ffn(f):
                p0 = G0[f"ffn{f}"]

                def unit(u, par, v):
                    split(p0 + 3 * u + 2, p0 + 3 * v + 2)
                    dve.wait_ge(silu_ready, FF_UNITS * f + u + 1)
                    g = sg1[:, 2 * par:2 * par + 2, :]
                    silu_times(g, g, ps[:, 4 + 2 * par:6 + 2 * par, 0:256], ps[:, 4 + 2 * par:6 + 2 * par, 256:512])
                    dve.drain()
                    hi, lo = (t.rearrange("p (c n) -> p c n", c=2) for t in T(AT + par * 512, 512))
                    dve.tensor_copy(hi, g)
                    dve.drain()
                    rest(lo, g, hi).then_inc(act_ready, 1)
                    if v < 10:
                        split(p0 + 3 * u + 3, p0 + 3 * v + 3)
                        split(p0 + 3 * u + 4, p0 + 3 * v + 4)

                unit(0, 0, 0)
                with dve.Fori(0, 2) as i:
                    for v in range(1, 5):
                        unit(4 * i + v, v % 2, v)
                unit(9, 1, 9)
                unit(10, 0, 10)
                split(p0 + 33)
                split(p0 + 34)
                residual(p0 + 33, 0.5)

            def head_norm(src, dst, nh, gain_row, scale, count, mid):
                dve.wait_ge(sq_ready, count)
                dve.tensor_reduce(ss[:, 0:nh], sqt.rearrange("p (h n) -> p h n", n=HD), X, ALU.add).then_inc(qks_ready, 1)
                split(mid)
                dve.drain()
                rstd(0, nh, 1 / HD, qkstd_ready, count)
                d3 = dst.rearrange("p (h n) -> p h n", n=HD)
                dve.tensor_tensor(d3, src.rearrange("p (h n) -> p h n", n=HD), spread(rs[:, 0:nh], [P, nh, HD]), ALU.mult)
                dve.drain()
                dve.scalar_tensor_tensor(d3, d3, scale, gain_row.unsqueeze(1).to_broadcast([P, nh, HD]),
                                         ALU.mult, ALU.mult).then_inc(qkn_ready, 1)

            def mix1(l):
                p = G0[f"in{l}"]
                r1 = rows1[:, l, :]
                dve.memset(zpad[:, :, 0:PAD], 0.0)
                dve.memset(zpad[:, :, PAD + SEQ:], 0.0)
                split(p + 3)
                dve.wait_ge(sig_ready, l + 1)
                dve.tensor_scalar(sig, sig, 0.5, 0.5, ALU.mult, ALU.add)
                dve.drain()
                dve.tensor_tensor(zpad[:, :, PAD:PAD + SEQ], ps[:, 0, :].rearrange("p (c n) -> p c n", c=2), sig,
                                  ALU.mult).then_inc(z_ready, 1)
                for x in (4, 5, 6, 7):
                    split(p + x)
                head_norm(psf[:, 3 * BANK:5 * BANK], qn, 16, r1[:, 0:HD], HD ** -0.5, 2 * l + 1, p + 8)
                split(p + 9)
                dve.drain()
                head_norm(psf[:, 5 * BANK:7 * BANK], kn, 16, r1[:, HD:2 * HD], 1.0, 2 * l + 2, p + 10)
                split(p + 11)
                dve.tensor_tensor_reduce(s1[:, 0, 0:HD], r1[:, 128:192], r1[:, 192:256], 1.0, 0.0,
                                         ALU.mult, ALU.add, lam[:, 0:1])
                dve.tensor_tensor_reduce(s1[:, 0, HD:2 * HD], r1[:, 256:320], r1[:, 320:384], 1.0, 0.0,
                                         ALU.mult, ALU.add, lam[:, 1:2])
                dve.drain().then_inc(lam_ready, 1)
                def centre():
                    dve.wait_ge(mean_ready, l + 1)
                    dve.tensor_tensor(conv_acc, conv_acc, ps[:, 2, 0:256].unsqueeze(1).to_broadcast([P, 2, 256]), ALU.subtract)
                    dve.drain()
                    dve.tensor_tensor(sig, conv_acc, conv_acc, ALU.mult).then_inc(xsq_ready, 1)

                def normalise():
                    dve.wait_ge(lnstd_ready, l + 1)
                    dve.tensor_scalar(dT[:, 0, :], ps[:, 2, 256:512], EPS, None, ALU.add)
                    dve.reciprocal(sig[:, 1, :], sig[:, 0, :])
                    dve.drain()
                    newton(sig[:, 1, :], dT[:, 0, :], dT[:, 1, :])
                    dve.drain()
                    dve.tensor_tensor(conv_acc, conv_acc, sig[:, 1, :].unsqueeze(1).to_broadcast([P, 2, 256]),
                                      ALU.mult).then_inc(ln_ready, 1)

                dve.wait_ge(lame_ready, l + 1)
                dve.tensor_tensor(lam[:, 4:5], lam[:, 3:4], lam[:, 2:3], ALU.subtract)
                dve.drain()
                dve.tensor_scalar(lam[:, 5:6], lam[:, 4:5], -lam_init[l], None, ALU.add)
                dve.drain()

                def bias_and_max(i):
                    qt, h = divmod(i, 4)
                    dve.wait_ge(sc_ready, 8 * l + i + 1)
                    dve.scalar_tensor_tensor(s1[:, i % 2, :].rearrange("p (c n) -> p c n", c=2),
                                             ndist[:, qt, :].unsqueeze(1).to_broadcast([P, 2, SEQ]), slopes[h],
                                             ps[:, 3 + 2 * (i % 2):5 + 2 * (i % 2), 0:256], ALU.mult, ALU.add)
                    dve.drain()
                    dve.tensor_reduce(m1[:, i % 2, 0:2], s1[:, i % 2, :].rearrange("p (c n) -> p c n", c=2), X,
                                      ALU.max, negate=True).then_inc(s_ready, 1)

                def weights(i):
                    b = i % 2
                    dve.wait_ge(p_ready, 8 * l + i + 1)
                    if i >= 2:
                        dve.wait_ge(at_ready, 8 * l + i - 1)
                    dve.reciprocal(m1[:, b, 4:6], m1[:, b, 2:4])
                    dve.drain()
                    dve.tensor_tensor(m1[:, b, 6:7], m1[:, b, 5:6], lam[:, 5:6], ALU.mult)
                    dve.tensor_scalar(a1[:, b, :], p1[:, b, 0:256], m1[:, b, 4:5], None, ALU.mult)
                    dve.drain()
                    dve.scalar_tensor_tensor(a1[:, b, :], p1[:, b, 256:512], m1[:, b, 6:7], a1[:, b, :],
                                             ALU.mult, ALU.add).then_inc(a_ready, 1)

                def sub_norm(qt):
                    dve.wait_ge(osq_ready, 2 * l + qt + 1)
                    dve.tensor_reduce(ss[:, 32:36], osq.rearrange("p (h n) -> p h n", h=4), X, ALU.add).then_inc(oss_ready, 1)
                    dve.drain()
                    rstd(32, 36, 1 / P, ostd_ready, 2 * l + qt + 1)
                    if qt == 1:
                        dve.wait_ge(ot_ready, 2 * l + 1)
                    o3 = on.rearrange("p (h n) -> p h n", h=4)
                    dve.tensor_tensor(o3, ps[:, (7, 0)[qt], :].rearrange("p (h n) -> p h n", h=4),
                                      spread(rs[:, 32:36], [P, 4, P]), ALU.mult)
                    dve.drain()
                    dve.scalar_tensor_tensor(o3, o3, 1.0 - lam_init[l],
                                             r1[:, 384:512].unsqueeze(1).to_broadcast([P, 4, P]),
                                             ALU.mult, ALU.mult).then_inc(on_ready, 1)
                    dve.wait_ge(ao_hi, 2 * l + qt + 1)
                    hi, lo = (t.rearrange("p (h n) -> p h n", h=4)[:, :, qt * P:(qt + 1) * P] for t in T(3072, 1024))
                    rest(lo, ps[:, 2, :].rearrange("p (h n) -> p h n", h=4), hi).then_inc(ao_lo, 1)

                for i in range(9):
                    if i < 8:
                        bias_and_max(i)
                    if i >= 1:
                        weights(i - 1)
                    if i == 5:
                        centre()
                    if i == 6:
                        normalise()
                    if i == 7:
                        sub_norm(0)
                    if i == 8:
                        dve.wait_ge(ys_hi, l + 1)
                        rest(t_lo[:, 2048:3072], ystage, t_hi[:, 2048:3072]).then_inc(ys_lo, 1)
                sub_norm(1)
                split(p + 12)
                split(p + 13)
                residual(p + 13, 1.0)

            for l in range(DEPTH):
                norm(4 * l, 2)
                hT_rest(4 * l)
                ffn(2 * l)
                norm(4 * l + 1, 2)
                hT_rest(4 * l + 1, mid=G0[f"in{l}"] + 2)
                mix1(l)
                norm(4 * l + 2, 2)
                hT_rest(4 * l + 2, mid=G0[f"ffn{2 * l + 1}"] + 1)
                ffn(2 * l + 1)
                norm(4 * l + 3, 2, rows_out=False)

            def gated_residual(last_panel, nt, gate_rows):
                dve.wait_ge(gate_landed, gate_rows)
                dve.wait_ge(panel_done, last_panel)
                for t in range(nt):
                    dve.tensor_tensor(prod, psf[:, 2 * t * BANK:(2 * t + 2) * BANK], g_rows[:, t // 2, :], ALU.mult)
                    dve.drain()
                    dve.tensor_tensor(xres[:, t, :], xres[:, t, :], prod, ALU.add)
                    dve.drain()
                dve.drain().then_inc(x_ready, 1)

            def even():
                p = G0["even"]
                dve.wait_ge(x_landed, 32)
                norm(8, 4, modulated=True)
                hT_rest(8, mid=p + 2)
                dve.memset(upad[:, :, :, 0:1], 0.0)
                dve.memset(upad[:, :, :, SEQ + 1:], 0.0)
                for x in (3, 4, 5):
                    split(p + x)
                dve.wait_ge(panel_done, p + 4)
                for m in range(4):
                    dve.tensor_copy(bT[:, m, :], ps[:, 4 + m, :]).then_inc(bcopy, 1)
                for x in (6, 7, 8, 9):
                    split(p + x)
                dve.wait_ge(ccopy, 4)
                dve.wait_ge(panel_done, p + 8)
                split(p + 10)
                dve.drain()
                for j in range(4):
                    u = upad[:, j % 2, :, :]
                    s3 = lambda v: v.rearrange("p (s n) -> p s n", s=2)
                    y = s3(conv2_y[:, j % 2, :])
                    dve.tensor_tensor(u[:, :, 1:SEQ + 1], s3(cT[:, j, :]), s3(ps[:, 4 + j, :]), ALU.mult)
                    dve.drain()
                    dve.tensor_scalar(y, u[:, :, 0:SEQ], conv2_w[:, j, 0:1], None, ALU.mult)
                    for tap in (1, 2):
                        dve.drain()
                        dve.scalar_tensor_tensor(y, u[:, :, tap:tap + SEQ], conv2_w[:, j, tap:tap + 1], y, ALU.mult, ALU.add)
                    dve.drain()
                    dve.tensor_tensor(y, y, s3(bT[:, j, :]), ALU.mult)
                    dve.drain()
                    hi, lo = T((4 + j) * 512, 512)
                    dve.tensor_copy(hi, conv2_y[:, j % 2, :])
                    dve.drain()
                    rest(lo, conv2_y[:, j % 2, :], hi).then_inc(conv2_ready, 1)
                    for i in (2 * j, 2 * j + 1):
                        s, grp = divmod(i, 4)
                        dve.wait_ge(fc_hi, i + 1)
                        hi, lo = T(grp * 512 + s * 256, 256)
                        rest(lo, ps[:, 2 + i % 2, 0:256], hi).then_inc(fc_lo, 1)
                split(p + 11)
                split(p + 12)
                gated_residual(p + 12, 4, GATE[0])

            def first_max(v, nt, width, mx, eq, cand, oh):
                iw = iota[:, 0:width].unsqueeze(1).to_broadcast([P, nt, width])
                dve.tensor_reduce(mx, v, X, ALU.max)
                dve.drain()
                dve.tensor_tensor(eq, v, spread(mx, [P, nt, width]), ALU.is_equal)
                dve.drain()
                dve.scalar_tensor_tensor(cand, eq, -1000.0, iw, ALU.mult, ALU.add)
                dve.drain()
                dve.tensor_reduce(r_s[:, 15, 0:nt], cand, X, ALU.min)
                dve.drain()
                dve.tensor_tensor(oh, cand, spread(r_s[:, 15, 0:nt], [P, nt, width]), ALU.is_equal)
                dve.drain()

            def moe(m):
                nt, n, nb, b0, nx = TILES[m], 9 + 2 * m, BLOCKS[m], BLOCK_BASE[m], EXTRA[m]
                p0, q0 = G0[f"moe{m}"], G0[f"extra{m}"]
                norm(n, nt, modulated=True)
                hT_rest(n, mid=p0 + 1)
                S = lambda i: r_s[:, i, 0:nt]
                lg = r_logit[:, 0:nt, :]
                dve.wait_ge(logit_ready, m + 1)
                dve.tensor_tensor(lg, ps[:, 0, 0:nt * NLOG].rearrange("p (t n) -> p t n", t=nt),
                                  router_b[:, m, :].unsqueeze(1).to_broadcast([P, nt, NLOG]), ALU.add)
                dve.drain()
                goh = r_goh[:, 0:nt, :]
                first_max(lg[:, :, 0:GROUPS], nt, GROUPS, S(0), r_gneg[:, 0:nt, :], r_gcand[:, 0:nt, :], goh)
                dve.tensor_tensor(r_gcand[:, 0:nt, :], lg[:, :, 0:GROUPS], spread(S(0), [P, nt, GROUPS]),
                                  ALU.subtract).then_inc(gmax_ready, 1)
                dve.tensor_scalar(r_gneg[:, 0:nt, :], goh, BIG, -BIG, ALU.mult, ALU.add)
                dve.drain()
                em, em2 = r_em[:, 0:nt, :], r_em2[:, 0:nt, :]
                oh1, oh2, cand = r_oh1[:, 0:nt, :], r_oh2[:, 0:nt, :], r_cand[:, 0:nt, :]
                for t in range(nt):
                    dve.tensor_tensor(r_em[:, t, :].rearrange("p (a b) -> p a b", a=GROUPS),
                                      r_logit[:, t, GROUPS:].rearrange("p (a b) -> p a b", a=GROUPS),
                                      spread(r_gneg[:, t, :], [P, GROUPS, PER_GROUP]), ALU.add)
                dve.drain()
                first_max(em, nt, EXPERTS, S(1), em2, cand, oh1)
                dve.scalar_tensor_tensor(em2, oh1, -3 * BIG, em, ALU.mult, ALU.add)
                dve.drain()
                first_max(em2, nt, EXPERTS, S(2), r_tmp[:, 0:nt, :], cand, oh2)
                dve.tensor_tensor(S(4), S(2), S(1), ALU.subtract).then_inc(top_ready, 1)
                dve.tensor_tensor(r_mem[:, 0:nt, :], oh1, oh2, ALU.add).then_inc(member_ready, 1)
                dve.wait_ge(gexp_ready, m + 1)
                dve.tensor_reduce(S(6), r_gexp[:, 0:nt, :], X, ALU.add)
                dve.wait_ge(texp_ready, m + 1)
                dve.tensor_scalar(S(7), S(5), 1.0, None, ALU.add)
                dve.drain()
                dve.tensor_tensor(S(8), S(6), S(7), ALU.mult)
                dve.drain()
                dve.reciprocal(gates[:, 0, 0:nt], S(8))
                dve.drain()
                dve.tensor_tensor(gates[:, 1, 0:nt], gates[:, 0, 0:nt], S(5), ALU.mult)
                dve.wait_ge(pos_ready, m + 1)
                pos = r_tmp[:, 0:nt, :]
                dve.tensor_copy(pos, ps[:, 1, 0:nt * 32].rearrange("p (t n) -> p t n", t=nt))
                dve.tensor_copy(r_cnt, ps[:, 1, nt * 32:nt * 32 + 32])
                dve.drain()
                dve.tensor_scalar(r_nx, r_cnt, 128.0, None, ALU.is_gt)
                for thr in (256.0, 384.0):
                    dve.drain()
                    dve.scalar_tensor_tensor(r_nx, r_cnt, thr, r_nx, ALU.is_gt, ALU.add)
                dve.drain()
                dve.tensor_copy(r_t1, r_nx)
                dve.drain()
                src, dst = r_t1, r_xs
                for sh in (1, 2, 4, 8, 16):
                    dve.tensor_copy(dst[:, 0:sh], src[:, 0:sh])
                    dve.tensor_tensor(dst[:, sh:], src[:, sh:], src[:, 0:EXPERTS - sh], ALU.add)
                    dve.drain()
                    src, dst = dst, src
                incl = src
                excl = dst
                dve.tensor_tensor(excl, incl, r_nx, ALU.subtract)
                dve.drain()
                dve.tensor_tensor(r_shift, excl, iota[:, 0:32], ALU.subtract)
                dve.drain()
                dve.tensor_scalar(r_shift, r_shift, float(EXPERTS - 1), 128.0, ALU.add, ALU.mult)
                dve.drain()
                bc = lambda v: v.unsqueeze(1).to_broadcast([P, nt, EXPERTS])
                sl = r_slot[:, 0:nt, :]
                dve.scalar_tensor_tensor(sl, pos, 128.0, bc(r_shift), ALU.is_ge, ALU.mult)
                dve.drain()
                dve.tensor_tensor(sl, sl, pos, ALU.add)
                dve.drain()
                dve.scalar_tensor_tensor(sl, bc(iota[:, 0:32]), 128.0, sl, ALU.mult, ALU.add)
                dve.drain()
                for kk, oh in enumerate((oh1, oh2)):
                    dve.tensor_tensor(cand, oh, sl, ALU.mult)
                    dve.drain()
                    dve.tensor_reduce(r_sl[:, kk, 0:nt], cand, X, ALU.add)
                    dve.drain()
                for kk in range(2):
                    dve.tensor_copy(r_sli[:, kk, 0:nt], r_sl[:, kk, 0:nt])
                    dve.tensor_copy(slot_id[:, 0:nt, kk], r_sl[:, kk, 0:nt])
                dve.drain()
                for kk in range(2):
                    dve.tensor_scalar(r_blki[:, kk, 0:nt], r_sli[:, kk, 0:nt], 7, None, ALU.logical_shift_right)
                    dve.tensor_scalar(r_ini[:, kk, 0:nt], r_sli[:, kk, 0:nt], 127, None, ALU.bitwise_and)
                dve.drain()
                for kk in range(2):
                    dve.tensor_copy(r_blkf[:, kk, 0:nt], r_blki[:, kk, 0:nt])
                    dve.tensor_copy(r_inf[:, kk, 0:nt], r_ini[:, kk, 0:nt])
                dve.drain()
                for kk in range(2):
                    for t in range(nt):
                        i = kk * nt + t
                        dve.tensor_scalar(r_onehot[:, i, :], iota, r_inf[:, kk, t:t + 1], None, ALU.is_equal)
                        dve.tensor_scalar(r_blk[:, i, 0:nb], iota[:, 0:nb], r_blkf[:, kk, t:t + 1],
                                          k("tokid")[:, t:t + 1], ALU.is_equal, ALU.mult)
                dve.drain().then_inc(onehot_ready, 1)
                ix = spread(iota[:, 0:nx], [P, nx, EXPERTS])
                ex, ex2 = r_ex[:, 0:nx, :], r_ex2[:, 0:nx, :]
                bx = lambda v: v.unsqueeze(1).to_broadcast([P, nx, EXPERTS])
                dve.tensor_tensor(ex, ix, bx(excl), ALU.is_ge)
                dve.tensor_tensor(ex2, ix, bx(incl), ALU.is_lt)
                dve.drain()
                dve.tensor_tensor(ex, ex, ex2, ALU.mult)
                dve.drain()
                dve.tensor_tensor(ex, ex, bx(iota[:, 0:32]), ALU.mult)
                dve.drain()
                dve.tensor_reduce(r_exid[:, 0:nx], ex, X, ALU.add)
                dve.drain()
                dve.tensor_copy(extra_id[:, 0:nx], r_exid[:, 0:nx])
                dve.tensor_copy(extra_used[0:1, 0:1], incl[0:1, EXPERTS - 1:EXPERTS])
                dve.wait_ge(tps_ready, m + 1)
                dve.tensor_copy(table[:, 0:nb], ps[:, 2, 0:nb])
                dve.drain().then_inc(table_ready, 1)

                def rows_lo(b, par):
                    for h in range(2):
                        dve.wait_ge(xgT_hi, 2 * (b0 + b) + h + 1)
                        a = slice(par * 1024 + h * BANK, par * 1024 + (h + 1) * BANK)
                        rest(t_lo[:, a], ps[:, h, :], t_hi[:, a]).then_inc(xgT_lo, 1)

                def silu_up(b, half):
                    dve.wait_ge(mtanh_ready, 2 * (b0 + b) + half + 1)
                    silu_times(am[:, half, :], sgm[:, half, :], ps[:, 2 + half, 0:256],
                               ps[:, 2 + half, 256:512]).then_inc(mact_ready, 1)

                def act_lo(b, half):
                    dve.wait_ge(maT_hi, 2 * (b0 + b) + half + 1)
                    a = slice(AT + half * 256, AT + half * 256 + 256)
                    rest(t_lo[:, a], ps[:, 4 + half, 0:256], t_hi[:, a]).then_inc(maT_lo, 1)

                def out_rows(b, par, done, first=False):
                    dve.wait_ge(panel_done, done)
                    if not first:
                        dve.wait_ge(y_stored[par], 8 * (b0 + b - par))
                    dve.tensor_copy(ysb[:, par, BANK:2 * BANK], ps[:, 7, :]).then_inc(y_dve, 1)

                def block_of(b, par, p, j, prev=True, first=False, last=False):
                    split(p + 3, j + 3)
                    silu_up(b, 0)
                    split(p + 4, j + 4)
                    if prev:
                        out_rows(b - 1, 1 - par, p + 2, first=first)
                    split(p + 5, j + 5)
                    act_lo(b, 0)
                    if not last:
                        rows_lo(b + 1, 1 - par)
                        split(p + 6, j + 6)
                    silu_up(b, 1)
                    if not last:
                        split(p + 7, j + 7)
                        split(p + 8, j + 8)
                    act_lo(b, 1)

                split(p0 + 2)
                rows_lo(0, 0)
                block_of(0, 0, p0, p0, prev=False)
                block_of(1, 1, p0 + 6, p0 + 6, first=m == 0)
                block_of(2, 0, p0 + 12, p0 + 12, first=m == 0)
                block_of(3, 1, p0 + 18, p0 + 18)
                with dve.Fori(2, EXPERTS // 2 - 1) as i:
                    for v in range(2):
                        block_of(2 * i + v, v, p0 + 12 * i + 6 * v, p0 + 6 * v)
                for b in (EXPERTS - 2, EXPERTS - 1):
                    block_of(b, b % 2, p0 + 6 * b, p0 + 6 * b, last=b == EXPERTS - 1)
                out_rows(EXPERTS - 1, 1, p0 + 6 * EXPERTS)

                used = dve.value_load(extra_used[0:1, 0:1], min_val=0, max_val=EXTRA[m])
                with dve.Fori(0, EXTRA[m] // 2) as i:
                    for v in range(2):
                        b, q, j = EXPERTS + 2 * i + v, q0 + 12 * i + 6 * v, q0 + 6 * v
                        with dve.If(used > 2 * i + v):
                            split(q, j)
                            split(q + 1, j + 1)
                            rows_lo(b, v)
                            split(q + 2, j + 2)
                            silu_up(b, 0)
                            split(q + 3, j + 3)
                            act_lo(b, 0)
                            split(q + 4, j + 4)
                            silu_up(b, 1)
                            split(q + 5, j + 5)
                            act_lo(b, 1)
                            out_rows(b, v, q + 6)
                        with dve.Else():
                            dve.drain()
                            dve.sem_inc(w_ready, 6)
                            dve.sem_inc(xgT_lo, 2)
                            dve.sem_inc(mact_ready, 2)
                            dve.sem_inc(maT_lo, 2)
                            dve.sem_inc(y_dve, 1)
                if m == 0:
                    split(G0["odd"])
                    split(G0["odd"] + 1)
                dve.wait_ge(gate_landed, GATE[2 * m + 1])
                for t in range(nt):
                    y1, y2 = yg[t][:, 0, :], yg[t][:, 1, :]
                    dve.wait_ge(y1_ready, TILES[0] * m + t + 1)
                    dve.scalar_tensor_tensor(y1, y2, gates[:, 1, t:t + 1], y1, ALU.mult, ALU.add)
                    dve.drain()
                    dve.tensor_tensor(y1, y1, g_rows[:, t // 2, :], ALU.mult)
                    dve.drain()
                    dve.tensor_tensor(xres[:, t, :], xres[:, t, :], y1, ALU.add)
                    dve.drain().then_inc(combined, 1)
                dve.drain().then_inc(x_ready, 1)

            def rope(rows, nh, t):
                v = rows.rearrange("p (h x) -> p h x", h=nh)
                cos = k("cos")[:, t * 32:(t + 1) * 32].rearrange("p (a n) -> p a n", a=2)
                sin = k("sin")[:, t * 32:(t + 1) * 32].rearrange("p (a n) -> p a n", a=2)
                A4 = rope_a.rearrange("p (c a h n) -> p c a h n", c=2, a=2, h=16)
                B4 = rope_b.rearrange("p (c a h n) -> p c a h n", c=2, a=2, h=16)
                for a in range(2):
                    c = cos[:, a, :].unsqueeze(1).to_broadcast([P, nh, 16])
                    s = sin[:, a, :].unsqueeze(1).to_broadcast([P, nh, 16])
                    x1, x2 = v[:, :, 32 * a:32 * a + 16], v[:, :, 32 * a + 16:32 * a + 32]
                    dve.tensor_tensor(A4[:, 0, a, 0:nh, :], x1, c, ALU.mult)
                    dve.tensor_tensor(A4[:, 1, a, 0:nh, :], x2, s, ALU.mult)
                    dve.tensor_tensor(B4[:, 0, a, 0:nh, :], x1, s, ALU.mult)
                    dve.tensor_tensor(B4[:, 1, a, 0:nh, :], x2, c, ALU.mult)
                dve.drain()
                for a in range(2):
                    x1, x2 = v[:, :, 32 * a:32 * a + 16], v[:, :, 32 * a + 16:32 * a + 32]
                    dve.tensor_tensor(x1, A4[:, 0, a, 0:nh, :], A4[:, 1, a, 0:nh, :], ALU.subtract)
                    dve.tensor_tensor(x2, B4[:, 0, a, 0:nh, :], B4[:, 1, a, 0:nh, :], ALU.add)
                dve.drain()

            def odd():
                p = G0["odd"]
                norm(10, 4, modulated=True)
                hT_rest(10, mid=p + 2)
                for x in (3, 4, 5, 6, 7):
                    split(p + x)
                dve.wait_ge(sq_ready, 5)
                dve.tensor_reduce(ss[:, 0:32], sq2.rearrange("p (h n) -> p h n", n=HD), X, ALU.add).then_inc(qks_ready, 1)
                dve.drain()
                rstd(0, 32, 1 / HD, qkstd_ready, 5)
                q3 = w(R0, 2048).rearrange("p (h n) -> p h n", n=HD)
                dve.tensor_tensor(q3, psf[:, 0:2048].rearrange("p (h n) -> p h n", n=HD), spread(rs[:, 0:32], [P, 32, HD]), ALU.mult)
                dve.drain()
                dve.scalar_tensor_tensor(q3, q3, HD ** -0.5, rows2[:, 0:HD].unsqueeze(1).to_broadcast([P, 32, HD]),
                                         ALU.mult, ALU.mult)
                dve.drain()
                for t in range(2):
                    rope(q2[:, t, :], 16, t)
                dve.drain().then_inc(q2_ready, 1)
                dve.wait_ge(sq_ready, 6)
                dve.tensor_reduce(ss[:, 0:16], sq2[:, 0:1024].rearrange("p (h n) -> p h n", n=HD), X, ALU.add).then_inc(qks_ready, 1)
                split(p + 8)
                dve.drain()
                rstd(0, 16, 1 / HD, qkstd_ready, 6)
                kf = sq2[:, 1024:2048]
                for t in range(4):
                    dve.tensor_tensor(kf[:, t * 256:(t + 1) * 256].rearrange("p (h n) -> p h n", n=HD),
                                      ps[:, 4 + t, 0:256].rearrange("p (h n) -> p h n", n=HD),
                                      spread(rs[:, 4 * t:4 * t + 4], [P, 4, HD]), ALU.mult)
                dve.drain()
                k3 = kf.rearrange("p (h n) -> p h n", n=HD)
                dve.tensor_tensor(k3, k3, rows2[:, HD:2 * HD].unsqueeze(1).to_broadcast([P, 16, HD]), ALU.mult)
                dve.drain()
                for t in range(2):
                    rope(kf[:, t * 256:(t + 1) * 256], 4, t)
                for t in range(4):
                    for c in range(2):
                        dve.tensor_copy(kdup[:, t, :, c, :], kf[:, t * 256:(t + 1) * 256].rearrange("p (h n) -> p h n", n=HD))
                dve.drain().then_inc(k2_ready, 1)
                dve.wait_ge(dftl_landed, 32)
                dve.wait_ge(qkT_ready, 12)

                def bias_and_max(i):
                    h, qt = divmod(i, 2)
                    b = i % 2
                    dve.wait_ge(sc_ready, 16 + i + 1)
                    dve.tensor_tensor(s2[:, b, 0:256], ps[:, b, 0:256], window[:, qt, :], ALU.add)
                    dve.tensor_copy(s2[:, b, 256:512], ps[:, b, 256:512])
                    dve.drain()
                    dve.tensor_reduce(m1[:, b, 0:1], s2[:, b, :], X, ALU.max)
                    dve.drain()
                    dve.tensor_scalar(m1[:, b, 1:2], m1[:, b, 0:1], rows2[:, 2 * HD + h:2 * HD + h + 1], -1.0,
                                      ALU.max, ALU.mult).then_inc(s_ready, 1)

                def weights(i):
                    b = i % 2
                    dve.wait_ge(p_ready, 16 + i + 1)
                    dve.tensor_tensor(m1[:, b, 4:5], m1[:, b, 2:3], m1[:, b, 3:4], ALU.add)
                    dve.drain()
                    dve.reciprocal(m1[:, b, 5:6], m1[:, b, 4:5])
                    dve.drain()
                    dve.tensor_scalar(p2[:, b, :], p2[:, b, :], m1[:, b, 5:6], None, ALU.mult).then_inc(a_ready, 1)

                for i in range(33):
                    if i < 32:
                        bias_and_max(i)
                    if i >= 1:
                        weights(i - 1)
                for b in range(4):
                    dve.wait_ge(ao_hi, 4 + b + 1)
                    a = slice(b * BANK, (b + 1) * BANK)
                    rest(t_lo[:, a], ps[:, 4 + b, :], t_hi[:, a]).then_inc(ao_lo, 1)
                split(p + 9)
                split(p + 10)
                gated_residual(p + 10, 2, GATE[2])

            even()
            moe(0)
            odd()
            moe(1)

        @block.gpsimd
        def _(pool):
            def moe(m):
                nt, nb, b0 = TILES[m], BLOCKS[m], BLOCK_BASE[m]
                pool.wait_ge(table_ready, m + 1)
                pool.wait_ge(h_stored, 64 if m == 0 else 96)

                def gather(b, par, first=False):
                    if not first:
                        pool.wait_ge(xgt_ready, b0 + b - 1)
                    pool.tensor_copy(table_col[:, par:par + 1], table[:, bass.ds(b, 1)])
                    pool.drain()
                    pool.indirect_dma_start(out=xg[:, par, :], out_offset=None, in_=h_dram,
                                            in_offset=bass.IndirectOffsetOnAxis(ap=table_col[:, par:par + 1], axis=0)
                                            ).then_inc(xg_landed[m][par], 16)

                gather(0, 0, True)
                gather(1, 1, True)
                with pool.Fori(1, EXPERTS // 2) as i:
                    gather(2 * i, 0)
                    gather(2 * i + 1, 1)
                used = pool.value_load(extra_used[0:1, 0:1], min_val=0, max_val=EXTRA[m])
                with pool.Fori(0, EXTRA[m] // 2) as i:
                    for v in range(2):
                        b = EXPERTS + 2 * i + v
                        with pool.If(used > 2 * i + v):
                            gather(b, v)
                for par in range(2):
                    pool.wait_ge(y_stored[par], 8 * (b0 + nb))
                for t in range(nt):
                    for kk in range(2):
                        pool.indirect_dma_start(out=yg[t][:, kk, :], out_offset=None, in_=y_dram,
                                                in_offset=bass.IndirectOffsetOnAxis(ap=slot_id[:, t, kk:kk + 1], axis=0)
                                                ).then_inc(yg_landed[t], 16)

            def conv(l):
                pool.wait_ge(z_ready, l + 1)
                taps = cols1[:, l, 0:2 * CONV_W].rearrange("p (c j) -> p c j", c=2)
                terms = (ystage[:, 0:512].rearrange("p (c n) -> p c n", c=2), sig)

                def term(j, dst):
                    return pool.tensor_tensor(dst, zpad[:, :, j:j + SEQ], taps[:, :, j:j + 1].to_broadcast([P, 2, SEQ]), ALU.mult)

                term(0, conv_acc)
                term(1, terms[1])
                pool.drain()
                for j in range(1, CONV_W):
                    pool.tensor_tensor(conv_acc, conv_acc, terms[j % 2], ALU.add)
                    if j + 1 < CONV_W:
                        term(j + 1, terms[(j + 1) % 2])
                    pool.drain()
                bias = cols1[:, l, 2 * CONV_W:2 * CONV_W + 2].unsqueeze(2).to_broadcast([P, 2, SEQ])
                pool.tensor_tensor(conv_acc, conv_acc, bias, ALU.add)
                pool.drain().then_inc(conv_ready, 1)

            conv(0)
            conv(1)
            moe(0)
            moe(1)


INPUTS = ["x", "ffn1_norm", "ffn1_w_gate", "ffn1_w_up", "ffn1_w_down", "mix_norm", "w_in", "pool_w", "w_out",
          "ffn2_norm", "ffn2_w_gate", "ffn2_w_up", "ffn2_w_down", "post_norm", "ctx_2", "w_mod_2", "b_mod_2",
          "norm_mix_g_2", "norm_ffn_g_2", "w_in_even_2", "w_out_even_2", "w_qkv_2", "w_o_2", "w1_2", "w3_2", "w2_2"]


def kernel(**inputs):
    import concourse.bacc as bacc
    from concourse.bass_utils import run_bass_kernel_spmd

    a = {n: np.ascontiguousarray(inputs[n]) for n in INPUTS}
    I = {n: np.asarray(v) for n, v in inputs.items()}

    def cols(v):
        return v.reshape(v.shape[0], -1, P).transpose(0, 2, 1)

    L = DEPTH
    taps = I["conv_dw"].reshape(L, CONV_W, 2, P).transpose(0, 3, 2, 1).reshape(L, P, 2 * CONV_W)
    a["cols1"] = np.ascontiguousarray(np.concatenate(
        [taps, cols(I["conv_dw_bias"]), cols(I["conv_ln_gain"]), cols(I["conv_ln_bias"]), cols(I["pool_scale"])],
        axis=2).transpose(1, 0, 2))
    a["rows1"] = np.ascontiguousarray(np.concatenate(
        [I["q_norm"], I["k_norm"], I["lambda_q1"], I["lambda_k1"], I["lambda_q2"], I["lambda_k2"],
         I["attn_subln"]], axis=1).reshape(-1))
    a["rows2"] = np.ascontiguousarray(np.concatenate(
        [I["q_norm_g_2"][0], I["k_norm_g_2"][0], I["sink_logit_2"][0]]))
    a["cond_cols"] = np.ascontiguousarray(
        np.stack([I["c_2"][0], I["c_ctx_2"]]).reshape(2, KD, P).transpose(2, 1, 0))
    a["router_w"] = np.ascontiguousarray(
        np.concatenate([I["w_router_g_2"], I["w_router_e_2"]], axis=2).reshape(L, KD, P, NLOG).transpose(2, 0, 1, 3))
    a["router_b"] = np.ascontiguousarray(
        np.concatenate([I["b_router_g_2"], I["b_router_e_2"]], axis=1).reshape(-1))
    a["conv2_cols"] = np.ascontiguousarray(I["conv_w_2"][0].reshape(3, 4, P).transpose(2, 1, 0))
    a["consts"] = const_table()[0]

    nc = bacc.Bacc("TRN2", target_bir_lowering=False, num_devices=1)
    arrays = {f"in_{n}": v for n, v in a.items()}
    aps = {n: nc.dram_tensor(f"in_{n}", v.shape, mybir.dt.from_np(v.dtype), kind="ExternalInput").ap()
           for n, v in a.items()}
    out = nc.dram_tensor("out", (1, SEQ, D), F32, kind="ExternalOutput").ap()
    build(nc, aps, out)
    r = run_bass_kernel_spmd(nc, [arrays], core_ids=[0])
    return r.results[0]["out"]
```
